# Optimizing a Trainium2 kernel written in Bass

```python
import math
import jax, jax.numpy as jnp
from jax import lax
import numpy as np

D_MODEL = 2048
BATCH = 1
SEQ = 512
DEPTH = 1

D_MIX = D_MODEL
SGU_WIDTH = D_MIX // 4
SGU_HEADS = 4
SGU_HEAD_DIM = SGU_WIDTH // SGU_HEADS
SGU_CHUNK = 128
CONV_CH = D_MIX // 4
CONV_K = 31
ATTN_WIDTH = D_MIX // 2
ATTN_HEADS = 8
ATTN_HEAD_DIM = ATTN_WIDTH // ATTN_HEADS
DILATED_CONFIGS = ((128, 1), (512, 4), (2048, 16))
QBLK = 128
D_IN = 2 * SGU_WIDTH + 2 * CONV_CH + 3 * ATTN_WIDTH
IN_SPLITS = (SGU_WIDTH, 2 * SGU_WIDTH, 2 * SGU_WIDTH + CONV_CH, 2 * SGU_WIDTH + 2 * CONV_CH,
             2 * SGU_WIDTH + 2 * CONV_CH + ATTN_WIDTH, 2 * SGU_WIDTH + 2 * CONV_CH + 2 * ATTN_WIDTH)
N_GROUPS = 4
EXPERTS_PER_GROUP = 8
N_EXPERTS = N_GROUPS * EXPERTS_PER_GROUP
TOP_K = 2
D_EXPERT = D_MODEL // 4
MOE_BLK = 128
EPS = 1e-6

kernel_name = "hymba_gmlp_conformer_dilated_attn_hmoe"

def rms_norm(x, g):
    xf = x.astype(jnp.float32)
    y = xf * lax.rsqrt(jnp.mean(xf * xf, axis=-1, keepdims=True) + EPS)
    return (y * g.astype(jnp.float32)).astype(x.dtype)

def layer_norm(x, g, b):
    xf = x.astype(jnp.float32)
    mu = jnp.mean(xf, axis=-1, keepdims=True)
    xc = xf - mu
    y = xc * lax.rsqrt(jnp.mean(xc * xc, axis=-1, keepdims=True) + EPS)
    return (y * g.astype(jnp.float32) + b.astype(jnp.float32)).astype(x.dtype)

def spatial_gating(u, v, g, w_s, b_s):
    B, S, _ = u.shape
    u = jax.nn.gelu(u)
    v = rms_norm(jax.nn.gelu(v), g)
    vc = v.reshape(B, S // SGU_CHUNK, SGU_CHUNK, SGU_HEADS, SGU_HEAD_DIM)
    causal = jnp.tril(jnp.ones((SGU_CHUNK, SGU_CHUNK), dtype=bool))
    w = jnp.where(causal[None], w_s, jnp.zeros((), w_s.dtype))
    z = jnp.einsum('hij,bnjhd->bnihd', w, vc) + b_s.T[None, None, :, :, None]
    return u * z.reshape(B, S, SGU_WIDTH)

def conformer_conv(a, g, w, b, ln_g, ln_b):
    z = a * jax.nn.sigmoid(g)
    z = lax.conv_general_dilated(z, w[:, None, :], window_strides=(1,),
                                 padding=[(CONV_K - 1, 0)],
                                 dimension_numbers=('NWC', 'WIO', 'NWC'),
                                 feature_group_count=CONV_CH) + b
    return jax.nn.silu(layer_norm(z, ln_g, ln_b))

def dilated_branch(q, k, v, window, dil):
    B, H, S, Dh = q.shape
    span = window // dil
    step = dil * QBLK
    P = -(-S // step) * step
    M = P // dil
    nb = M // QBLK

    def phase(t):
        t = jnp.pad(t, ((0, 0), (0, 0), (0, P - S), (0, 0)))
        t = t.reshape(B, H, M, dil, Dh).transpose(0, 1, 3, 2, 4)
        return t.reshape(B, H, dil, nb, QBLK, Dh)

    def with_prev(t):
        prev = jnp.pad(t[:, :, :, :-1], ((0, 0), (0, 0), (0, 0), (1, 0), (0, 0), (0, 0)))
        return jnp.concatenate([prev, t], axis=4)

    qb = phase(q).astype(jnp.float32)
    kb = with_prev(phase(k)).astype(jnp.float32)
    vb = with_prev(phase(v)).astype(jnp.float32)
    s = jnp.einsum('bhrnid,bhrnjd->bhrnij', qb, kb) * (Dh ** -0.5)
    i = jnp.arange(QBLK)[:, None]
    j = jnp.arange(2 * QBLK)[None, :]
    dist = QBLK + i - j
    blk = jnp.arange(nb)[:, None, None]
    valid = (dist >= 0) & (dist <= span) & ((blk > 0) | (j >= QBLK))[None] if False else \
        ((dist >= 0) & (dist <= span))[None] & ((blk > 0) | (j >= QBLK))
    s = jnp.where(valid, s, -jnp.inf)
    lse = jax.nn.logsumexp(s, axis=-1)
    p = jnp.exp(s - lse[..., None])
    o = jnp.einsum('bhrnij,bhrnjd->bhrnid', p, vb)
    o = o.reshape(B, H, dil, M, Dh).transpose(0, 1, 3, 2, 4).reshape(B, H, P, Dh)[:, :, :S]
    lse = lse.reshape(B, H, dil, M).transpose(0, 1, 3, 2).reshape(B, H, P)[:, :, :S]
    return o, lse

def dilated_attention(q, k, v, q_g, k_g):
    B, S, _ = q.shape

    def heads(t):
        return t.reshape(B, S, ATTN_HEADS, ATTN_HEAD_DIM).transpose(0, 2, 1, 3)

    qh = rms_norm(heads(q), q_g)
    kh = rms_norm(heads(k), k_g)
    vh = heads(v)
    outs, lses = [], []
    for window, dil in DILATED_CONFIGS:
        o, lse = dilated_branch(qh, kh, vh, window, dil)
        outs.append(o)
        lses.append(lse)
    wts = jax.nn.softmax(jnp.stack(lses), axis=0)
    o = jnp.einsum('gbhs,gbhsd->bhsd', wts, jnp.stack(outs))
    return o.astype(v.dtype).transpose(0, 2, 1, 3).reshape(B, S, ATTN_WIDTH)

def hier_moe(h, w_rg, b_rg, w_re, b_re, w_g, w_u, w_d):
    B, S, D = h.shape
    T = B * S
    xt = h.reshape(T, D)
    logit_g = (xt @ w_rg).astype(jnp.float32) + b_rg.astype(jnp.float32)
    p_g = jax.nn.softmax(logit_g, axis=-1)
    grp = jnp.argmax(logit_g, axis=-1).astype(jnp.int32)
    gate_g = jnp.take_along_axis(p_g, grp[:, None], axis=1)[:, 0]
    logit_e = ((xt @ w_re).astype(jnp.float32) + b_re.astype(jnp.float32)).reshape(T, N_GROUPS, EXPERTS_PER_GROUP)
    logit_e = jnp.take_along_axis(logit_e, grp[:, None, None], axis=1)[:, 0]
    top_v, top_i = lax.top_k(logit_e, TOP_K)
    gates = gate_g[:, None] * jax.nn.softmax(top_v, axis=-1)
    eid = grp[:, None] * EXPERTS_PER_GROUP + top_i.astype(jnp.int32)

    n_assign = T * TOP_K
    flat_e = eid.reshape(-1)
    flat_tok = jnp.repeat(jnp.arange(T, dtype=jnp.int32), TOP_K)
    flat_gate = gates.reshape(-1)
    order = jnp.argsort(flat_e)
    se = flat_e[order]
    counts = jnp.bincount(flat_e, length=N_EXPERTS).astype(jnp.int32)
    starts = jnp.cumsum(counts) - counts
    pcounts = (counts + MOE_BLK - 1) // MOE_BLK * MOE_BLK
    pends = jnp.cumsum(pcounts)
    pstarts = pends - pcounts
    dest = pstarts[se] + (jnp.arange(n_assign, dtype=jnp.int32) - starts[se])
    cap = n_assign + N_EXPERTS * MOE_BLK
    nblk = cap // MOE_BLK
    buf_tok = jnp.full((cap,), T, jnp.int32).at[dest].set(flat_tok[order])
    buf_gate = jnp.zeros((cap,), jnp.float32).at[dest].set(flat_gate[order])
    blk_e = jnp.minimum(jnp.searchsorted(pends, jnp.arange(nblk, dtype=jnp.int32) * MOE_BLK, side='right'),
                        N_EXPERTS - 1).astype(jnp.int32)
    xpad = jnp.concatenate([xt, jnp.zeros((1, D), xt.dtype)], axis=0)

    def expert_block(args):
        tok, e = args
        xb = xpad[tok]
        hb = jax.nn.silu(xb @ w_g[e]) * (xb @ w_u[e])
        return hb @ w_d[e]

    yb = lax.map(expert_block, (buf_tok.reshape(nblk, MOE_BLK), blk_e)).reshape(cap, D)
    y = jnp.zeros((T + 1, D), xt.dtype).at[buf_tok].add(yb * buf_gate[:, None].astype(yb.dtype))
    return y[:T].reshape(B, S, D)

def setup_inputs(seed: int = 0) -> dict:
    key = jax.random.key(seed)
    ks = jax.random.split(key, 24)
    f32 = jnp.float32

    def nrm(k, shape, scale):
        return jax.random.normal(k, shape, f32) * scale

    return {
        "x": nrm(ks[0], (BATCH, SEQ, D_MODEL), 1.0),
        "norm1": 1.0 + nrm(ks[1], (DEPTH, D_MODEL), 0.02),
        "w_in": nrm(ks[2], (DEPTH, D_MODEL, D_IN), D_MODEL ** -0.5),
        "sgu_norm": 1.0 + nrm(ks[3], (DEPTH, SGU_WIDTH), 0.02),
        "sgu_w": nrm(ks[4], (DEPTH, SGU_HEADS, SGU_CHUNK, SGU_CHUNK), SGU_CHUNK ** -0.5),
        "sgu_b": 1.0 + nrm(ks[5], (DEPTH, SGU_HEADS, SGU_CHUNK), 0.02),
        "conv_w": nrm(ks[6], (DEPTH, CONV_K, CONV_CH), CONV_K ** -0.5),
        "conv_b": nrm(ks[7], (DEPTH, CONV_CH), 0.02),
        "conv_ln_g": 1.0 + nrm(ks[8], (DEPTH, CONV_CH), 0.02),
        "conv_ln_b": nrm(ks[9], (DEPTH, CONV_CH), 0.02),
        "q_norm": 1.0 + nrm(ks[10], (DEPTH, ATTN_HEAD_DIM), 0.02),
        "k_norm": 1.0 + nrm(ks[11], (DEPTH, ATTN_HEAD_DIM), 0.02),
        "out_norm": 1.0 + nrm(ks[12], (DEPTH, D_MIX), 0.02),
        "w_out": nrm(ks[13], (DEPTH, D_MIX, D_MODEL), D_MIX ** -0.5),
        "norm2": 1.0 + nrm(ks[14], (DEPTH, D_MODEL), 0.02),
        "w_router_group": nrm(ks[15], (DEPTH, D_MODEL, N_GROUPS), D_MODEL ** -0.5),
        "b_router_group": nrm(ks[16], (DEPTH, N_GROUPS), 0.01),
        "w_router_expert": nrm(ks[17], (DEPTH, D_MODEL, N_EXPERTS), D_MODEL ** -0.5),
        "b_router_expert": nrm(ks[18], (DEPTH, N_EXPERTS), 0.01),
        "w_expert_gate": nrm(ks[19], (DEPTH, N_EXPERTS, D_MODEL, D_EXPERT), D_MODEL ** -0.5),
        "w_expert_up": nrm(ks[20], (DEPTH, N_EXPERTS, D_MODEL, D_EXPERT), D_MODEL ** -0.5),
        "w_expert_down": nrm(ks[21], (DEPTH, N_EXPERTS, D_EXPERT, D_MODEL), D_EXPERT ** -0.5),
    }

def reference(x, norm1, w_in, sgu_norm, sgu_w, sgu_b, conv_w, conv_b, conv_ln_g, conv_ln_b,
              q_norm, k_norm, out_norm, w_out, norm2, w_router_group, b_router_group,
              w_router_expert, b_router_expert, w_expert_gate, w_expert_up, w_expert_down):
    h = x
    a_end = SGU_WIDTH
    b_end = SGU_WIDTH + CONV_CH
    for l in range(DEPTH):
        hn = rms_norm(h, norm1[l])
        proj = hn @ w_in[l]
        u_a, v_a, a_b, g_b, q, k, v = jnp.split(proj, list(IN_SPLITS), axis=-1)
        y_a = spatial_gating(u_a, v_a, sgu_norm[l], sgu_w[l], sgu_b[l])
        y_b = conformer_conv(a_b, g_b, conv_w[l], conv_b[l], conv_ln_g[l], conv_ln_b[l])
        y_c = dilated_attention(q, k, v, q_norm[l], k_norm[l])
        g = out_norm[l]
        mix = jnp.concatenate([rms_norm(y_a, g[:a_end]),
                               rms_norm(y_b, g[a_end:b_end]),
                               rms_norm(y_c, g[b_end:])], axis=-1)
        h = h + mix @ w_out[l]
        h = h + hier_moe(rms_norm(h, norm2[l]), w_router_group[l], b_router_group[l],
                         w_router_expert[l], b_router_expert[l],
                         w_expert_gate[l], w_expert_up[l], w_expert_down[l])
    return h


_drawn_inputs = setup_inputs


def setup_inputs(seed=0):
    import zlib

    import numpy as np

    out = dict(_drawn_inputs(seed))
    spreads = {}
    factors = {'sgu_norm': 8.0,
     'sgu_b': 7.81,
     'conv_ln_g': 4.082,
     'conv_ln_b': 4.059,
     'q_norm': 2.871,
     'k_norm': 3.54,
     'norm2': 2.877,
     'b_router_group': 8.0,
     'b_router_expert': 6.132}
    for name, (base, spread) in spreads.items():
        noise = np.random.default_rng([zlib.crc32(name.encode()), seed]).standard_normal(out[name].shape)
        drawn = base * np.exp(spread * noise) if base else spread * noise
        out[name] = __import__('jax').numpy.asarray(drawn.astype(out[name].dtype))
    for name, factor in factors.items():
        out[name] = (out[name] * factor).astype(out[name].dtype)
    return out
```

```python
import math
from contextlib import ExitStack

import numpy as np

import concourse.bass as bass
from concourse import mybir

F32 = mybir.dt.float32
I32 = mybir.dt.int32
ALU = mybir.AluOpType
ACT = mybir.ActivationFunctionType
AX = mybir.AxisListType.X

P = 128
T = 512
D = 2048
TT = T // P
KT = D // P
W = 512
CH = 2048
H = 8
TAPS = 31
E = 32
EG = 8
NG = E // EG
FE = 512
FT = FE // P
TB = 64
NBLK = E + 2 * T // TB
NT = NBLK + 1
EC = 12
EPS = 1e-6
SCALE = P ** -0.5
OFF = -1.0e30
GONE = -3.0e38
NOWHERE = 1 << 20
BIG = 64.0

C_ID, C_ONE, C_LOW, C_TRI, C_BAND = 0, 128, 256, 384, 512
C_GI = C_BAND + W
C_EI = C_GI + TT * NG
C_EG = C_EI + TT * E
C_P = C_EG + TT * E
NC_CONST = C_P + 1

K_CW, K_LG, K_LB, K_OB = 0, 128, 132, 136
K_Q, K_K, K_SB = 140, 141, 142
NC_COLS = 146

R_SGU, R_OA = 0, 512

Q_V, Q_B, Q_A, Q_QK, Q_O, QUADS = 0, 2, 4, 6, 10, 14


class Chain:

    def __init__(self, eng, sem, base=0):
        self.eng, self.sem, self.base, self.n = eng, sem, base, 0

    def add(self, ins):
        ins.then_inc(self.sem, 1)
        self.n += 1

    def wait(self):
        self.eng.wait_ge(self.sem, self.base + self.n)

    def link(self, ins):
        self.add(ins)
        self.wait()


def build(nc, x, consts, pairs, cols, rows_a, row_c, row_n1, row_n2, rbias, sgu_wt, w_stream, w_rt,
          w_gate, w_up, w_down, out):
    with ExitStack() as ctx:
        def sb(name, shape, dt=F32):
            return ctx.enter_context(nc.sbuf_tensor(name, shape, dt))

        def sem(name):
            return ctx.enter_context(nc.semaphore(name))

        h2_dram = nc.dram_tensor("h2_rows", [T, D], F32, kind="Internal").ap()
        y_dram = nc.dram_tensor("y_rows", [4 * T, D // 2], F32, kind="Internal").ap()
        slot_tab = nc.dram_tensor("slot_table", [TB * NT, 4], I32, kind="Internal").ap()

        arena = sb("arena", [P, EC * CH])
        xh = sb("xh", [P, TT, D])
        hnT = sb("hnT", [P, KT, T])
        mixT = sb("mixT", [P, KT, T])
        cst = sb("cst", [P, NC_CONST])
        col = sb("col", [P, NC_COLS])
        rowa = sb("rowa", [P, 2 * W])
        sguw = sb("sguw", [P, 4, P])
        ss = sb("ss", [P, 16])
        rs = sb("rs", [P, 16])
        nmax = sb("nmax", [P, TT])
        pmax = sb("pmax", [P, TT])
        den = sb("den", [P, 2 * TT])
        rden = sb("rden", [P, TT])
        cwj = sb("cwj", [P, 32])
        eps = sb("eps", [P, 1])
        pairs_sb = sb("pairs_sb", [P, 2 * TT, 4], I32)
        dest_i = sb("dest_i", [P, 2, TT], I32)
        gates = sb("gates", [P, 2, TT])
        sched = sb("sched", [1, P + 1], I32)
        tab = sb("tab", [2 * TB, NT, 4], I32)
        tmp_i = sb("tmp_i", [P, 2, TT], I32)
        idx_tok = sb("idx_tok", [TB, 1], I32)
        idx_row = sb("idx_row", [2 * TB, 1], I32)
        tab_spare = sb("tab_spare", [1, 4], I32)
        sg = sb("sg", [P, FT * TB])
        hT = sb("hT", [P, FT * TB])

        ident = cst[:, C_ID:C_ID + P]
        ones = cst[:, C_ONE:C_ONE + P]
        low = cst[:, C_LOW:C_LOW + P]

        def slot(c):
            return arena[:, c * CH:(c + 1) * CH]

        vt = arena[:, 4 * CH:6 * CH].rearrange("p (t n) -> p t n", t=TT)
        tmp = arena[:, 6 * CH:12 * CH]
        n1row = tmp[:, 0:2048]
        hn = [tmp[:, 2048:4096], tmp[:, 4096:6144]]
        u_sb = tmp[:, 0:2048].rearrange("p (t n) -> p t n", t=TT)
        va = tmp[:, 2048:4096].rearrange("p (t n) -> p t n", t=TT)
        BB = 6144
        sig = tmp[:, BB:BB + 512]
        ZW = W + 32
        z = [tmp[:, BB + 512 + ZW * i:BB + 512 + ZW * (i + 1)] for i in range(2)]
        cacc = tmp[:, BB + 1600:BB + 2112]
        sqb = tmp[:, BB:BB + 2048].rearrange("p (j n) -> p j n", j=4)
        cbuf = tmp[:, BB + 2112:BB + 4160].rearrange("p (j n) -> p j n", j=4)
        mu = tmp[:, BB + 4160:BB + 4672]
        rb = tmp[:, BB + 4672:BB + 5184]
        yc = tmp[:, 0:4096].rearrange("p (t n) -> p t n", t=TT)
        qT = [tmp[:, 4096 + 1024 * i:4608 + 1024 * i] for i in range(2)]
        kT = [tmp[:, 4608 + 1024 * i:5120 + 1024 * i] for i in range(2)]
        sqq, sqk = tmp[:, 6144:6656], tmp[:, 6656:7168]
        rqk = [tmp[:, 7168:7680], tmp[:, 10752:11264]]
        sp_ = [tmp[:, 7680 + 512 * i:8192 + 512 * i] for i in range(2)]
        pT = [tmp[:, 8704 + 512 * i:9216 + 512 * i] for i in range(2)]
        rowc = tmp[:, 9728:10752]
        n2row = tmp[:, 4 * CH:5 * CH]
        wrt = tmp[:, 5 * CH:5 * CH + KT * 36].rearrange("p (k n) -> p k n", n=36)
        rbr = tmp[:, 5 * CH + 600:5 * CH + 600 + TT * 36].rearrange("p (t n) -> p t n", t=TT)
        h2 = mixT[:, :, :].rearrange("p k t -> p (k t)").rearrange("p (t n) -> p t n", t=TT)
        junk = mixT[:, 8:16, :].rearrange("p (t k) n -> p t (k n)", t=TT)
        rt = hnT[:, :, :].rearrange("p k t -> p (k t)")
        blk = mixT[:, :, :].rearrange("p k t -> p (k t)")
        xg = blk[0:TB, 0:D]
        ysb = blk[:, D:D + 2 * W]
        gu = blk[:, D + 2 * W:D + 3 * W]
        xgT = blk[:, 2 * D:2 * D + KT * TB]
        yrow = [[slot(2 * t + k) for k in range(2)] for t in range(TT)]

        bank = [ctx.enter_context(nc.psum_tensor(f"bank{i}", [P, W], F32)) for i in range(8)]
        acc, pat = bank[0:4], bank[4:8]
        guT = bank[1][:, :].rearrange("p (f n) -> p f n", f=FT)

        eps_set = sem("eps_set")
        x_in = [sem(f"x_in{t}") for t in range(TT)]
        const_in = sem("const_in")
        n1_in = sem("n1_in")
        rowc_in = sem("rowc_in")
        n2_in = sem("n2_in")
        w_in_slot = [sem(f"w_in_slot{c}") for c in range(4)]
        dve_own = sem("dve_own")
        hn_ready = sem("hn_ready")
        turned = sem("turned")
        act_evac = sem("act_evac")
        proj_steps = sem("proj_steps")
        z_ready = sem("z_ready")
        sig_ready = sem("sig_ready")
        conv_own = sem("conv_own")
        conv_done = sem("conv_done")
        b_sum = sem("b_sum")
        b_cent = sem("b_cent")
        b_norm = sem("b_norm")
        b_sq = sem("b_sq")
        b_silu = sem("b_silu")
        b_mixed = sem("b_mixed")
        sguw_ready = sem("sguw_ready")
        va_normed = sem("va_normed")
        spatial = sem("spatial")
        ya_ready = sem("ya_ready")
        qk_sq = sem("qk_sq")
        qk_sum = sem("qk_sum")
        qkT_ready = sem("qkT_ready")
        qk_root = sem("qk_root")
        r_own = sem("r_own")
        stat_ready = sem("stat_ready")
        root_done = sem("root_done")
        s_ready = sem("s_ready")
        s_max = sem("s_max")
        s_masked = sem("s_masked")
        p_ready = sem("p_ready")
        p_turned = sem("p_turned")
        pT_ready = sem("pT_ready")
        pv_done = sem("pv_done")
        rden_ready = sem("rden_ready")
        o_done = sem("o_done")
        yc_ready = sem("yc_ready")
        h_added = sem("h_added")
        h2_ready = sem("h2_ready")
        h2_stored = sem("h2_stored")
        logits = sem("logits")
        gate_exp = sem("gate_exp")
        exp_in = sem("exp_in")
        picked = sem("picked")
        ranked = sem("ranked")
        sched_col = sem("sched_col")
        sched_row = sem("sched_row")
        dest_ready = sem("dest_ready")
        sched_ready = sem("sched_ready")
        pairs_in = sem("pairs_in")
        tab_set = sem("tab_set")
        tab_clear = sem("tab_clear")
        tab_in = sem("tab_in")
        xg_zero = sem("xg_zero")
        e_in_slot = [sem(f"e_in_slot{c}") for c in range(EC)]
        e_used = sem("e_used")
        idx_in = sem("idx_in")
        idx_t_ready = sem("idx_t_ready")
        idx_r_ready = sem("idx_r_ready")
        xg_in = sem("xg_in")
        xg_turned = sem("xg_turned")
        xgT_ready = sem("xgT_ready")
        gu_ready = sem("gu_ready")
        gu_turned = sem("gu_turned")
        sg_ready = sem("sg_ready")
        hT_ready = sem("hT_ready")
        y_evac_a = sem("y_evac_a")
        y_evac_v = sem("y_evac_v")
        y_stored = sem("y_stored")
        yrow_in = [sem(f"yrow_in{t}") for t in range(TT)]
        part_sum = sem("part_sum")
        out_ready = sem("out_ready")
        out_stored = sem("out_stored")

        CR_Z, CR_QK, CR_S, CR_PT, CR_O = 2, 2, 4, 4, 1
        CR_E, CR_GU, CR_GT, CR_SG, CR_H, CR_Y, CR_YS = EC, 2, 1, 1, 1, 1, 16
        EV_V = 16
        EV_U = EV_V + 8
        EV_A = EV_U + 8
        EV_C = EV_A + 4
        EV_R = EV_C + 8
        EV_END = EV_R + 16

        counts = {}

        def wait_alone(eng, *waits):
            for i in range(len(waits)):
                if (eng, i) not in counts:
                    counts[eng, i] = eng.alloc_register(f"count{i}")
                eng.reg_mov(counts[eng, i], waits[i][1])
            eng.wait_ge(const_in, 16 * 4)
            for i, (s, _) in enumerate(waits):
                eng.wait_ge(s, counts[eng, i])

        block = ctx.enter_context(nc.Block())

        @block.sync
        def _(sp):
            sp.dma_start(n1row, row_n1).then_inc(n1_in, 16)
            for t in range(TT):
                sp.dma_start(xh[:, t, :], x[t * P:(t + 1) * P, :]).then_inc(x_in[t], 16)
            sp.dma_start(cst[:, :], consts).then_inc(const_in, 16)
            sp.dma_start(col[:, :], cols).then_inc(const_in, 16)
            sp.dma_start(rowa[:, :], rows_a).then_inc(const_in, 16)
            sp.dma_start(sguw[:, :, :], sgu_wt).then_inc(const_in, 16)
            for c in range(4):
                sp.dma_start(slot(c), w_stream[c]).then_inc(w_in_slot[c], 16)
            with sp.Fori(1, QUADS) as q:
                for c in range(4):
                    wait_alone(sp, (proj_steps, q * 16 + (4 * c + 4 - 16)))
                    sp.dma_start(slot(c), w_stream[bass.ds(q * 4 + c, 1)].rearrange("o p n -> (o p) n"))\
                        .then_inc(w_in_slot[c], 16)
            sp.wait_ge(yc_ready, TT)
            sp.dma_start(n2row, row_n2).then_inc(n2_in, 16)
            sp.dma_start(wrt, w_rt).then_inc(n2_in, 16)
            sp.dma_start(rbr, rbias).then_inc(n2_in, 16)

            def expert(c, e):
                if c < 8:
                    m = w_gate if c % 2 == 0 else w_up
                    k = (c // 2) * 4
                    return m[e].rearrange("o (p k) n -> (o p) k n", k=KT)[:, k:k + 4, :]
                return w_down[e].rearrange("o (f p) n -> f (o p) n", p=P)[c - 8]

            def dst(c):
                return slot(c).rearrange("p (k n) -> p k n", k=4) if c < 8 else slot(c)

            sp.wait_ge(proj_steps, 16 * QUADS)
            for c in range(EC - 2):
                sp.dma_start(dst(c), expert(c, slice(0, 1))).then_inc(e_in_slot[c], 16)
            for t in range(TT):
                sp.wait_ge(h2_ready, t + 1)
                sp.dma_start(h2_dram[t * P:(t + 1) * P, :], h2[:, t, :]).then_inc(h2_stored, 16)
            sp.wait_ge(picked, 1)
            for c in range(EC - 2, EC):
                sp.dma_start(dst(c), expert(c, slice(0, 1))).then_inc(e_in_slot[c], 16)
            sp.wait_ge(sched_ready, 1)
            nb = sp.value_load(sched[0:1, P:P + 1], min_val=E, max_val=NBLK)
            with sp.Fori(1, nb) as b:
                e = sp.value_load(sched[0:1, bass.ds(b, 1)], min_val=0, max_val=E - 1)
                before = sp.value_load(sched[0:1, bass.ds(b - 1, 1)], min_val=0, max_val=E - 1)
                for c in range(EC):
                    wait_alone(sp, (e_used, b * EC + (c + 1)))
                    sp.dma_start(dst(c), expert(c, bass.ds(e, 1)), cond=(e != before))\
                        .then_inc(e_in_slot[c], 16)
            sp.wait_ge(y_stored, nb * 16 + CR_YS)
            for t in range(TT):
                for k in range(2):
                    r = k * T + t * P
                    sp.dma_start(yrow[t][k], y_dram.rearrange("(r h) n -> r (h n)", h=2)[r:r + P, :])\
                        .then_inc(yrow_in[t], 16)
            for t in range(TT):
                sp.wait_ge(out_ready, t + 1)
                sp.dma_start(out[t * P:(t + 1) * P, :], xh[:, t, :]).then_inc(out_stored, 16)
            sp.wait_ge(out_stored, 16 * TT)

        @block.gpsimd
        def _(pool):
            pool.memset(eps[:, :], EPS).then_inc(eps_set, 1)
            pool.memset(tab[:, :, :], NOWHERE).then_inc(tab_set, 1)
            pool.wait_ge(tab_set, 1)
            pool.dma_start(slot_tab.rearrange("(s b) four -> s b four", b=NT), tab[0:TB, :, :]).then_inc(tab_clear, 16)
            pool.wait_ge(tab_clear, 16)
            pool.dma_start(pairs_sb[:, :, :], pairs).then_inc(pairs_in, 16)
            pool.wait_ge(pairs_in, 16)
            pool.wait_ge(dest_ready, 1)
            for k in range(2):
                for t in range(TT):
                    pool.indirect_dma_start(
                        out=slot_tab, out_offset=bass.IndirectOffsetOnAxis(ap=dest_i[:, k, t:t + 1], axis=0),
                        in_=pairs_sb[:, k * TT + t, :], in_offset=None).then_inc(tab_in, 16)
            pool.wait_ge(h2_stored, 16 * TT)
            pool.wait_ge(turned, EV_END - 20)
            pool.memset(xg, 0.0).then_inc(xg_zero, 1)
            pool.wait_ge(tab_in, 16 * 2 * TT)
            for h in range(2):
                pool.dma_start(tab[h * TB:(h + 1) * TB, :, :], slot_tab.rearrange("(s b) four -> s b four", b=NT))\
                    .then_inc(idx_in, 16)
            pool.wait_ge(xg_zero, 1)
            pool.wait_ge(idx_in, 32)

            def tokens(b):
                pool.tensor_copy(idx_tok[:, :], tab[0:TB, b, 0:1].rearrange("p o n -> p (o n)"))\
                    .then_inc(idx_t_ready, 1)

            def gather():
                pool.indirect_dma_start(
                    out=xg, out_offset=None, in_=h2_dram,
                    in_offset=bass.IndirectOffsetOnAxis(ap=idx_tok[:, 0:1], axis=0),
                    bounds_check=T - 1, oob_is_err=False).then_inc(xg_in, 16)

            tokens(slice(0, 1))
            pool.wait_ge(idx_t_ready, 1)
            gather()
            pool.dma_start(tab_spare[0:1, :], slot_tab[0:1, :]).then_inc(y_stored, CR_YS)
            pool.wait_ge(sched_ready, 1)
            nb = pool.value_load(sched[0:1, P:P + 1], min_val=E, max_val=NBLK)
            with pool.Fori(0, nb) as b:
                wait_alone(pool, (xg_in, b * 16 + 16))
                tokens(bass.ds(b + 1, 1))
                wait_alone(pool, (idx_t_ready, b + 2), (xg_turned, b * 2 + 2))
                gather()
                wait_alone(pool, (idx_r_ready, b * 2 + 2), (y_evac_a, b + (CR_Y + 1)),
                           (y_evac_v, b + (CR_Y + 1)))
                pool.indirect_dma_start(
                    out=y_dram, out_offset=bass.IndirectOffsetOnAxis(ap=idx_row[:, 0:1], axis=0),
                    in_=ysb, in_offset=None, bounds_check=4 * T - 1, oob_is_err=False).then_inc(y_stored, 16)

        @block.tensor
        def _(pe):
            def turn(dst_bank, col0, src, idn, rows, last=None):
                m = pe.transpose(dst_bank[0:rows, col0:col0 + src.shape[0]], src, idn)
                if last is not None:
                    m.then_inc(last, 1)

            pe.wait_ge(const_in, 16 * 4)
            for t in range(TT):
                pe.wait_ge(hn_ready, t + 1)
                for q in range(4):
                    f = t * 4 + q
                    if f >= 8:
                        pe.wait_ge(act_evac, f - 7)
                    for i in range(4):
                        k = q * 4 + i
                        turn(bank[f % 8], i * P, hn[t % 2][:, k * P:(k + 1) * P], ident, P,
                             turned if i == 3 else None)
            pe.wait_ge(act_evac, EV_V)

            def chunk_tokens(c, q, src, free):
                pe.wait_ge(w_in_slot[c], q * 16 + 16)
                for j in range(TT):
                    if c == 0:
                        free(j)
                    for i in range(4):
                        k = 4 * c + i
                        m = pe.matmul(acc[j][:, :], src[:, k, j * P:(j + 1) * P],
                                      slot(c)[:, i * W:(i + 1) * W], start=(k == 0), stop=(k == KT - 1))
                    m.then_inc(proj_steps, 1)

            def tile_step(c, b, k):
                m = pe.matmul(acc[b][:, :], slot(c)[:, k * P:(k + 1) * P], hnT[:, k, :],
                              start=(k == 0), stop=(k == KT - 1))
                if k % 4 == 3:
                    m.then_inc(proj_steps, 1)

            with pe.Fori(0, 2) as g:
                for c in range(4):
                    chunk_tokens(c, g, hnT, lambda j: pe.wait_ge(act_evac, g * 4 + (EV_V - 3 + j)))
            pe.wait_ge(act_evac, EV_U)
            with pe.Fori(0, 2) as i:
                for u in range(2):
                    for w in range(2):
                        c = 2 * u + w
                        pe.wait_ge(w_in_slot[c], i * 16 + 16 * (Q_B + 1))
                        pe.wait_ge(z_ready if w == 0 else sig_ready, i * 2 + (u + CR_Z - 1))
                        for k in range(KT):
                            tile_step(c, c, k)
            pe.wait_ge(z_ready, CR_Z + 4)
            pe.wait_ge(sig_ready, CR_Z + 4)
            for c in range(4):
                chunk_tokens(c, Q_A, hnT, lambda j: None)
            pe.wait_ge(conv_done, 4)
            for j in range(4):
                m = pe.matmul(pat[3][:, :], ones, cbuf[:, j, :], start=(j == 0), stop=(j == 3))
            m.then_inc(b_sum, 1)
            for c in range(4):
                chunk_tokens(c, Q_A + 1, hnT, lambda j: pe.wait_ge(act_evac, EV_U + 1 + j))
            for j in range(4):
                pe.wait_ge(b_sq, j + 1)
                m = pe.matmul(pat[3][:, :], ones, sqb[:, j, :], start=(j == 0), stop=(j == 3))
            m.then_inc(b_sum, 1)

            def proj_head(h, q, c0, lo, hi):
                for s in range(lo, hi):
                    w, k = divmod(s, KT)
                    if k == 0:
                        pe.wait_ge(w_in_slot[c0 + w], q * 16 + 16)
                        if w == 0:
                            pe.wait_ge(qkT_ready, h * 2 + (CR_QK - 2))
                    tile_step(c0 + w, c0 + w, k)

            pe.wait_ge(act_evac, EV_A)
            for k in range(KT):
                if k == 0:
                    pe.wait_ge(w_in_slot[0], 16 * (Q_QK + 1))
                tile_step(0, 0, k)
            for j in range(4):
                pe.wait_ge(b_sq, 4 + j + 1)
                m = pe.matmul(pat[3][:, :], ones, sqb[:, j, :], start=(j == 0), stop=(j == 3))
            m.then_inc(b_sum, 1)
            pe.wait_ge(sguw_ready, 1)
            for n in range(TT):
                pe.wait_ge(va_normed, n + 1)
                if n == 3:
                    pe.wait_ge(b_mixed, 4)
                for hh in range(4):
                    m = pe.matmul(pat[n][:, hh * P:(hh + 1) * P], sguw[:, hh, :], va[:, n, hh * P:(hh + 1) * P],
                                  start=True, stop=True)
                m.then_inc(spatial, 1)
            for k in range(KT):
                if k == 0:
                    pe.wait_ge(w_in_slot[1], 16 * (Q_QK + 1))
                tile_step(1, 1, k)
            for n in range(TT):
                pe.wait_ge(ya_ready, n + 1)
                for i in range(4):
                    turn(pat[n], i * P, u_sb[:, n, i * P:(i + 1) * P], ident, P, turned if i == 3 else None)
            pe.wait_ge(act_evac, EV_C)

            def norm_sums(g):
                pe.wait_ge(s_masked, g * 4 + CR_S)
                for w, sq in enumerate((sqq, sqk)):
                    pe.wait_ge(qk_sq, g * 2 + (w + 1))
                    pe.matmul(pat[w][:, :], ones, sq, start=True, stop=True).then_inc(qk_sum, 1)

            def scores(g, par, qi):
                if qi == 0:
                    pe.wait_ge(qkT_ready, g * 2 + (CR_QK + 2))
                if qi >= 2:
                    pe.wait_ge(s_masked, g * 4 + (CR_S + qi - 1))
                n = (qi + 1) * P
                pe.matmul(pat[qi % 2][:, 0:n], qT[par][:, qi * P:n], kT[par][:, 0:n],
                          start=True, stop=True).then_inc(s_ready, 1)

            def turn_p(g, qi):
                pe.wait_ge(p_ready, g * 4 + (qi + 1))
                pe.wait_ge(pT_ready, g * 4 + (CR_PT + qi))
                for j in range(qi + 1):
                    turn(pat[2], j * P, sp_[qi % 2][:, j * P:(j + 1) * P], ident, P,
                         p_turned if j == qi else None)

            def pv(g, qi):
                pe.wait_ge(pT_ready, g * 4 + (CR_PT + qi + 1))
                if qi == 0:
                    pe.wait_ge(o_done, g + CR_O)
                for j in range(qi + 1):
                    v_head = vt[:, j, bass.ds(g * P, P)] if not isinstance(g, int) else vt[:, j, g * P:(g + 1) * P]
                    m = pe.matmul(pat[3][:, qi * P:(qi + 1) * P], pT[qi % 2][:, j * P:(j + 1) * P], v_head,
                                  start=(j == 0), stop=(j == qi))
                m.then_inc(pv_done, 1)

            def attention_part(g, par, s):
                if s == 0:
                    norm_sums(g)
                if 1 <= s <= 4:
                    scores(g, par, s - 1)
                if 2 <= s <= 5:
                    turn_p(g, s - 2)
                if 3 <= s <= 6:
                    pv(g, s - 3)

            CUTS = [0, 5, 10, 15, 20, 24, 28, 32]
            with pe.Fori(0, 3) as i:
                for s in range(7):
                    proj_head(i * 2 + 1, i + Q_QK, 2, CUTS[s], CUTS[s + 1])
                    attention_part(i * 2, 0, s)
                for s in range(7):
                    proj_head(i * 2 + 2, i + (Q_QK + 1), 0, CUTS[s], CUTS[s + 1])
                    attention_part(i * 2 + 1, 1, s)
            for s in range(7):
                proj_head(H - 1, Q_QK + 3, 2, CUTS[s], CUTS[s + 1])
                attention_part(H - 2, 0, s)

            def mix_steps(c, j, k_lo, k_hi):
                for i in range(k_lo, k_hi):
                    k = 4 * c + i
                    m = pe.matmul(acc[j][:, :], mixT[:, k, j * P:(j + 1) * P], slot(c)[:, i * W:(i + 1) * W],
                                  start=(k == 0), stop=(k == KT - 1))
                if k_hi == 4:
                    m.then_inc(proj_steps, 1)

            order = [(c, j) for c in range(2) for j in range(TT)]
            seen = set()
            for s in range(8):
                c, j = order[s]
                if c not in seen:
                    seen.add(c)
                    pe.wait_ge(w_in_slot[c], 16 * (Q_O + 1))
                if c == 0 and j == 0:
                    pe.wait_ge(qkT_ready, CR_QK + 2 * (H - 1))
                    pe.wait_ge(qk_sq, 2 * (H - 1))
                if c == 0 and j == 2:
                    pe.wait_ge(qkT_ready, CR_QK + 2 * H)
                mix_steps(c, j, 0, 4)
                if s < 7:
                    attention_part(H - 1, 1, s)
            for n in range(TT):
                pe.wait_ge(yc_ready, n + 1)
                for w in range(2):
                    f = 2 * n + w
                    if f >= 4:
                        pe.wait_ge(act_evac, EV_C + f - 3)
                    if f < 4:
                        pe.wait_ge(o_done, CR_O + H)
                    for i in range(4):
                        turn(pat[f % 4], i * P, yc[:, n, (4 * w + i) * P:(4 * w + i + 1) * P], ident, P,
                             turned if i == 3 else None)
            pe.wait_ge(act_evac, EV_R)
            for c in range(2, 4):
                pe.wait_ge(w_in_slot[c], 16 * (Q_O + 1))
                for j in range(TT):
                    mix_steps(c, j, 0, 4)
            with pe.Fori(1, 4) as g:
                for c in range(4):
                    chunk_tokens(c, g + Q_O, mixT, lambda j: pe.wait_ge(h_added, g * 4 + (j - 3)))

            for t in range(TT):
                pe.wait_ge(h2_ready, t + 1)
                for q in range(4):
                    f = t * 4 + q
                    if f >= 8:
                        pe.wait_ge(act_evac, EV_R + f - 7)
                    for i in range(4):
                        k = q * 4 + i
                        turn(bank[f % 8], i * P, h2[:, t, k * P:(k + 1) * P], ident, P,
                             turned if i == 3 else None)
            pe.wait_ge(act_evac, EV_END)
            pe.wait_ge(n2_in, 16 * 3)
            for t in range(TT):
                for k in range(KT):
                    m = pe.matmul(bank[0][:, t * 36:(t + 1) * 36], hnT[:, k, t * P:(t + 1) * P], wrt[:, k, :],
                                  start=(k == 0), stop=(k == KT - 1))
            m.then_inc(logits, 1)
            pe.wait_ge(picked, 1)
            taken = rt[:, 0:TT * E].rearrange("p (t e) -> p t e", t=TT)
            for t in range(TT):
                for s in range(t + 1):
                    pe.matmul(bank[1][:, t * E:(t + 1) * E], low if s == t else ones, taken[:, s, :],
                              start=(s == 0), stop=(s == t))
            for s in range(TT):
                m = pe.matmul(bank[1][:, TT * E:(TT + 1) * E], ones, taken[:, s, :],
                              start=(s == 0), stop=(s == TT - 1))
            m.then_inc(ranked, 1)
            pe.wait_ge(sched_col, 1)
            pe.transpose(bank[2][0:1, 0:P], ss[:, 15:16], ident).then_inc(sched_row, 1)

            pgu, pguT, px, py = bank[0], bank[1], bank[2:4], bank[4:6]

            def turn_rows():
                for k in range(KT):
                    turn(px[k // 8], (k % 8) * TB, xg[:, k:D:KT], cst[0:TB, C_ID:C_ID + TB], P,
                         xg_turned if k % 8 == 7 else None)

            pe.sem_inc(e_used, CR_E)
            pe.wait_ge(sched_ready, 1)
            nb = pe.value_load(sched[0:1, P:P + 1], min_val=E, max_val=NBLK)
            pe.wait_ge(xg_in, 16)
            turn_rows()
            with pe.Fori(0, nb) as b:
                pe.wait_ge(xgT_ready, b * 2 + 2)
                for c in range(4):
                    pe.wait_ge(e_in_slot[2 * c], b * 16 + 16)
                    pe.wait_ge(e_in_slot[2 * c + 1], b * 16 + 16)
                    if c == 0:
                        pe.wait_ge(gu_ready, b * 2 + CR_GU)
                    for i in range(4):
                        k = 4 * c + i
                        for w in range(2):
                            m = pe.matmul(pgu[w * TB:(w + 1) * TB, :], xgT[:, k * TB:(k + 1) * TB],
                                          slot(2 * c + w)[:, i * FE:(i + 1) * FE], start=(k == 0), stop=(k == KT - 1))
                            if i == 3:
                                m.then_inc(e_used, 1)
                wait_alone(pe, (xg_in, b * 16 + 32))
                turn_rows()
                pe.wait_ge(gu_ready, b * 2 + (CR_GU + 2))
                for f in range(FT):
                    turn(pguT, f * P, gu[:, f * P:(f + 1) * P], ident, P, gu_turned if f == FT - 1 else None)
                pe.wait_ge(hT_ready, b + (CR_H + 1))
                pe.wait_ge(y_evac_a, b + CR_Y)
                pe.wait_ge(y_evac_v, b + CR_Y)
                for f in range(FT):
                    pe.wait_ge(e_in_slot[8 + f], b * 16 + 16)
                    for n, w in ((0, 0), (0, 1), (1, 0), (1, 1)):
                        m = pe.matmul(py[n][w * TB:(w + 1) * TB, :], hT[:, f * TB:(f + 1) * TB],
                                      slot(8 + f)[:, (2 * w + n) * W:(2 * w + n + 1) * W], start=(f == 0), stop=(f == FT - 1))
                    m.then_inc(e_used, 1)

        @block.scalar
        def _(act):
            def evac(dst, src):
                nc.scalar.activation(dst, src, ACT.Copy).then_inc(act_evac, 1)

            def root(dst, src, width):
                nc.scalar.activation(dst, src, ACT.Sqrt, bias=eps[:, 0:1], scale=1.0 / width).then_inc(root_done, 1)

            act.wait_ge(eps_set, 1)
            for f in range(16):
                t, q = divmod(f, 4)
                if q == 0:
                    act.wait_ge(stat_ready, t + 1)
                    root(rs[:, t:t + 1], ss[:, t:t + 1], D)
                act.wait_ge(turned, f + 1)
                evac(hnT[:, 4 * q:4 * q + 4, t * P:(t + 1) * P],
                     bank[f % 8][:, :].rearrange("p (k n) -> p k n", k=4))
            with act.Fori(0, 2) as g:
                for j in range(TT):
                    act.wait_ge(proj_steps, g * 16 + (12 + j + 1))
                    nc.scalar.activation(vt[:, j, bass.ds(g * W, W)], acc[j][:, :], ACT.Copy).then_inc(act_evac, 1)
            act.sem_inc(sig_ready, CR_Z)
            with act.Fori(0, 2) as i:
                for u in range(2):
                    act.wait_ge(proj_steps, i * 16 + (16 * Q_B + 8 * u + 8))
                    act.wait_ge(z_ready, i * 2 + (u + CR_Z))
                    nc.scalar.activation(sig, acc[2 * u + 1][:, :], ACT.Sigmoid).then_inc(sig_ready, 1)
            act.wait_ge(conv_done, 4)
            for g in range(2):
                dst = u_sb if g == 0 else va
                for j in range(TT):
                    act.wait_ge(proj_steps, 16 * (Q_A + g) + 12 + j + 1)
                    nc.scalar.activation(dst[:, j, :], acc[j][:, :], ACT.Gelu_apprx_tanh).then_inc(act_evac, 1)
                if g == 0:
                    for j in range(4):
                        act.wait_ge(b_cent, j + 1)
                        nc.scalar.activation(sqb[:, j, :], cbuf[:, j, :], ACT.Square).then_inc(b_sq, 1)
            act.wait_ge(b_sum, 2)
            root(rb, pat[3][:, :], W)
            act.wait_ge(stat_ready, 8)
            root(rs[:, 4:8], ss[:, 4:8], W)
            for j in range(4):
                act.wait_ge(b_norm, j + 1)
                nc.scalar.activation(cbuf[:, j, :], cbuf[:, j, :], ACT.Silu, bias=col[:, K_LB + j:K_LB + j + 1],
                                     scale=col[:, K_LG + j:K_LG + j + 1]).then_inc(b_silu, 1)
            for j in range(4):
                act.wait_ge(b_silu, j + 1)
                nc.scalar.activation(sqb[:, j, :], cbuf[:, j, :], ACT.Square).then_inc(b_sq, 1)
            act.wait_ge(b_sum, 3)
            root(rb, pat[3][:, :], W)
            act.wait_ge(stat_ready, 12)
            root(rs[:, 8:12], ss[:, 8:12], W)
            for n in range(TT):
                act.wait_ge(turned, 16 + n + 1)
                evac(mixT[:, 0:4, n * P:(n + 1) * P], pat[n][:, :].rearrange("p (k n) -> p k n", k=4))

            def squares(h, q, c0):
                for w, sq in enumerate((sqq, sqk)):
                    act.wait_ge(proj_steps, q * 16 + (4 * (c0 + w) + 4))
                    if not isinstance(h, int) or h > 0:
                        act.wait_ge(qk_sum, h * 2 + (w - 1))
                    nc.scalar.activation(sq, acc[c0 + w][:, :], ACT.Square).then_inc(qk_sq, 1)

            def qk_roots(g):
                for w in range(2):
                    act.wait_ge(qk_sum, g * 2 + (w + 1))
                    nc.scalar.activation(rqk[w], pat[w][:, :], ACT.Sqrt, bias=eps[:, 0:1], scale=1.0 / P)\
                        .then_inc(qk_root, 1)

            def probs(g):
                qk_roots(g)
                for qi in range(TT):
                    n = (qi + 1) * P
                    act.wait_ge(s_masked, g * 4 + (CR_S + qi + 1))
                    nc.scalar.activation(sp_[qi % 2][:, 0:n], sp_[qi % 2][:, 0:n], ACT.Exp,
                                         bias=nmax[:, qi:qi + 1], scale=SCALE,
                                         accum_out=den[:, qi:qi + 1]).then_inc(p_ready, 1)
                    act.wait_ge(p_turned, g * 4 + (qi + 1))
                    if qi >= 2:
                        act.wait_ge(pv_done, g * 4 + (qi - 1))
                    nc.scalar.activation(pT[qi % 2][:, 0:n], pat[2][:, 0:n], ACT.Copy).then_inc(pT_ready, 1)

            act.wait_ge(b_mixed, 4)
            act.dma_start(rowc, row_c).then_inc(rowc_in, 16)
            act.sem_inc(pT_ready, CR_PT)
            squares(0, Q_QK, 0)
            with act.Fori(0, 3) as i:
                probs(i * 2)
                squares(i * 2 + 1, i + Q_QK, 2)
                probs(i * 2 + 1)
                squares(i * 2 + 2, i + (Q_QK + 1), 0)
            probs(H - 2)
            squares(H - 1, Q_QK + 3, 2)
            probs(H - 1)
            act.wait_ge(stat_ready, 16)
            root(rs[:, 12:16], ss[:, 12:16], 2 * W)
            for n in range(TT):
                for w in range(2):
                    f = 2 * n + w
                    act.wait_ge(turned, 20 + f + 1)
                    evac(mixT[:, 8 + 4 * w:12 + 4 * w, n * P:(n + 1) * P],
                         pat[f % 4][:, :].rearrange("p (k n) -> p k n", k=4))
            for f in range(16):
                t, q = divmod(f, 4)
                if q == 0:
                    act.wait_ge(stat_ready, 16 + t + 1)
                    root(rs[:, t:t + 1], ss[:, t:t + 1], D)
                act.wait_ge(turned, 28 + f + 1)
                evac(hnT[:, 4 * q:4 * q + 4, t * P:(t + 1) * P],
                     bank[f % 8][:, :].rearrange("p (k n) -> p k n", k=4))
            for n, (lo, hi) in enumerate(((R_EXG, R_EXG + TT * NG), (R_EX2, R_EX2 + TT))):
                act.wait_ge(exp_in, n + 1)
                nc.scalar.activation(rt[:, lo:hi], rt[:, lo:hi], ACT.Exp).then_inc(gate_exp, 1)

            px, py = bank[2:4], bank[4:6]
            act.sem_inc(gu_ready, CR_GU)
            act.sem_inc(sg_ready, CR_SG)
            act.sem_inc(y_evac_a, CR_Y)
            act.wait_ge(sched_ready, 1)
            nb = act.value_load(sched[0:1, P:P + 1], min_val=E, max_val=NBLK)

            def rows_turned(base):
                for w in range(2):
                    act.wait_ge(xg_turned, base + (w + 1))
                    nc.scalar.activation(xgT[:, w * W:(w + 1) * W], px[w][:, :], ACT.Copy).then_inc(xgT_ready, 1)

            rows_turned(0)
            with act.Fori(0, nb) as b:
                act.wait_ge(e_used, b * EC + (CR_E + 8))
                act.wait_ge(gu_turned, b + CR_GT)
                nc.scalar.activation(gu[0:TB, :], bank[0][0:TB, :], ACT.Copy).then_inc(gu_ready, 1)
                rows_turned(b * 2 + 2)
                act.wait_ge(gu_turned, b + (CR_GT + 1))
                act.wait_ge(hT_ready, b + CR_H)
                nc.scalar.activation(sg[:, :].rearrange("p (f n) -> p f n", f=FT), guT[:, :, 0:TB], ACT.Silu)\
                    .then_inc(sg_ready, 1)
                act.wait_ge(y_stored, b * 16 + CR_YS)
                act.wait_ge(e_used, b * EC + (CR_E + EC))
                nc.scalar.activation(ysb[:, 0:W], py[0][:, :], ACT.Copy).then_inc(y_evac_a, 1)

        @block.vector
        def _(dve):
            own = Chain(dve, dve_own)

            roots = [0]

            def inverse(ap):
                roots[0] += 1
                dve.wait_ge(root_done, roots[0])
                own.link(nc.vector.reciprocal(ap, ap))

            def sum_sq(scratch, src, c):
                nc.vector.tensor_tensor_reduce(out=scratch, in0=src, in1=src, scale=1.0, scalar=0.0,
                                               op0=ALU.mult, op1=ALU.add, accum_out=ss[:, c:c + 1])\
                    .then_inc(stat_ready, 1)

            dve.wait_ge(n1_in, 16)
            for t in range(TT):
                dve.wait_ge(x_in[t], 16)
                if t >= 2:
                    dve.wait_ge(turned, 4 * (t - 1))
                sum_sq(hn[t % 2], xh[:, t, :], t)
                inverse(rs[:, t:t + 1])
                nc.vector.scalar_tensor_tensor(out=hn[t % 2], in0=xh[:, t, :], scalar=rs[:, t:t + 1], in1=n1row,
                                               op0=ALU.mult, op1=ALU.mult).then_inc(hn_ready, 1)
            dve.wait_ge(const_in, 16 * 4)
            for hh in range(4):
                m = nc.vector.tensor_tensor(sguw[:, hh, :], sguw[:, hh, :], cst[:, C_TRI:C_TRI + P], ALU.mult)
                if hh < 3:
                    own.add(m)
            m.then_inc(sguw_ready, 1)
            for i in range(2):
                own.add(nc.vector.memset(z[i][:, 0:TAPS - 1], 0.0))
            own.wait()

            dve.sem_inc(z_ready, CR_Z)
            STEPS = TAPS
            with dve.Fori(0, 2) as i:
                for u in range(2):
                    conv = Chain(dve, conv_own, i * (2 * STEPS) + u * STEPS)
                    conv.add(nc.vector.tensor_copy(cwj[:, :], col[:, bass.ds(i * 64 + u * 32, TAPS + 1)]))
                    dve.wait_ge(proj_steps, i * 16 + (16 * Q_B + 8 * u + 4))
                    dve.wait_ge(sig_ready, i * 2 + (u + CR_Z + 1))
                    nc.vector.tensor_tensor(z[u][:, TAPS - 1:TAPS - 1 + T], acc[2 * u][:, :], sig, ALU.mult)\
                        .then_inc(z_ready, 1)
                    dve.wait_ge(z_ready, i * 2 + (u + CR_Z + 1))
                    conv.wait()
                    conv.link(nc.vector.tensor_scalar(cacc, z[u][:, 0:T], cwj[:, 0:1], cwj[:, TAPS:TAPS + 1],
                                                      ALU.mult, ALU.add))
                    for k in range(1, TAPS - 1):
                        conv.link(nc.vector.scalar_tensor_tensor(
                            out=cacc, in0=z[u][:, k:k + T], scalar=cwj[:, k:k + 1], in1=cacc,
                            op0=ALU.mult, op1=ALU.add))
                    assert conv.n == STEPS
                    nc.vector.scalar_tensor_tensor(
                        out=cbuf[:, bass.ds(i * 2 + u, 1), :].rearrange("p o n -> p (o n)"),
                        in0=z[u][:, TAPS - 1:TAPS - 1 + T], scalar=cwj[:, TAPS - 1:TAPS],
                        in1=cacc, op0=ALU.mult, op1=ALU.add).then_inc(conv_done, 1)
                    dve.wait_ge(conv_done, i * 2 + (u + 1))
            dve.wait_ge(conv_done, 4)
            dve.wait_ge(b_sum, 1)
            own.link(nc.vector.tensor_scalar(mu, pat[3][:, :], 1.0 / W, None, ALU.mult))
            for j in range(4):
                nc.vector.tensor_tensor(cbuf[:, j, :], cbuf[:, j, :], mu, ALU.subtract).then_inc(b_cent, 1)
            for n in range(TT):
                dve.wait_ge(act_evac, EV_U + 4 + n + 1)
                sum_sq(junk[:, n, 0:W], va[:, n, :], 4 + n)
            inverse(rb)
            for j in range(4):
                nc.vector.tensor_tensor(cbuf[:, j, :], cbuf[:, j, :], rb, ALU.mult).then_inc(b_norm, 1)
            inverse(rs[:, 4:4 + TT])
            for n in range(TT):
                nc.vector.scalar_tensor_tensor(out=va[:, n, :], in0=va[:, n, :], scalar=rs[:, 4 + n:5 + n],
                                               in1=rowa[:, R_SGU:R_SGU + W], op0=ALU.mult, op1=ALU.mult)\
                    .then_inc(va_normed, 1)
            inverse(rb)
            for j in range(4):
                nc.vector.scalar_tensor_tensor(out=mixT[:, 4 + j, :], in0=cbuf[:, j, :],
                                               scalar=col[:, K_OB + j:K_OB + j + 1], in1=rb,
                                               op0=ALU.mult, op1=ALU.mult).then_inc(b_mixed, 1)
            for n in range(TT):
                dve.wait_ge(spatial, n + 1)
                for hh in range(4):
                    sl = u_sb[:, n, hh * P:(hh + 1) * P]
                    own.add(nc.vector.scalar_tensor_tensor(out=sl, in0=pat[n][:, hh * P:(hh + 1) * P],
                                                           scalar=col[:, K_SB + hh:K_SB + hh + 1], in1=sl,
                                                           op0=ALU.add, op1=ALU.mult))
                own.wait()
                sum_sq(junk[:, n, 0:W], u_sb[:, n, :], 8 + n)
            inverse(rs[:, 8:8 + TT])
            for n in range(TT):
                nc.vector.scalar_tensor_tensor(out=u_sb[:, n, :], in0=u_sb[:, n, :], scalar=rs[:, 8 + n:9 + n],
                                               in1=rowa[:, R_OA:R_OA + W], op0=ALU.mult, op1=ALU.mult)\
                    .then_inc(ya_ready, 1)

            def qk_norm(g, c0):
                for w, dst in enumerate((qT[c0 // 2], kT[c0 // 2])):
                    dve.wait_ge(qk_root, g * 2 + (w + 1))
                    nc.vector.reciprocal(rqk[w], rqk[w]).then_inc(r_own, 1)
                    dve.wait_ge(r_own, g * 2 + (w + 1))
                    nc.vector.scalar_tensor_tensor(out=dst, in0=acc[c0 + w][:, :], scalar=col[:, K_Q + w:K_Q + w + 1],
                                                   in1=rqk[w], op0=ALU.mult, op1=ALU.mult).then_inc(qkT_ready, 1)

            def mask_max(g):
                for qi in range(TT):
                    n = (qi + 1) * P
                    if qi >= 2:
                        dve.wait_ge(p_turned, g * 4 + (qi - 1))
                    wait_alone(dve, (s_ready, g * 4 + (qi + 1)))
                    nc.vector.tensor_tensor_reduce(
                        out=sp_[qi % 2][:, 0:n], in0=pat[qi % 2][:, 0:n], in1=cst[:, C_BAND + T - n:C_BAND + T],
                        scale=1.0, scalar=-3.0e38, op0=ALU.add, op1=ALU.max, accum_out=pmax[:, qi:qi + 1])\
                        .then_inc(s_max, 1)
                    dve.wait_ge(s_max, g * 4 + (qi + 1))
                    nc.vector.tensor_scalar(nmax[:, qi:qi + 1], pmax[:, qi:qi + 1], -SCALE, None, ALU.mult)\
                        .then_inc(s_masked, 1)

            def rows_out(g):
                dve.wait_ge(p_ready, g * 4 + 4)
                nc.vector.reciprocal(rden[:, :], den[:, 0:TT]).then_inc(rden_ready, 1)
                dve.wait_ge(rden_ready, g + 1)
                dve.wait_ge(pv_done, g * 4 + 4)
                for qi in range(TT):
                    dst = yc[:, qi, g * P:(g + 1) * P] if isinstance(g, int) else yc[:, qi, bass.ds(g * P, P)]
                    m = nc.vector.tensor_scalar(dst, pat[3][:, qi * P:(qi + 1) * P], rden[:, qi:qi + 1], None, ALU.mult)
                m.then_inc(o_done, 1)

            dve.wait_ge(turned, 20)
            dve.sem_inc(qkT_ready, CR_QK)
            dve.sem_inc(s_masked, CR_S)
            dve.sem_inc(o_done, CR_O)
            with dve.Fori(0, 3) as i:
                for u in range(2):
                    qk_norm(i * 2 + u, 2 * u)
                    mask_max(i * 2 + u)
                    rows_out(i * 2 + u)
            for g in range(H - 2, H):
                qk_norm(g, 2 * (g % 2))
                mask_max(g)
                rows_out(g)
            dve.wait_ge(o_done, CR_O + H)
            for n in range(TT):
                sum_sq(junk[:, n, :], yc[:, n, :], 12 + n)
            inverse(rs[:, 12:12 + TT])
            dve.wait_ge(rowc_in, 16)
            for n in range(TT):
                nc.vector.scalar_tensor_tensor(out=yc[:, n, :], in0=yc[:, n, :], scalar=rs[:, 12 + n:13 + n],
                                               in1=rowc, op0=ALU.mult, op1=ALU.mult).then_inc(yc_ready, 1)
            with dve.Fori(0, 4) as g:
                for j in range(TT):
                    dve.wait_ge(proj_steps, g * 16 + (16 * Q_O + 12 + j + 1))
                    nc.vector.tensor_tensor(xh[:, j, bass.ds(g * W, W)], acc[j][:, :], xh[:, j, bass.ds(g * W, W)],
                                            ALU.add).then_inc(h_added, 1)
            dve.wait_ge(h_added, 16)
            dve.wait_ge(n2_in, 48)
            for t in range(TT):
                sum_sq(h2[:, t, :], xh[:, t, :], t)
                inverse(rs[:, t:t + 1])
                nc.vector.scalar_tensor_tensor(out=h2[:, t, :], in0=xh[:, t, :], scalar=rs[:, t:t + 1], in1=n2row,
                                               op0=ALU.mult, op1=ALU.mult).then_inc(h2_ready, 1)

            def r3(o, n):
                return rt[:, o:o + TT * n].rearrange("p (t n) -> p t n", t=TT)

            def per_tile(ap, n):
                return ap.unsqueeze(2).to_broadcast([P, TT, n])

            taken, oh1, oh2 = r3(R_TAKEN, E), r3(R_OH1, E), r3(R_OH2, E)
            lg, le, eq, pos = r3(R_LG, 36), r3(R_LE, E), r3(R_EQ, E), r3(R_POS, E)
            exg, eqg = r3(R_EXG, NG), r3(R_EQG, NG)
            one = lambda i: rt[:, R_ONE + TT * i:R_ONE + TT * (i + 1)]
            gmax, gsum, gi, m1, i1, m2, i2, gg, g2r, den2, d1 = (one(i) for i in range(11))
            ex2 = rt[:, R_EX2:R_EX2 + TT]
            c3 = lambda o, n: cst[:, o:o + TT * n].rearrange("p (t n) -> p t n", t=TT)
            v = nc.vector
            dve.wait_ge(logits, 1)
            own.link(v.tensor_tensor(lg, bank[0][:, 0:TT * 36].rearrange("p (t n) -> p t n", t=TT), rbr, ALU.add))
            own.link(v.tensor_reduce(gmax, lg[:, :, 0:NG], AX, ALU.max))
            v.tensor_tensor(exg, lg[:, :, 0:NG], per_tile(gmax, NG), ALU.subtract).then_inc(exp_in, 1)
            own.link(v.tensor_tensor(eqg, lg[:, :, 0:NG], per_tile(gmax, NG), ALU.is_equal))
            own.link(v.scalar_tensor_tensor(out=eqg, in0=eqg, scalar=-BIG, in1=c3(C_GI, NG), op0=ALU.mult, op1=ALU.add))
            own.link(v.tensor_reduce(gi, eqg, AX, ALU.min))
            own.link(v.tensor_tensor(eq, c3(C_EG, E), per_tile(gi, E), ALU.not_equal))
            own.link(v.scalar_tensor_tensor(out=le, in0=eq, scalar=OFF, in1=lg[:, :, NG:36], op0=ALU.mult, op1=ALU.add))

            def largest(mx, ix, oh):
                own.link(v.tensor_reduce(mx, le, AX, ALU.max))
                own.link(v.tensor_tensor(eq, le, per_tile(mx, E), ALU.not_equal))
                own.link(v.scalar_tensor_tensor(out=pos, in0=eq, scalar=BIG, in1=c3(C_EI, E), op0=ALU.mult, op1=ALU.add))
                own.link(v.tensor_reduce(ix, pos, AX, ALU.min))
                own.link(v.tensor_tensor(oh, c3(C_EI, E), per_tile(ix, E), ALU.is_equal))

            largest(m1, i1, oh1)
            own.link(v.scalar_tensor_tensor(out=le, in0=oh1, scalar=GONE, in1=le, op0=ALU.mult, op1=ALU.add))
            largest(m2, i2, oh2)
            v.tensor_tensor(taken, oh1, oh2, ALU.add).then_inc(picked, 1)
            v.tensor_tensor(ex2, m2, m1, ALU.subtract).then_inc(exp_in, 1)
            dve.wait_ge(gate_exp, 2)
            own.link(v.tensor_reduce(gsum, exg, AX, ALU.add))
            own.link(v.tensor_scalar(den2, ex2, 1.0, None, ALU.add))
            own.link(v.tensor_tensor(den2, den2, gsum, ALU.mult))
            own.link(v.reciprocal(gates[:, 0, :], den2))
            own.link(v.tensor_tensor(gates[:, 1, :], gates[:, 0, :], ex2, ALU.mult))
            dve.wait_ge(ranked, 1)
            cnt, nblk = rt[:, R_CNT:R_CNT + E], rt[:, R_NB:R_NB + E]
            own.link(v.tensor_copy(cnt, bank[1][:, TT * E:(TT + 1) * E]))
            own.link(v.tensor_scalar(nblk, cnt, float(TB), 1.0, ALU.is_gt, ALU.add))
            for m in range(2, T // TB):
                own.link(v.scalar_tensor_tensor(out=nblk, in0=cnt, scalar=float(m * TB), in1=nblk,
                                                op0=ALU.is_gt, op1=ALU.add))
            a, bb = rt[:, R_SA:R_SA + E], rt[:, R_SB:R_SB + E]
            own.link(v.tensor_copy(a, nblk))
            s = 1
            while s < E:
                own.add(v.tensor_copy(bb[:, 0:s], a[:, 0:s]))
                own.link(v.tensor_tensor(bb[:, s:E], a[:, s:E], a[:, 0:E - s], ALU.add))
                a, bb = bb, a
                s *= 2
            own.link(v.tensor_copy(sched[0:1, P:P + 1], a[0:1, E - 1:E]))
            own.link(v.tensor_tensor(bb, a, nblk, ALU.subtract))
            own.link(v.tensor_scalar(cnt, bb, cst[:, C_P:C_P + 1], None, ALU.is_le))
            own.link(v.tensor_reduce(ss[:, 14:15], cnt, AX, ALU.add))
            v.tensor_scalar(ss[:, 15:16], ss[:, 14:15], -1.0, None, ALU.add).then_inc(sched_col, 1)
            own.link(v.tensor_scalar(bb, bb, float(TB), None, ALU.mult))
            for t in range(TT):
                own.add(v.tensor_tensor(pos[:, t, :], bank[1][:, t * E:(t + 1) * E], bb, ALU.add))
            own.wait()
            for k, oh in enumerate((oh1, oh2)):
                own.link(v.tensor_tensor(eq, pos, oh, ALU.mult))
                own.link(v.tensor_reduce(d1, eq, AX, ALU.add))
                own.link(v.tensor_copy(dest_i[:, k, :], d1))
            own.link(v.tensor_scalar(tmp_i[:, :, :], dest_i[:, :, :], TB.bit_length() - 1, None,
                                     ALU.logical_shift_right))
            own.link(v.tensor_scalar(tmp_i[:, :, :], tmp_i[:, :, :], 1 - TB * NT, None, ALU.mult))
            v.scalar_tensor_tensor(out=dest_i[:, :, :], in0=dest_i[:, :, :], scalar=float(NT), in1=tmp_i[:, :, :],
                                   op0=ALU.mult, op1=ALU.add).then_inc(dest_ready, 1)
            dve.wait_ge(sched_row, 1)
            v.tensor_copy(sched[0:1, 0:P], bank[2][0:1, 0:P]).then_inc(sched_ready, 1)

            dve.sem_inc(gu_turned, CR_GT)
            dve.sem_inc(hT_ready, CR_H)
            dve.sem_inc(y_evac_v, CR_Y)
            dve.wait_ge(sched_ready, 1)
            nb = dve.value_load(sched[0:1, P:P + 1], min_val=E, max_val=NBLK)
            with dve.Fori(0, nb) as b:
                dve.wait_ge(e_used, b * EC + (CR_E + 8))
                dve.wait_ge(gu_turned, b + CR_GT)
                v.tensor_copy(gu[TB:P, :], bank[0][TB:P, :]).then_inc(gu_ready, 1)
                dve.wait_ge(sg_ready, b + (CR_SG + 1))
                dve.wait_ge(e_used, b * EC + CR_E)
                v.tensor_tensor(hT[:, :].rearrange("p (f n) -> p f n", f=FT), guT[:, :, TB:P],
                                sg[:, :].rearrange("p (f n) -> p f n", f=FT), ALU.mult).then_inc(hT_ready, 1)
                dve.wait_ge(y_stored, b * 16 + CR_YS)
                for h in range(2):
                    v.tensor_copy(idx_row[h * TB:(h + 1) * TB, :],
                                  tab[h * TB:(h + 1) * TB, bass.ds(b, 1), h + 1:h + 2]
                                  .rearrange("p o n -> p (o n)")).then_inc(idx_r_ready, 1)
                dve.wait_ge(e_used, b * EC + (CR_E + EC))
                v.tensor_copy(ysb[:, W:2 * W], bank[5][:, :]).then_inc(y_evac_v, 1)
            for t in range(TT):
                h = xh[:, t, :]
                dve.wait_ge(yrow_in[t], 32)
                v.scalar_tensor_tensor(out=h, in0=yrow[t][0], scalar=gates[:, 0, t:t + 1], in1=h,
                                       op0=ALU.mult, op1=ALU.add).then_inc(part_sum, 1)
                dve.wait_ge(part_sum, t + 1)
                v.scalar_tensor_tensor(out=h, in0=yrow[t][1], scalar=gates[:, 1, t:t + 1], in1=h,
                                       op0=ALU.mult, op1=ALU.add).then_inc(out_ready, 1)


R_TAKEN, R_OH1, R_OH2, R_LE, R_EQ, R_POS = (TT * E * i for i in range(6))
R_LG = TT * E * 6
R_EXG = R_LG + TT * 36
R_EQG = R_EXG + TT * NG
R_EX2 = R_EQG + TT * NG
R_ONE = R_EX2 + TT
R_CNT = R_ONE + TT * 11
R_NB = R_CNT + E
R_SA = R_NB + E
R_SB = R_SA + E


def shape_constants():
    c = np.zeros((P, NC_CONST), np.float32)
    p = np.arange(P)
    c[:, C_ID:C_ID + P] = np.eye(P)
    c[:, C_ONE:C_ONE + P] = 1.0
    c[:, C_LOW:C_LOW + P] = p[:, None] < p[None, :]
    c[:, C_TRI:C_TRI + P] = p[:, None] <= p[None, :]
    d = p[:, None] + (T - P) - np.arange(T)[None, :]
    n = np.zeros(d.shape)
    for window, dil in ((128, 1), (512, 4), (2048, 16)):
        n += (d >= 0) & (d <= window) & (d % dil == 0)
    c[:, C_BAND:C_BAND + T] = np.where(n > 0, np.log(np.maximum(n, 1)) / SCALE, OFF)
    c[:, C_GI:C_GI + TT * NG] = np.tile(np.arange(NG) + BIG, TT)
    c[:, C_EI:C_EI + TT * E] = np.tile(np.arange(E), TT)
    c[:, C_EG:C_EG + TT * E] = np.tile(np.arange(E) // EG, TT)
    c[:, C_P] = p
    pairs = np.zeros((P, 2 * TT, 4), np.int32)
    for k in range(2):
        for t in range(TT):
            pairs[:, k * TT + t, 0] = t * P + p
            for h in range(2):
                pairs[:, k * TT + t, 1 + h] = 2 * (k * T + t * P + p) + h
    return c, pairs


def kernel(**inputs):
    import concourse.bacc as bacc
    from concourse.bass_utils import run_bass_kernel_spmd

    a = {k: np.asarray(v) for k, v in inputs.items()}
    consts, pairs = shape_constants()

    def by_tile(v):
        return v.reshape(-1, P).T

    def spread(v):
        return np.broadcast_to(v, (P, v.shape[-1]))

    cols = np.concatenate([
        np.concatenate([a["conv_w"][0], a["conv_b"]]).reshape(TAPS + 1, 4, P).transpose(2, 1, 0).reshape(P, -1),
        by_tile(a["conv_ln_g"][0]), by_tile(a["conv_ln_b"][0]),
        by_tile(a["out_norm"][0, W:2 * W]), a["q_norm"][0][:, None], a["k_norm"][0][:, None],
        a["sgu_b"][0].T], axis=1)
    w_in, w_out = a["w_in"][0], a["w_out"][0]
    U, VA, CA, CG, QQ, KK, VV = 0, 512, 1024, 1536, 2048, 3072, 4096

    def token_group(w, c0):
        return w[:, c0:c0 + W].reshape(4, 4, P, W).transpose(0, 2, 1, 3).reshape(4, P, CH)

    def tiles(*starts):
        return np.stack([w_in[:, c:c + P].reshape(KT, P, P).transpose(1, 0, 2).reshape(P, CH) for c in starts])

    stream = np.concatenate(
        [token_group(w_in, VV), token_group(w_in, VV + W)]
        + [tiles(CA + j * P, CG + j * P) for j in range(4)]
        + [token_group(w_in, U), token_group(w_in, VA)]
        + [tiles(QQ + h * P, KK + h * P) for h in range(H)]
        + [token_group(w_out, g * W) for g in range(4)])
    w_rt = np.concatenate([a["w_router_group"][0], a["w_router_expert"][0]], axis=1)
    w_rt = w_rt.reshape(KT, P, 36).transpose(1, 0, 2)
    rbias = np.broadcast_to(np.concatenate([a["b_router_group"][0], a["b_router_expert"][0]]), (P, TT, 36))
    ins = {
        "x": a["x"][0], "consts": consts, "pairs": pairs, "cols": cols,
        "rows_a": np.concatenate([spread(a["sgu_norm"][0]), spread(a["out_norm"][0, :W])], axis=1),
        "row_c": spread(a["out_norm"][0, 2 * W:]), "row_n1": spread(a["norm1"][0]),
        "row_n2": spread(a["norm2"][0]), "rbias": rbias, "sgu_wt": a["sgu_w"][0].transpose(2, 0, 1),
        "w_stream": stream, "w_rt": w_rt,
        "w_gate": a["w_expert_gate"][0], "w_up": a["w_expert_up"][0], "w_down": a["w_expert_down"][0],
    }
    ins = {f"in_{k}": np.ascontiguousarray(v) for k, v in ins.items()}
    nc = bacc.Bacc("TRN2", target_bir_lowering=False, num_devices=1)
    args = [nc.dram_tensor(k, list(v.shape), mybir.dt.from_np(v.dtype), kind="ExternalInput").ap()
            for k, v in ins.items()]
    out = nc.dram_tensor("out_rows", [T, D], F32, kind="ExternalOutput").ap()
    build(nc, *args, out)
    r = run_bass_kernel_spmd(nc, [ins], core_ids=[0])
    return r.results[0]["out_rows"].reshape(1, T, D)
```

```python
import math
from contextlib import ExitStack

import numpy as np

import concourse.bass as bass
from concourse import mybir

F32 = mybir.dt.float32
I32 = mybir.dt.int32
F32R = mybir.dt.float32r
ALU = mybir.AluOpType
ACT = mybir.ActivationFunctionType
AX = mybir.AxisListType.X

P = 128
T = 512
D = 2048
TT = T // P
KT = D // P
W = 512
CH = 2048
HC = CH // 2
QS = 32
H = 8
TAPS = 31
E = 32
EG = 8
NG = E // EG
FE = 512
FT = FE // P
TB = 64
NBLK = E + 2 * T // TB
NT = NBLK + 1
RC = 64
EC = 12
EPS = 1e-6
SCALE = P ** -0.5
OFF = -1.0e30
GONE = -3.0e38
NOWHERE = 1 << 20
BIG = 64.0

C_ID, C_ONE, C_LOW, C_TRI, C_BAND = 0, 128, 256, 384, 512
C_GI = C_BAND + W
C_EI = C_GI + TT * NG
C_EG = C_EI + TT * E
C_P = C_EG + TT * E
C_HALF = C_P + 1
C_TH = C_HALF + 1
C_SLOT = C_TH + T // TB - 1
C_BLK = C_SLOT + P
C_PAIR = C_BLK + NT
C_FOLD = C_PAIR + 2 * TT
NC_CONST = C_FOLD + 36

K_CW, K_LG, K_LB, K_OB = 0, 128, 132, 136
K_Q, K_K, K_SB = 140, 141, 142
K_N2, K_N2R = 146, 162
NC_COLS = 178

R_SGU, R_OA = 0, 512

Q_V, Q_B, Q_A, Q_QK, Q_O, QUADS = 0, 2, 4, 6, 10, 14


class Chain:

    def __init__(self, eng, sem, base=0):
        self.eng, self.sem, self.base, self.n = eng, sem, base, 0

    def add(self, ins):
        ins.then_inc(self.sem, 1)
        self.n += 1

    def wait(self):
        self.eng.wait_ge(self.sem, self.base + self.n)

    def link(self, ins):
        self.add(ins)
        self.wait()


def build(nc, x, consts, cols, rows_a, row_c, row_n1, rbias, sgu_wt, w_stream, w_rt,
          w_gate, w_up, w_down, out):
    with ExitStack() as ctx:
        def sb(name, shape, dt=F32):
            return ctx.enter_context(nc.sbuf_tensor(name, shape, dt))

        def sem(name):
            return ctx.enter_context(nc.semaphore(name))

        h_dram = nc.dram_tensor("h_rows", [T, D], F32, kind="Internal").ap()
        y_dram = nc.dram_tensor("y_rows", [4 * T, D // 2], F32, kind="Internal").ap()

        def shared(*shapes):
            with ExitStack() as place:
                return [place.enter_context(nc.sbuf_tensor(name, shape, dt)) for name, shape, dt in shapes]

        _, w_parts = shared(("stream_slots", [P, 2 * CH], F32), ("w_parts", [P, 2 * CH], F32R))
        arena = sb("arena", [P, EC * CH])
        hn_low, = shared(("hn_low", [P, KT, T], F32R))
        xh = sb("xh", [P, TT, D])
        hn_high, = shared(("hn_high", [P, KT, T], F32R))
        hnT = sb("hnT", [P, KT, T])
        mix_ab, = shared(("mix_ab", [P, KT, T], F32R))
        mixT = sb("mixT", [P, KT, T])
        cst = sb("cst", [P, NC_CONST])
        col = sb("col", [P, NC_COLS])
        rowa = sb("rowa", [P, 2 * W])
        sguw = sb("sguw", [P, 4, P])
        ss = sb("ss", [P, 16])
        rs = sb("rs", [P, 16])
        nmax = sb("nmax", [P, TT])
        pmax = sb("pmax", [P, TT])
        den = sb("den", [P, 2 * TT])
        rden = sb("rden", [P, TT])
        cwj = sb("cwj", [P, 32])
        eps = sb("eps", [P, 1])
        dest_i = sb("dest_i", [P, 2, TT], I32)
        gates = sb("gates", [P, 2, TT])
        sched = sb("sched", [1, P + 1], I32)
        tab_tok = sb("tab_tok", [TB, NT], I32)
        tab_row = sb("tab_row", [P, NT], I32)
        tab_rs = sb("tab_rs", [P, NT])
        slot_i = sb("slot_i", [P, 2, TT], I32)
        blk_i = sb("blk_i", [P, 2, TT], I32)
        ss_h = sb("ss_h", [P, TT, 4])
        idx_tok = sb("idx_tok", [TB, 1], I32)
        idx_row = sb("idx_row", [2 * TB, 1], I32)

        ident = cst[:, C_ID:C_ID + P]
        ones = cst[:, C_ONE:C_ONE + P]
        low = cst[:, C_LOW:C_LOW + P]

        def rows_by_tile(ap):
            return ap.rearrange("(t p) n -> p t n", p=P)

        def slot(c):
            return arena[:, c * CH:(c + 1) * CH]

        w_hi = [w_parts[:, i * HC:(i + 1) * HC] for i in range(2)]
        w_lo = [w_parts[:, CH + i * HC:CH + (i + 1) * HC] for i in range(2)]
        x_rows = mixT[:, :, :].rearrange("p k t -> p (k t)").rearrange("p (t n) -> p t n", t=TT)

        def hn_parts(k):
            return hn_high[:, k, :], hn_low[:, k, :]

        def mix_parts(k):
            home = mix_ab if k < 8 else mix_c
            return home[:, k % 8, :], home[:, 8 + k % 8, :]

        mix_c = hn_high

        def low_part(eng, low, x, high):
            return eng.tensor_tensor(low, x, high.bitcast(F32), ALU.subtract)

        vt = arena[:, 4 * CH:6 * CH].rearrange("p (t n) -> p t n", t=TT)
        tmp = arena[:, 6 * CH:12 * CH]
        n1row = tmp[:, 0:2048]
        hn = [tmp[:, 2048:4096], tmp[:, 4096:6144]]
        x_sq = tmp[:, 6144:8192]
        u_sb = tmp[:, 0:2048].rearrange("p (t n) -> p t n", t=TT)
        va = tmp[:, 2048:4096].rearrange("p (t n) -> p t n", t=TT)
        BB = 6144
        sig = tmp[:, BB:BB + 512]
        ZW = W + 32
        z = [tmp[:, BB + 512 + ZW * i:BB + 512 + ZW * (i + 1)] for i in range(2)]
        sqb = tmp[:, BB:BB + 2048].rearrange("p (j n) -> p j n", j=4)
        cbuf = tmp[:, BB + 2112:BB + 4160].rearrange("p (j n) -> p j n", j=4)
        mu = tmp[:, BB + 4160:BB + 4672]
        rb = tmp[:, BB + 4672:BB + 5184]
        yc = tmp[:, 0:4096].rearrange("p (t n) -> p t n", t=TT)
        qT = [tmp[:, 4096 + 1024 * i:4608 + 1024 * i] for i in range(2)]
        kT = [tmp[:, 4608 + 1024 * i:5120 + 1024 * i] for i in range(2)]
        sqq, sqk = tmp[:, 6144:6656], tmp[:, 6656:7168]
        rqk = [tmp[:, 7168:7680], tmp[:, 10752:11264]]
        sp_ = [tmp[:, 7680 + 512 * i:8192 + 512 * i] for i in range(2)]
        pT = [tmp[:, 8704 + 512 * i:9216 + 512 * i] for i in range(2)]
        rowc = tmp[:, 9728:10752]
        wrt = tmp[:, 4 * CH:4 * CH + KT * RC].rearrange("p (k n) -> p k n", n=RC)
        rbr = tmp[:, 4 * CH + 1024:4 * CH + 1024 + TT * 36].rearrange("p (t n) -> p t n", t=TT)
        h_sq = tmp[:, 4 * CH + 1200:4 * CH + 1712]
        hT_all = arena[:, 4 * CH:8 * CH].rearrange("p (k n) -> p k n", k=KT)
        junk_a = mixT[:, 8:12, :]
        junk_c = hnT[:, 0:8, :].rearrange("p (t k) n -> p t (k n)", t=TT)
        rt = hnT[:, :, :].rearrange("p k t -> p (k t)")
        logitT = rt[:, 6144:6144 + T]
        oh_slot = rt[:, 2048:2048 + 2 * TT * P].rearrange("p (i n) -> p i n", n=P)
        oh_blk, oh_pair, oh_rs = (rt[:, 3072 + 512 * i:3072 + 512 * i + 2 * TT * NT]
                                  .rearrange("p (i n) -> p i n", n=NT) for i in range(3))
        blk = mixT[:, :, :].rearrange("p k t -> p (k t)")
        xg = blk[0:TB, 0:D]
        ysb = blk[:, D:D + 2 * W]
        gu = blk[:, D + 2 * W:D + 3 * W]
        xgT = blk[:, 2 * D:2 * D + KT * TB]
        sg, hT = (blk[:, 5120 + i * FT * TB:5120 + (i + 1) * FT * TB] for i in range(2))
        yrow = [[slot(2 * t + k) for k in range(2)] for t in range(TT)]

        bank = [ctx.enter_context(nc.psum_tensor(f"bank{i}", [P, W], F32)) for i in range(8)]
        acc, pat = bank[0:4], bank[4:8]
        u_bank = acc[0:2] + pat[1:3]
        cacc = pat[0][:, :]
        guT = bank[1][:, :].rearrange("p (f n) -> p f n", f=FT)

        eps_set = sem("eps_set")
        x_in = [sem(f"x_in{t}") for t in range(TT)]
        const_in = sem("const_in")
        ident_in = sem("ident_in")
        n1_in = sem("n1_in")
        rowc_in = sem("rowc_in")
        n2_in = sem("n2_in")
        w_in_slot = [sem(f"w_in_slot{c}") for c in range(2)]
        w_hi_ready = sem("w_hi_ready")
        w_lo_ready = sem("w_lo_ready")
        lo_evac = sem("lo_evac")
        dve_own = sem("dve_own")
        hn_ready = sem("hn_ready")
        turned = sem("turned")
        act_evac = sem("act_evac")
        proj_steps = sem("proj_steps")
        z_ready = sem("z_ready")
        sig_ready = sem("sig_ready")
        conv_own = sem("conv_own")
        conv_done = sem("conv_done")
        b_sum = sem("b_sum")
        b_cent = sem("b_cent")
        b_norm = sem("b_norm")
        b_sq = sem("b_sq")
        b_silu = sem("b_silu")
        b_mixed = sem("b_mixed")
        sguw_ready = sem("sguw_ready")
        va_normed = sem("va_normed")
        spatial = sem("spatial")
        ya_ready = sem("ya_ready")
        qk_sq = sem("qk_sq")
        qk_sum = sem("qk_sum")
        qkT_ready = sem("qkT_ready")
        qk_root = sem("qk_root")
        r_own = sem("r_own")
        stat_ready = sem("stat_ready")
        root_done = sem("root_done")
        s_ready = sem("s_ready")
        s_max = sem("s_max")
        s_masked = sem("s_masked")
        p_ready = sem("p_ready")
        p_turned = sem("p_turned")
        pT_ready = sem("pT_ready")
        pv_done = sem("pv_done")
        rden_ready = sem("rden_ready")
        o_done = sem("o_done")
        yc_ready = sem("yc_ready")
        h_added = sem("h_added")
        h_sq_done = sem("h_sq_done")
        wrt_scaled = sem("wrt_scaled")
        h_stored = sem("h_stored")
        logitT_ready = sem("logitT_ready")
        folded = sem("folded")
        logits = sem("logits")
        gate_exp = sem("gate_exp")
        exp_in = sem("exp_in")
        picked = sem("picked")
        ranked = sem("ranked")
        sched_col = sem("sched_col")
        sched_row = sem("sched_row")
        sched_ready = sem("sched_ready")
        onehots = sem("onehots")
        tabs_made = sem("tabs_made")
        tabs_ready = sem("tabs_ready")
        xg_zero = sem("xg_zero")
        e_in_slot = [sem(f"e_in_slot{c}") for c in range(EC)]
        e_used = sem("e_used")
        idx_t_ready = sem("idx_t_ready")
        idx_r_ready = sem("idx_r_ready")
        xg_in = sem("xg_in")
        xg_turned = sem("xg_turned")
        xgT_ready = sem("xgT_ready")
        gu_ready = sem("gu_ready")
        gu_turned = sem("gu_turned")
        sg_ready = sem("sg_ready")
        hT_ready = sem("hT_ready")
        y_evac_a = sem("y_evac_a")
        y_evac_v = sem("y_evac_v")
        y_stored = sem("y_stored")
        yrow_in = [sem(f"yrow_in{t}") for t in range(TT)]
        part_sum = sem("part_sum")
        out_ready = sem("out_ready")
        out_stored = sem("out_stored")

        CR_Z, CR_QK, CR_S, CR_PT, CR_O = 2, 2, 4, 4, 1
        CR_E, CR_GU, CR_GT, CR_SG, CR_H, CR_Y, CR_YS = EC, 1, 1, 1, 1, 1, 16
        EV_V = 16
        EV_U = EV_V + 8
        EV_A = EV_U + 8
        EV_C = EV_A + 4
        EV_R = EV_C + 8
        EV_END = EV_R + 16

        counts = {}

        def wait_alone(eng, *waits):
            for i in range(len(waits)):
                if (eng, i) not in counts:
                    counts[eng, i] = eng.alloc_register(f"count{i}")
                eng.reg_mov(counts[eng, i], waits[i][1])
            eng.wait_ge(const_in, 16 * 3)
            for i, (s, _) in enumerate(waits):
                eng.wait_ge(s, counts[eng, i])

        block = ctx.enter_context(nc.Block())

        @block.sync
        def _(sp):
            sp.dma_start(x_rows[:, 0, :], x[0:P, :]).then_inc(x_in[0], 16)
            sp.dma_start(n1row, row_n1).then_inc(n1_in, 16)
            sp.dma_start(cst[:, :], consts).then_inc(ident_in, 16)
            for t in range(1, TT):
                sp.dma_start(x_rows[:, t, :], x[t * P:(t + 1) * P, :]).then_inc(x_in[t], 16)
            for c in range(2):
                sp.dma_start(slot(c), w_stream[c]).then_inc(w_in_slot[c], 16)
            sp.dma_start(col[:, :], cols).then_inc(const_in, 16)
            sp.dma_start(rowa[:, :], rows_a).then_inc(const_in, 16)
            sp.dma_start(sguw[:, :, :], sgu_wt).then_inc(const_in, 16)

            def stream(q, c):
                src = w_stream[4 * q + c] if isinstance(q, int) else \
                    w_stream[bass.ds(q * 4 + c, 1)].rearrange("o p n -> (o p) n")
                wait_alone(sp, (w_lo_ready, q * 16 + (4 * c - 4)))
                sp.dma_start(slot(c % 2), src).then_inc(w_in_slot[c % 2], 16)

            for c in range(2, 4):
                stream(0, c)
            with sp.Fori(1, Q_O) as q:
                for c in range(4):
                    stream(q, c)
            for c in range(4):
                stream(Q_O, c)
            sp.wait_ge(proj_steps, QS * Q_O)
            for t in range(TT):
                sp.dma_start(xh[:, t, :], x[t * P:(t + 1) * P, :]).then_inc(x_in[t], 16)
            with sp.Fori(Q_O + 1, QUADS) as q:
                for c in range(4):
                    stream(q, c)

            def expert(c, e):
                if c < 8:
                    m = w_gate if c % 2 == 0 else w_up
                    k = (c // 2) * 4
                    return m[e].rearrange("o (p k) n -> (o p) k n", k=KT)[:, k:k + 4, :]
                return w_down[e].rearrange("o (f p) n -> f (o p) n", p=P)[c - 8]

            def dst(c):
                return slot(c).rearrange("p (k n) -> p k n", k=4) if c < 8 else slot(c)

            def first_expert(*chunks):
                for c in chunks:
                    sp.dma_start(dst(c), expert(c, slice(0, 1))).then_inc(e_in_slot[c], 16)

            sp.wait_ge(lo_evac, 28)
            first_expert(8, 9, 11)
            sp.wait_ge(h_added, 4 * TT)
            sp.dma_start(rows_by_tile(h_dram)[:, :, 3 * W:], xh[:, :, 3 * W:]).then_inc(h_stored, 16)
            sp.wait_ge(w_lo_ready, 16 * QUADS)
            first_expert(0, 1)
            sp.wait_ge(proj_steps, QS * QUADS)
            first_expert(2, 3)
            sp.wait_ge(logits, 1)
            first_expert(4, 5, 6, 7)
            sp.wait_ge(picked, 1)
            first_expert(10)
            sp.wait_ge(sched_ready, 1)
            nb = sp.value_load(sched[0:1, P:P + 1], min_val=E, max_val=NBLK)
            with sp.Fori(1, nb) as b:
                e = sp.value_load(sched[0:1, bass.ds(b, 1)], min_val=0, max_val=E - 1)
                before = sp.value_load(sched[0:1, bass.ds(b - 1, 1)], min_val=0, max_val=E - 1)
                for c in range(EC):
                    wait_alone(sp, (e_used, b * EC + (c + 1)))
                    sp.dma_start(dst(c), expert(c, bass.ds(e, 1)), cond=(e != before))\
                        .then_inc(e_in_slot[c], 16)
            sp.wait_ge(y_stored, nb * 16 + CR_YS)
            for t in range(TT):
                for k in range(2):
                    r = k * T + t * P
                    sp.dma_start(yrow[t][k], y_dram.rearrange("(r h) n -> r (h n)", h=2)[r:r + P, :])\
                        .then_inc(yrow_in[t], 16)
            for t in range(TT):
                sp.wait_ge(out_ready, t + 1)
                sp.dma_start(out[t * P:(t + 1) * P, :], xh[:, t, :]).then_inc(out_stored, 16)
            sp.wait_ge(out_stored, 16 * TT)

        @block.gpsimd
        def _(pool):
            pool.memset(eps[:, :], EPS).then_inc(eps_set, 1)
            with pool.Fori(0, QUADS) as q:
                for h in range(8):
                    for i in range(2):
                        c0 = i * W
                        pool.wait_ge(w_hi_ready, q * 8 + (h + 1))
                        low_part(pool, w_lo[h % 2][:, c0:c0 + W],
                                 slot((h // 2) % 2)[:, (h % 2) * HC + c0:(h % 2) * HC + c0 + W],
                                 w_hi[h % 2][:, c0:c0 + W]).then_inc(w_lo_ready, 1)
            pool.wait_ge(proj_steps, QS * QUADS)
            pool.memset(xg, 0.0).then_inc(xg_zero, 1)
            pool.wait_ge(xg_zero, 1)
            pool.wait_ge(tabs_ready, 1)

            def tokens(b):
                pool.tensor_copy(idx_tok[:, :], tab_tok[:, b]).then_inc(idx_t_ready, 1)

            def gather():
                pool.indirect_dma_start(
                    out=xg, out_offset=None, in_=h_dram,
                    in_offset=bass.IndirectOffsetOnAxis(ap=idx_tok[:, 0:1], axis=0),
                    bounds_check=T - 1, oob_is_err=False).then_inc(xg_in, 16)

            tokens(slice(0, 1))
            pool.wait_ge(idx_t_ready, 1)
            pool.wait_ge(h_stored, 16 * TT)
            gather()
            pool.dma_start(idx_row[0:1, :].bitcast(F32), x[0:1, 0:1]).then_inc(y_stored, CR_YS)
            pool.wait_ge(sched_ready, 1)
            nb = pool.value_load(sched[0:1, P:P + 1], min_val=E, max_val=NBLK)
            with pool.Fori(0, nb) as b:
                wait_alone(pool, (xg_in, b * 16 + 16))
                tokens(bass.ds(b + 1, 1))
                wait_alone(pool, (idx_t_ready, b + 2), (xg_turned, b * 2 + 2))
                gather()
                wait_alone(pool, (idx_r_ready, b + 1), (y_evac_a, b + (CR_Y + 1)),
                           (y_evac_v, b + (CR_Y + 1)))
                pool.indirect_dma_start(
                    out=y_dram, out_offset=bass.IndirectOffsetOnAxis(ap=idx_row[:, 0:1], axis=0),
                    in_=ysb, in_offset=None, bounds_check=4 * T - 1, oob_is_err=False).then_inc(y_stored, 16)

        @block.tensor
        def _(pe):
            def turn(dst_bank, col0, src, idn, rows, last=None):
                m = pe.transpose(dst_bank[0:rows, col0:col0 + src.shape[0]], src, idn)
                if last is not None:
                    m.then_inc(last, 1)

            pe.wait_ge(ident_in, 16)
            for t in range(TT):
                pe.wait_ge(hn_ready, t + 1)
                for q in range(4):
                    f = t * 4 + q
                    if f >= 8:
                        pe.wait_ge(lo_evac, f - 7)
                    for i in range(4):
                        k = q * 4 + i
                        turn(bank[f % 8], i * P, hn[t % 2][:, k * P:(k + 1) * P], ident, P,
                             turned if i == 3 else None)
            pe.wait_ge(lo_evac, 16)

            def three(bank_, a, b, first, last):
                pe.matmul(bank_, a[0], b[0], start=first, stop=False)
                pe.matmul(bank_, a[1], b[0], start=False, stop=False)
                return pe.matmul(bank_, a[0], b[1], start=False, stop=last)

            def half_split(q, h):
                pe.wait_ge(w_lo_ready, q * 16 + (2 * h + 2))

            def tokens_step(h, j, parts, banks=acc):
                for i in range(2):
                    k = 2 * h + i
                    m = three(banks[j][:, :], [a[:, j * P:(j + 1) * P] for a in parts(k)],
                              [w[h % 2][:, i * W:(i + 1) * W] for w in (w_hi, w_lo)], k == 0, k == KT - 1)
                m.then_inc(proj_steps, 1)

            def half_tokens(h, q, parts, free, banks=acc):
                half_split(q, h)
                for j in range(TT):
                    if h == 0:
                        free(j)
                    tokens_step(h, j, parts, banks)

            def tile_step(c, k, q):
                h = 2 * c + k // 8
                if k % 8 == 0:
                    half_split(q, h)
                m = three(acc[c][:, :], [w[h % 2][:, (k % 8) * P:(k % 8 + 1) * P] for w in (w_hi, w_lo)],
                          hn_parts(k), k == 0, k == KT - 1)
                if k % 2 == 1:
                    m.then_inc(proj_steps, 1)

            with pe.Fori(0, 2) as g:
                for h in range(8):
                    half_tokens(h, g, hn_parts, lambda j: pe.wait_ge(act_evac, g * 4 + (EV_V - 3 + j)))
            pe.wait_ge(act_evac, EV_U)
            with pe.Fori(0, 2) as i:
                for u in range(2):
                    for w in range(2):
                        c = 2 * u + w
                        pe.wait_ge(z_ready if w == 0 else sig_ready, i * 2 + (u + CR_Z - 1))
                        for k in range(KT):
                            tile_step(c, k, i + Q_B)
            pe.wait_ge(z_ready, CR_Z + 3)
            for h in range(8):
                half_tokens(h, Q_A, hn_parts, lambda j: None, u_bank)

            def free_va(j):
                if j < 2:
                    pe.wait_ge(act_evac, EV_U + 1 + j)
                else:
                    pe.wait_ge(z_ready, CR_Z + 4)

            for h in range(8):
                half_tokens(h, Q_A + 1, hn_parts, free_va)
                if h == 3:
                    pe.wait_ge(conv_done, 4)
                    for j in range(4):
                        m = pe.matmul(pat[3][:, :], ones, cbuf[:, j, :], start=(j == 0), stop=(j == 3))
                    m.then_inc(b_sum, 1)
            for j in range(4):
                pe.wait_ge(b_sq, j + 1)
                m = pe.matmul(pat[3][:, :], ones, sqb[:, j, :], start=(j == 0), stop=(j == 3))
            m.then_inc(b_sum, 1)

            def proj_head(h, q, c0, lo, hi):
                for s in range(lo, hi):
                    w, k = divmod(s, KT)
                    if k == 0:
                        if w == 0:
                            pe.wait_ge(qkT_ready, h * 2 + (CR_QK - 2))
                    tile_step(c0 + w, k, q)

            pe.wait_ge(act_evac, EV_A)
            for k in range(KT):
                tile_step(0, k, Q_QK)
            for j in range(4):
                pe.wait_ge(b_sq, 4 + j + 1)
                m = pe.matmul(pat[3][:, :], ones, sqb[:, j, :], start=(j == 0), stop=(j == 3))
            m.then_inc(b_sum, 1)
            pe.wait_ge(sguw_ready, 1)
            for n in range(TT):
                pe.wait_ge(va_normed, n + 1)
                if n == 3:
                    pe.wait_ge(b_mixed, 4)
                for hh in range(4):
                    m = pe.matmul(pat[n][:, hh * P:(hh + 1) * P], sguw[:, hh, :], va[:, n, hh * P:(hh + 1) * P],
                                  start=True, stop=True)
                m.then_inc(spatial, 1)
            for k in range(KT):
                tile_step(1, k, Q_QK)
            for n in range(TT):
                pe.wait_ge(ya_ready, n + 1)
                for i in range(4):
                    turn(pat[n], i * P, u_sb[:, n, i * P:(i + 1) * P], ident, P, turned if i == 3 else None)
            pe.wait_ge(lo_evac, 20)

            def norm_sums(g):
                pe.wait_ge(s_masked, g * 4 + CR_S)
                for w, sq in enumerate((sqq, sqk)):
                    pe.wait_ge(qk_sq, g * 2 + (w + 1))
                    pe.matmul(pat[w][:, :], ones, sq, start=True, stop=True).then_inc(qk_sum, 1)

            def scores(g, par, qi):
                if qi == 0:
                    pe.wait_ge(qkT_ready, g * 2 + (CR_QK + 2))
                if qi >= 2:
                    pe.wait_ge(s_masked, g * 4 + (CR_S + qi - 1))
                n = (qi + 1) * P
                pe.matmul(pat[qi % 2][:, 0:n], qT[par][:, qi * P:n], kT[par][:, 0:n],
                          start=True, stop=True).then_inc(s_ready, 1)

            def turn_p(g, qi):
                pe.wait_ge(p_ready, g * 4 + (qi + 1))
                pe.wait_ge(pT_ready, g * 4 + (CR_PT + qi))
                for j in range(qi + 1):
                    turn(pat[2], j * P, sp_[qi % 2][:, j * P:(j + 1) * P], ident, P,
                         p_turned if j == qi else None)

            def pv(g, qi):
                pe.wait_ge(pT_ready, g * 4 + (CR_PT + qi + 1))
                if qi == 0:
                    pe.wait_ge(o_done, g + CR_O)
                for j in range(qi + 1):
                    v_head = vt[:, j, bass.ds(g * P, P)] if not isinstance(g, int) else vt[:, j, g * P:(g + 1) * P]
                    m = pe.matmul(pat[3][:, qi * P:(qi + 1) * P], pT[qi % 2][:, j * P:(j + 1) * P], v_head,
                                  start=(j == 0), stop=(j == qi))
                m.then_inc(pv_done, 1)

            def attention_part(g, par, s):
                if s == 0:
                    norm_sums(g)
                if 1 <= s <= 4:
                    scores(g, par, s - 1)
                if 2 <= s <= 5:
                    turn_p(g, s - 2)
                if 3 <= s <= 6:
                    pv(g, s - 3)

            CUTS = [0, 2, 14, 18, 22, 25, 28, 32]
            with pe.Fori(0, 3) as i:
                for s in range(7):
                    proj_head(i * 2 + 1, i + Q_QK, 2, CUTS[s], CUTS[s + 1])
                    attention_part(i * 2, 0, s)
                for s in range(7):
                    proj_head(i * 2 + 2, i + (Q_QK + 1), 0, CUTS[s], CUTS[s + 1])
                    attention_part(i * 2 + 1, 1, s)
            for s in range(7):
                proj_head(H - 1, Q_QK + 3, 2, CUTS[s], CUTS[s + 1])
                attention_part(H - 2, 0, s)

            for h in range(4):
                half_split(Q_O, h)
                for j in range(TT):
                    if h == 0 and j == 0:
                        pe.wait_ge(qkT_ready, CR_QK + 2 * (H - 1))
                        pe.wait_ge(qk_sq, 2 * (H - 1))
                    if h == 0 and j == 2:
                        pe.wait_ge(qkT_ready, CR_QK + 2 * H)
                    tokens_step(h, j, mix_parts)
                    if j % 2 == 1 and 2 * h + j // 2 < 7:
                        attention_part(H - 1, 1, 2 * h + j // 2)
            for n in range(TT):
                pe.wait_ge(yc_ready, n + 1)
                for w in range(2):
                    f = 2 * n + w
                    if f >= 4:
                        pe.wait_ge(lo_evac, 20 + f - 3)
                    if f < 4:
                        pe.wait_ge(o_done, CR_O + H)
                    for i in range(4):
                        turn(pat[f % 4], i * P, yc[:, n, (4 * w + i) * P:(4 * w + i + 1) * P], ident, P,
                             turned if i == 3 else None)
            pe.wait_ge(lo_evac, 28)
            for h in range(4, 8):
                half_tokens(h, Q_O, mix_parts, None)
            def group_added(g):
                return lambda j: pe.wait_ge(h_added, g * 4 + (j - 3))

            with pe.Fori(1, 3) as g:
                for h in range(8):
                    half_tokens(h, g + Q_O, mix_parts, group_added(g))

            def turn_h(g, banks):
                for t in range(TT):
                    pe.wait_ge(h_added, 4 * g + t + 1)
                    pe.wait_ge(act_evac, EV_R + (4 * (g - 1) + t + 1 if g else 0))
                    for i in range(4):
                        k = 4 * g + i
                        turn(banks[t], i * P, xh[:, t, k * P:(k + 1) * P], ident, P, turned if i == 3 else None)

            for h in range(8):
                half_tokens(h, QUADS - 1, mix_parts, group_added(3))
                if h in (1, 3, 5):
                    turn_h(h // 2, pat)

            def router(k_lo, k_hi):
                for k in range(k_lo, k_hi):
                    m = pe.matmul(pat[3][(k % 2) * RC:(k % 2 + 1) * RC, :], wrt[:, k, :], hT_all[:, k, :],
                                  start=(k < 2), stop=(k >= KT - 2))
                return m

            pe.wait_ge(act_evac, EV_R + 12)
            pe.wait_ge(wrt_scaled, 1)
            router(0, 12)
            turn_h(3, pat[0:3] + acc[0:1])
            pe.wait_ge(act_evac, EV_R + 16)
            router(12, KT).then_inc(logits, 1)
            pe.wait_ge(logitT_ready, 1)
            for t in range(TT):
                m = pe.matmul(bank[1][:, t * 36:(t + 1) * 36], logitT[:, t * P:(t + 1) * P],
                              cst[:, C_FOLD:C_FOLD + 36], start=True, stop=True)
            m.then_inc(folded, 1)
            pe.wait_ge(picked, 1)
            taken = rt[:, 0:TT * E]
            pe.matmul(bank[2][:, 0:TT * E], low, taken, start=True, stop=True)
            pe.matmul(bank[2][:, TT * E:2 * TT * E], ones, taken, start=True, stop=True).then_inc(ranked, 1)
            pe.wait_ge(sched_col, 1)
            pe.transpose(bank[3][0:1, 0:P], ss[:, 15:16], ident).then_inc(sched_row, 1)
            for n, vals in enumerate((oh_pair, oh_rs)):
                pe.wait_ge(onehots, n + 1)
                for i in range(2 * TT):
                    m = pe.matmul(bank[4 + n][:, 0:NT], oh_slot[:, i, :], vals[:, i, :],
                                  start=(i == 0), stop=(i == 2 * TT - 1))
                m.then_inc(tabs_made, 1)

            pgu, pguT, px, py = bank[0], bank[1], bank[2:4], bank[4:6]

            def turn_rows():
                for k in range(KT):
                    turn(px[k // 8], (k % 8) * TB, xg[:, k:D:KT], cst[0:TB, C_ID:C_ID + TB], P,
                         xg_turned if k % 8 == 7 else None)

            pe.sem_inc(e_used, CR_E)
            pe.wait_ge(sched_ready, 1)
            nb = pe.value_load(sched[0:1, P:P + 1], min_val=E, max_val=NBLK)
            pe.wait_ge(xg_in, 16)
            turn_rows()
            with pe.Fori(0, nb) as b:
                pe.wait_ge(xgT_ready, b * 2 + 2)
                for c in range(4):
                    pe.wait_ge(e_in_slot[2 * c], b * 16 + 16)
                    pe.wait_ge(e_in_slot[2 * c + 1], b * 16 + 16)
                    if c == 0:
                        pe.wait_ge(gu_ready, b + CR_GU)
                    for i in range(4):
                        k = 4 * c + i
                        for w in range(2):
                            m = pe.matmul(pgu[w * TB:(w + 1) * TB, :], xgT[:, k * TB:(k + 1) * TB],
                                          slot(2 * c + w)[:, i * FE:(i + 1) * FE], start=(k == 0), stop=(k == KT - 1))
                            if i == 3:
                                m.then_inc(e_used, 1)
                pe.wait_ge(gu_ready, b + (CR_GU + 1))
                for f in range(FT):
                    turn(pguT, f * P, gu[:, f * P:(f + 1) * P], ident, P, gu_turned if f == FT - 1 else None)
                pe.wait_ge(hT_ready, b + (CR_H + 1))
                pe.wait_ge(y_evac_a, b + CR_Y)
                pe.wait_ge(y_evac_v, b + CR_Y)
                for f in range(FT):
                    pe.wait_ge(e_in_slot[8 + f], b * 16 + 16)
                    for n, w in ((0, 0), (0, 1), (1, 0), (1, 1)):
                        m = pe.matmul(py[n][w * TB:(w + 1) * TB, :], hT[:, f * TB:(f + 1) * TB],
                                      slot(8 + f)[:, (2 * w + n) * W:(2 * w + n + 1) * W], start=(f == 0), stop=(f == FT - 1))
                    m.then_inc(e_used, 1)
                wait_alone(pe, (xg_in, b * 16 + 32))
                turn_rows()

        @block.scalar
        def _(act):
            def evac(dst, src):
                nc.scalar.activation(dst, src, ACT.Copy).then_inc(act_evac, 1)

            def root(dst, src, width):
                nc.scalar.activation(dst, src, ACT.Sqrt, bias=eps[:, 0:1], scale=1.0 / width).then_inc(root_done, 1)

            act.wait_ge(eps_set, 1)

            def high(dst, src):
                nc.scalar.activation(dst, src, ACT.Copy).then_inc(act_evac, 1)

            def split(q, h):
                q, h = q + h // 8, h % 8
                c = h // 2
                act.wait_ge(w_in_slot[c % 2], q * 32 + (16 * (c // 2) + 16))
                if not (isinstance(q, int) and 8 * q + h < 2):
                    act.wait_ge(proj_steps, q * QS + (4 * h - 4))
                nc.scalar.activation(w_hi[h % 2], slot(c % 2)[:, (h % 2) * HC:(h % 2 + 1) * HC],
                                     ACT.Copy).then_inc(w_hi_ready, 1)

            def x_stats(t):
                act.wait_ge(x_in[t], 16)
                nc.scalar.activation(x_sq, x_rows[:, t, :], ACT.Square, accum_out=ss[:, t:t + 1]).then_inc(stat_ready, 1)
                act.wait_ge(stat_ready, t + 1)
                root(rs[:, t:t + 1], ss[:, t:t + 1], D)

            x_stats(0)
            x_stats(1)
            for f in range(16):
                t, q = divmod(f, 4)
                act.wait_ge(turned, f + 1)
                high(hn_high[:, 4 * q:4 * q + 4, t * P:(t + 1) * P],
                     bank[f % 8][:, :].rearrange("p (k n) -> p k n", k=4))
                if q == 3 and t + 2 < TT:
                    x_stats(t + 2)
                if f in (9, 13):
                    split(0, f // 12)
            with act.Fori(0, 2) as g:
                for h in range(2, 9):
                    split(g, h)
                for j in range(TT):
                    act.wait_ge(proj_steps, g * QS + (28 + j + 1))
                    nc.scalar.activation(vt[:, j, bass.ds(g * W, W)], acc[j][:, :], ACT.Copy).then_inc(act_evac, 1)
                split(g, 9)
            act.sem_inc(sig_ready, CR_Z)
            with act.Fori(0, 2) as i:
                for u in range(2):
                    for h in range(4 * u + 2, 4 * u + 6):
                        split(i + Q_B, h)
                    act.wait_ge(proj_steps, i * QS + (QS * Q_B + 16 * u + 16))
                    act.wait_ge(z_ready, i * 2 + (u + CR_Z))
                    nc.scalar.activation(sig, acc[2 * u + 1][:, :], ACT.Sigmoid).then_inc(sig_ready, 1)
            for g in range(2):
                dst = u_sb if g == 0 else va
                for h in range(2, 9):
                    split(Q_A + g, h)
                    if g == 1 and h == 5:
                        for j in range(4):
                            act.wait_ge(b_cent, j + 1)
                            nc.scalar.activation(sqb[:, j, :], cbuf[:, j, :], ACT.Square).then_inc(b_sq, 1)
                for j in range(TT):
                    act.wait_ge(proj_steps, QS * (Q_A + g) + 28 + j + 1)
                    nc.scalar.activation(dst[:, j, :], (acc if g else u_bank)[j][:, :], ACT.Gelu_apprx_tanh).then_inc(act_evac, 1)
                split(Q_A + g, 9)
            act.wait_ge(b_sum, 2)
            root(rb, pat[3][:, :], W)
            act.wait_ge(stat_ready, 8)
            root(rs[:, 4:8], ss[:, 4:8], W)
            split(Q_QK, 2)
            for j in range(4):
                act.wait_ge(b_norm, j + 1)
                nc.scalar.activation(cbuf[:, j, :], cbuf[:, j, :], ACT.Silu, bias=col[:, K_LB + j:K_LB + j + 1],
                                     scale=col[:, K_LG + j:K_LG + j + 1]).then_inc(b_silu, 1)
            for j in range(4):
                act.wait_ge(b_silu, j + 1)
                nc.scalar.activation(sqb[:, j, :], cbuf[:, j, :], ACT.Square).then_inc(b_sq, 1)
            split(Q_QK, 3)
            act.wait_ge(b_sum, 3)
            root(rb, pat[3][:, :], W)
            act.wait_ge(stat_ready, 12)
            root(rs[:, 8:12], ss[:, 8:12], W)
            split(Q_QK, 4)
            for n in range(TT):
                act.wait_ge(turned, 16 + n + 1)
                high(mix_ab[:, 0:4, n * P:(n + 1) * P], pat[n][:, :].rearrange("p (k n) -> p k n", k=4))

            def squares(h, q, c0):
                for w, sq in enumerate((sqq, sqk)):
                    act.wait_ge(proj_steps, q * QS + (8 * (c0 + w) + 8))
                    if not isinstance(h, int) or h > 0:
                        act.wait_ge(qk_sum, h * 2 + (w - 1))
                    nc.scalar.activation(sq, acc[c0 + w][:, :], ACT.Square).then_inc(qk_sq, 1)

            def qk_roots(g):
                for w in range(2):
                    act.wait_ge(qk_sum, g * 2 + (w + 1))
                    nc.scalar.activation(rqk[w], pat[w][:, :], ACT.Sqrt, bias=eps[:, 0:1], scale=1.0 / P)\
                        .then_inc(qk_root, 1)

            def probs(g, q, h):
                qk_roots(g)
                split(q, h + 2)
                for qi in range(TT):
                    n = (qi + 1) * P
                    act.wait_ge(s_masked, g * 4 + (CR_S + qi + 1))
                    nc.scalar.activation(sp_[qi % 2][:, 0:n], sp_[qi % 2][:, 0:n], ACT.Exp,
                                         bias=nmax[:, qi:qi + 1], scale=SCALE,
                                         accum_out=den[:, qi:qi + 1]).then_inc(p_ready, 1)
                    if qi in (1, 2):
                        split(q, h + 2 + qi)
                    act.wait_ge(p_turned, g * 4 + (qi + 1))
                    if qi >= 2:
                        act.wait_ge(pv_done, g * 4 + (qi - 1))
                    nc.scalar.activation(pT[qi % 2][:, 0:n], pat[2][:, 0:n], ACT.Copy).then_inc(pT_ready, 1)

            act.wait_ge(b_mixed, 4)
            act.dma_start(rowc, row_c).then_inc(rowc_in, 16)
            act.sem_inc(pT_ready, CR_PT)
            split(Q_QK, 5)
            squares(0, Q_QK, 0)
            with act.Fori(0, 3) as i:
                probs(i * 2, i + Q_QK, 4)
                split(i + Q_QK, 9)
                squares(i * 2 + 1, i + Q_QK, 2)
                probs(i * 2 + 1, i + (Q_QK + 1), 0)
                split(i + (Q_QK + 1), 5)
                squares(i * 2 + 2, i + (Q_QK + 1), 0)
            probs(H - 2, Q_QK + 3, 4)
            split(Q_O, 1)
            squares(H - 1, Q_QK + 3, 2)
            probs(H - 1, Q_O, 0)
            split(Q_O, 5)
            act.wait_ge(stat_ready, 16)
            root(rs[:, 12:16], ss[:, 12:16], 2 * W)
            for n in range(TT):
                for w in range(2):
                    f = 2 * n + w
                    act.wait_ge(turned, 20 + f + 1)
                    high(mix_c[:, 4 * w:4 * w + 4, n * P:(n + 1) * P],
                         pat[f % 4][:, :].rearrange("p (k n) -> p k n", k=4))
            act.dma_start(wrt, w_rt).then_inc(n2_in, 16)
            act.dma_start(rbr, rbias).then_inc(n2_in, 16)
            for h in range(6, 10):
                split(Q_O, h)
            with act.Fori(Q_O + 1, QUADS - 1) as q:
                for h in range(2, 10):
                    split(q, h)

            def h_turned(g, banks):
                for t in range(TT):
                    act.wait_ge(turned, 28 + 4 * g + t + 1)
                    evac(hT_all[:, 4 * g:4 * g + 4, t * P:(t + 1) * P],
                         banks[t][:, :].rearrange("p (k n) -> p k n", k=4))

            for h in range(2, 8):
                split(QUADS - 1, h)
                if h % 2 == 1:
                    h_turned(h // 2 - 1, pat)
                    g = h // 2 - 1
                    act.wait_ge(h_added, 4 * g + 4)
                    act.dma_start(rows_by_tile(h_dram)[:, :, g * W:(g + 1) * W], xh[:, :, g * W:(g + 1) * W])\
                        .then_inc(h_stored, 16)
            h_turned(3, pat[0:3] + acc[0:1])
            act.wait_ge(stat_ready, 17)
            root(rs[:, 0:TT], ss[:, 0:TT], D)
            for n, (lo, hi) in enumerate(((R_EXG, R_EXG + TT * NG), (R_EX2, R_EX2 + TT))):
                act.wait_ge(exp_in, n + 1)
                nc.scalar.activation(rt[:, lo:hi], rt[:, lo:hi], ACT.Exp).then_inc(gate_exp, 1)

            px, py = bank[2:4], bank[4:6]
            act.sem_inc(sg_ready, CR_SG)
            act.sem_inc(y_evac_a, CR_Y)
            act.wait_ge(sched_ready, 1)
            nb = act.value_load(sched[0:1, P:P + 1], min_val=E, max_val=NBLK)

            with act.Fori(0, nb) as b:
                act.wait_ge(gu_turned, b + (CR_GT + 1))
                act.wait_ge(hT_ready, b + CR_H)
                nc.scalar.activation(sg.rearrange("p (f n) -> p f n", f=FT), guT[:, :, 0:TB], ACT.Silu)\
                    .then_inc(sg_ready, 1)
                act.wait_ge(y_stored, b * 16 + CR_YS)
                act.wait_ge(e_used, b * EC + (CR_E + EC))
                nc.scalar.activation(ysb[:, 0:W], py[0][:, :], ACT.Copy).then_inc(y_evac_a, 1)

        @block.vector
        def _(dve):
            own = Chain(dve, dve_own)

            roots = [0]

            def inverse(ap):
                roots[0] += 1
                dve.wait_ge(root_done, roots[0])
                own.link(nc.vector.reciprocal(ap, ap))

            def sum_sq(scratch, src, c):
                nc.vector.tensor_tensor_reduce(out=scratch, in0=src, in1=src, scale=1.0, scalar=0.0,
                                               op0=ALU.mult, op1=ALU.add, accum_out=ss[:, c:c + 1])\
                    .then_inc(stat_ready, 1)

            def low_turned(f, low, src, high):
                dve.wait_ge(act_evac, f)
                low_part(nc.vector, low, src[:, :].rearrange("p (k n) -> p k n", k=4), high).then_inc(lo_evac, 1)

            def low_x(t):
                for q in range(4):
                    at = (slice(None), slice(4 * q, 4 * q + 4), slice(t * P, (t + 1) * P))
                    low_turned(4 * t + q + 1, hn_low[at], bank[(4 * t + q) % 8], hn_high[at])

            dve.wait_ge(n1_in, 16)
            for t in range(TT):
                if t >= 2:
                    dve.wait_ge(turned, 4 * (t - 1))
                inverse(rs[:, t:t + 1])
                nc.vector.scalar_tensor_tensor(out=hn[t % 2], in0=x_rows[:, t, :], scalar=rs[:, t:t + 1], in1=n1row,
                                               op0=ALU.mult, op1=ALU.mult).then_inc(hn_ready, 1)
                if t >= 1:
                    low_x(t - 1)
            low_x(TT - 1)
            dve.wait_ge(const_in, 16 * 3)
            for hh in range(4):
                m = nc.vector.tensor_tensor(sguw[:, hh, :], sguw[:, hh, :], cst[:, C_TRI:C_TRI + P], ALU.mult)
                if hh < 3:
                    own.add(m)
            m.then_inc(sguw_ready, 1)
            for i in range(2):
                own.add(nc.vector.memset(z[i][:, 0:TAPS - 1], 0.0))
            own.wait()

            dve.sem_inc(z_ready, CR_Z)
            STEPS = TAPS
            with dve.Fori(0, 2) as i:
                for u in range(2):
                    conv = Chain(dve, conv_own, i * (2 * STEPS) + u * STEPS)
                    conv.add(nc.vector.tensor_copy(cwj[:, :], col[:, bass.ds(i * 64 + u * 32, TAPS + 1)]))
                    dve.wait_ge(proj_steps, i * QS + (QS * Q_B + 16 * u + 8))
                    dve.wait_ge(sig_ready, i * 2 + (u + CR_Z + 1))
                    nc.vector.tensor_tensor(z[u][:, TAPS - 1:TAPS - 1 + T], acc[2 * u][:, :], sig, ALU.mult)\
                        .then_inc(z_ready, 1)
                    dve.wait_ge(z_ready, i * 2 + (u + CR_Z + 1))
                    conv.wait()
                    conv.link(nc.vector.tensor_scalar(cacc, z[u][:, 0:T], cwj[:, 0:1], cwj[:, TAPS:TAPS + 1],
                                                      ALU.mult, ALU.add))
                    for k in range(1, TAPS - 1):
                        conv.link(nc.vector.scalar_tensor_tensor(
                            out=cacc, in0=z[u][:, k:k + T], scalar=cwj[:, k:k + 1], in1=cacc,
                            op0=ALU.mult, op1=ALU.add))
                    assert conv.n == STEPS
                    nc.vector.scalar_tensor_tensor(
                        out=cbuf[:, bass.ds(i * 2 + u, 1), :].rearrange("p o n -> p (o n)"),
                        in0=z[u][:, TAPS - 1:TAPS - 1 + T], scalar=cwj[:, TAPS - 1:TAPS],
                        in1=cacc, op0=ALU.mult, op1=ALU.add).then_inc(conv_done, 1)
                    dve.wait_ge(conv_done, i * 2 + (u + 1))
            dve.wait_ge(conv_done, 4)
            dve.wait_ge(b_sum, 1)
            own.link(nc.vector.tensor_scalar(mu, pat[3][:, :], 1.0 / W, None, ALU.mult))
            for j in range(4):
                nc.vector.tensor_tensor(cbuf[:, j, :], cbuf[:, j, :], mu, ALU.subtract).then_inc(b_cent, 1)
            for n in range(TT):
                dve.wait_ge(act_evac, EV_U + 4 + n + 1)
                sum_sq(junk_a[:, n, :], va[:, n, :], 4 + n)
            inverse(rb)
            for j in range(4):
                nc.vector.tensor_tensor(cbuf[:, j, :], cbuf[:, j, :], rb, ALU.mult).then_inc(b_norm, 1)
            inverse(rs[:, 4:4 + TT])
            for n in range(TT):
                nc.vector.scalar_tensor_tensor(out=va[:, n, :], in0=va[:, n, :], scalar=rs[:, 4 + n:5 + n],
                                               in1=rowa[:, R_SGU:R_SGU + W], op0=ALU.mult, op1=ALU.mult)\
                    .then_inc(va_normed, 1)
            inverse(rb)
            for j in range(4):
                own.add(nc.vector.scalar_tensor_tensor(out=cbuf[:, j, :], in0=cbuf[:, j, :],
                                                       scalar=col[:, K_OB + j:K_OB + j + 1], in1=rb,
                                                       op0=ALU.mult, op1=ALU.mult))
            own.wait()
            for j in range(4):
                own.add(nc.vector.tensor_copy(mix_ab[:, 4 + j, :], cbuf[:, j, :]))
            own.wait()
            for j in range(4):
                low_part(nc.vector, mix_ab[:, 12 + j, :], cbuf[:, j, :], mix_ab[:, 4 + j, :]).then_inc(b_mixed, 1)
            for n in range(TT):
                dve.wait_ge(spatial, n + 1)
                for hh in range(4):
                    sl = u_sb[:, n, hh * P:(hh + 1) * P]
                    own.add(nc.vector.scalar_tensor_tensor(out=sl, in0=pat[n][:, hh * P:(hh + 1) * P],
                                                           scalar=col[:, K_SB + hh:K_SB + hh + 1], in1=sl,
                                                           op0=ALU.add, op1=ALU.mult))
                own.wait()
                sum_sq(junk_a[:, n, :], u_sb[:, n, :], 8 + n)
            inverse(rs[:, 8:8 + TT])
            for n in range(TT):
                nc.vector.scalar_tensor_tensor(out=u_sb[:, n, :], in0=u_sb[:, n, :], scalar=rs[:, 8 + n:9 + n],
                                               in1=rowa[:, R_OA:R_OA + W], op0=ALU.mult, op1=ALU.mult)\
                    .then_inc(ya_ready, 1)

            def qk_norm(g, c0):
                for w, dst in enumerate((qT[c0 // 2], kT[c0 // 2])):
                    dve.wait_ge(qk_root, g * 2 + (w + 1))
                    nc.vector.reciprocal(rqk[w], rqk[w]).then_inc(r_own, 1)
                    dve.wait_ge(r_own, g * 2 + (w + 1))
                    nc.vector.scalar_tensor_tensor(out=dst, in0=acc[c0 + w][:, :], scalar=col[:, K_Q + w:K_Q + w + 1],
                                                   in1=rqk[w], op0=ALU.mult, op1=ALU.mult).then_inc(qkT_ready, 1)

            def mask_max(g):
                for qi in range(TT):
                    n = (qi + 1) * P
                    if qi >= 2:
                        dve.wait_ge(p_turned, g * 4 + (qi - 1))
                    wait_alone(dve, (s_ready, g * 4 + (qi + 1)))
                    nc.vector.tensor_tensor_reduce(
                        out=sp_[qi % 2][:, 0:n], in0=pat[qi % 2][:, 0:n], in1=cst[:, C_BAND + T - n:C_BAND + T],
                        scale=1.0, scalar=-3.0e38, op0=ALU.add, op1=ALU.max, accum_out=pmax[:, qi:qi + 1])\
                        .then_inc(s_max, 1)
                    dve.wait_ge(s_max, g * 4 + (qi + 1))
                    nc.vector.tensor_scalar(nmax[:, qi:qi + 1], pmax[:, qi:qi + 1], -SCALE, None, ALU.mult)\
                        .then_inc(s_masked, 1)

            def rows_out(g):
                dve.wait_ge(p_ready, g * 4 + 4)
                nc.vector.reciprocal(rden[:, :], den[:, 0:TT]).then_inc(rden_ready, 1)
                dve.wait_ge(rden_ready, g + 1)
                dve.wait_ge(pv_done, g * 4 + 4)
                for qi in range(TT):
                    dst = yc[:, qi, g * P:(g + 1) * P] if isinstance(g, int) else yc[:, qi, bass.ds(g * P, P)]
                    m = nc.vector.tensor_scalar(dst, pat[3][:, qi * P:(qi + 1) * P], rden[:, qi:qi + 1], None, ALU.mult)
                m.then_inc(o_done, 1)

            for n in range(TT):
                low_turned(EV_A + n + 1, mix_ab[:, 8:12, n * P:(n + 1) * P], pat[n], mix_ab[:, 0:4, n * P:(n + 1) * P])
            dve.sem_inc(qkT_ready, CR_QK)
            dve.sem_inc(s_masked, CR_S)
            dve.sem_inc(o_done, CR_O)
            with dve.Fori(0, 3) as i:
                for u in range(2):
                    qk_norm(i * 2 + u, 2 * u)
                    mask_max(i * 2 + u)
                    rows_out(i * 2 + u)
            for g in range(H - 2, H):
                qk_norm(g, 2 * (g % 2))
                mask_max(g)
                rows_out(g)
            dve.wait_ge(o_done, CR_O + H)
            for n in range(TT):
                sum_sq(junk_c[:, n, :], yc[:, n, :], 12 + n)
            inverse(rs[:, 12:12 + TT])
            dve.wait_ge(rowc_in, 16)
            for n in range(TT):
                nc.vector.scalar_tensor_tensor(out=yc[:, n, :], in0=yc[:, n, :], scalar=rs[:, 12 + n:13 + n],
                                               in1=rowc, op0=ALU.mult, op1=ALU.mult).then_inc(yc_ready, 1)
            for f in range(2 * TT):
                n, w = divmod(f, 2)
                low_turned(EV_C + f + 1, mix_c[:, 8 + 4 * w:12 + 4 * w, n * P:(n + 1) * P], pat[f % 4],
                           mix_c[:, 4 * w:4 * w + 4, n * P:(n + 1) * P])
            dve.wait_ge(n2_in, 32)
            nc.vector.tensor_tensor(wrt, wrt, col[:, K_N2:K_N2 + KT].unsqueeze(2).to_broadcast([P, KT, RC]), ALU.mult)\
                .then_inc(wrt_scaled, 1)
            for t in range(TT):
                dve.wait_ge(x_in[t], 32)
            dve.sem_inc(h_sq_done, 1)
            for g in range(4):
                for j in range(TT):
                    part = xh[:, j, g * W:(g + 1) * W]
                    dve.wait_ge(proj_steps, QS * (Q_O + g) + 28 + j + 1)
                    nc.vector.tensor_tensor(part, acc[j][:, :], part, ALU.add).then_inc(h_added, 1)
                for j in range(TT):
                    part = xh[:, j, g * W:(g + 1) * W]
                    dve.wait_ge(h_added, 4 * g + j + 1)
                    dve.wait_ge(h_sq_done, 4 * g + j + 1)
                    nc.vector.tensor_tensor_reduce(out=h_sq, in0=part, in1=part, scale=1.0, scalar=0.0, op0=ALU.mult,
                                                   op1=ALU.add, accum_out=ss_h[:, j, g:g + 1]).then_inc(h_sq_done, 1)
            dve.wait_ge(h_sq_done, 4 * TT + 1)
            nc.vector.tensor_reduce(ss[:, 0:TT], ss_h[:, :, :], AX, ALU.add).then_inc(stat_ready, 1)

            def r3(o, n):
                return rt[:, o:o + TT * n].rearrange("p (t n) -> p t n", t=TT)

            def per_tile(ap, n):
                return ap.unsqueeze(2).to_broadcast([P, TT, n])

            taken, oh1, oh2 = r3(R_TAKEN, E), r3(R_OH1, E), r3(R_OH2, E)
            lg, le, eq, pos = r3(R_LG, 36), r3(R_LE, E), r3(R_EQ, E), r3(R_POS, E)
            exg, eqg = r3(R_EXG, NG), r3(R_EQG, NG)
            one = lambda i: rt[:, R_ONE + TT * i:R_ONE + TT * (i + 1)]
            gmax, gsum, gi, m1, i1, m2, i2, gg, g2r, den2, d1 = (one(i) for i in range(11))
            ex2 = rt[:, R_EX2:R_EX2 + TT]
            c3 = lambda o, n: cst[:, o:o + TT * n].rearrange("p (t n) -> p t n", t=TT)
            v = nc.vector
            dve.wait_ge(logits, 1)
            v.tensor_copy(logitT, pat[3][:, :]).then_inc(logitT_ready, 1)
            inverse(rs[:, 0:TT])
            dve.wait_ge(folded, 1)
            for t in range(TT):
                own.add(v.scalar_tensor_tensor(out=lg[:, t, :], in0=bank[1][:, t * 36:(t + 1) * 36],
                                               scalar=rs[:, t:t + 1], in1=rbr[:, t, :], op0=ALU.mult, op1=ALU.add))
            own.wait()
            own.link(v.tensor_reduce(gmax, lg[:, :, 0:NG], AX, ALU.max))
            v.tensor_tensor(exg, lg[:, :, 0:NG], per_tile(gmax, NG), ALU.subtract).then_inc(exp_in, 1)
            own.link(v.tensor_tensor(eqg, lg[:, :, 0:NG], per_tile(gmax, NG), ALU.is_equal))
            own.link(v.scalar_tensor_tensor(out=eqg, in0=eqg, scalar=-BIG, in1=c3(C_GI, NG), op0=ALU.mult, op1=ALU.add))
            own.link(v.tensor_reduce(gi, eqg, AX, ALU.min))
            own.link(v.tensor_tensor(eq, c3(C_EG, E), per_tile(gi, E), ALU.not_equal))
            own.link(v.scalar_tensor_tensor(out=le, in0=eq, scalar=OFF, in1=lg[:, :, NG:36], op0=ALU.mult, op1=ALU.add))

            def largest(mx, ix, oh):
                own.link(v.tensor_reduce(mx, le, AX, ALU.max))
                own.link(v.tensor_tensor(eq, le, per_tile(mx, E), ALU.not_equal))
                own.link(v.scalar_tensor_tensor(out=pos, in0=eq, scalar=BIG, in1=c3(C_EI, E), op0=ALU.mult, op1=ALU.add))
                own.link(v.tensor_reduce(ix, pos, AX, ALU.min))
                own.link(v.tensor_tensor(oh, c3(C_EI, E), per_tile(ix, E), ALU.is_equal))

            largest(m1, i1, oh1)
            own.link(v.scalar_tensor_tensor(out=le, in0=oh1, scalar=GONE, in1=le, op0=ALU.mult, op1=ALU.add))
            largest(m2, i2, oh2)
            v.tensor_tensor(taken, oh1, oh2, ALU.add).then_inc(picked, 1)
            v.tensor_tensor(ex2, m2, m1, ALU.subtract).then_inc(exp_in, 1)
            dve.wait_ge(gate_exp, 2)
            own.link(v.tensor_reduce(gsum, exg, AX, ALU.add))
            own.link(v.tensor_scalar(den2, ex2, 1.0, None, ALU.add))
            own.link(v.tensor_tensor(den2, den2, gsum, ALU.mult))
            own.link(v.reciprocal(gates[:, 0, :], den2))
            own.link(v.tensor_tensor(gates[:, 1, :], gates[:, 0, :], ex2, ALU.mult))
            dve.wait_ge(ranked, 1)
            cnt, nblk, over = rt[:, R_CNT:R_CNT + E], rt[:, R_NB:R_NB + E], rt[:, R_OVER:R_OVER + E * (T // TB - 1)]
            sums = r3(R_SUMS, E)
            own.link(v.tensor_copy(sums, bank[2][:, TT * E:2 * TT * E].rearrange("p (t e) -> p t e", t=TT)))
            for t in range(1, TT):
                own.link(v.tensor_tensor(sums[:, t, :], sums[:, t, :], sums[:, t - 1, :], ALU.add))
            over = over.rearrange("p (e m) -> p e m", e=E)
            M = T // TB - 1
            own.link(v.tensor_tensor(over, sums[:, TT - 1, :].unsqueeze(2).to_broadcast([P, E, M]),
                                     cst[:, C_TH:C_TH + M].unsqueeze(1).to_broadcast([P, E, M]), ALU.is_gt))
            own.link(v.tensor_reduce(nblk, over, AX, ALU.add))
            own.link(v.tensor_scalar(nblk, nblk, 1.0, None, ALU.add))
            a, bb = rt[:, R_SA:R_SA + E], rt[:, R_SB:R_SB + E]
            own.link(v.tensor_copy(a, nblk))
            s = 1
            while s < E:
                own.add(v.tensor_copy(bb[:, 0:s], a[:, 0:s]))
                own.link(v.tensor_tensor(bb[:, s:E], a[:, s:E], a[:, 0:E - s], ALU.add))
                a, bb = bb, a
                s *= 2
            own.link(v.tensor_copy(sched[0:1, P:P + 1], a[0:1, E - 1:E]))
            own.link(v.tensor_tensor(bb, a, nblk, ALU.subtract))
            own.link(v.tensor_scalar(cnt, bb, cst[:, C_P:C_P + 1], None, ALU.is_le))
            own.link(v.tensor_reduce(ss[:, 14:15], cnt, AX, ALU.add))
            v.tensor_scalar(ss[:, 15:16], ss[:, 14:15], -1.0, None, ALU.add).then_inc(sched_col, 1)
            own.link(v.tensor_scalar(bb, bb, float(TB), None, ALU.mult))
            own.link(v.tensor_tensor(pos, bank[2][:, 0:TT * E].rearrange("p (t e) -> p t e", t=TT),
                                     bb.unsqueeze(1).to_broadcast([P, TT, E]), ALU.add))
            own.link(v.tensor_tensor(pos[:, 1:TT, :], pos[:, 1:TT, :], sums[:, 0:TT - 1, :], ALU.add))
            dest = rt[:, R_DEST:R_DEST + 2 * TT].rearrange("p (k t) -> p k t", k=2)
            for k, (oh, at) in enumerate(((oh1, eq), (oh2, le))):
                own.add(v.tensor_tensor(at, pos, oh, ALU.mult))
            own.wait()
            for k, at in enumerate((eq, le)):
                own.add(v.tensor_reduce(dest[:, k, :], at, AX, ALU.add))
            own.wait()
            own.link(v.tensor_copy(dest_i[:, :, :], dest))
            own.add(v.tensor_scalar(slot_i[:, :, :], dest_i[:, :, :], TB - 1, None, ALU.bitwise_and))
            own.link(v.tensor_scalar(blk_i[:, :, :], dest_i[:, :, :], TB.bit_length() - 1, None,
                                     ALU.logical_shift_right))

            def pairs_by(ap, n):
                return ap.rearrange("p k t -> p (k t)").unsqueeze(2).to_broadcast([P, 2 * TT, n])

            own.add(v.tensor_tensor(oh_blk, cst[:, C_BLK:C_BLK + NT].unsqueeze(1).to_broadcast([P, 2 * TT, NT]),
                                    pairs_by(blk_i[:, :, :], NT), ALU.is_equal))
            own.link(v.tensor_tensor(oh_slot, cst[:, C_SLOT:C_SLOT + P].unsqueeze(1).to_broadcast([P, 2 * TT, P]),
                                     pairs_by(slot_i[:, :, :], P), ALU.is_equal))
            v.tensor_tensor(oh_pair, oh_blk, cst[:, C_PAIR:C_PAIR + 2 * TT].unsqueeze(2)
                            .to_broadcast([P, 2 * TT, NT]), ALU.mult).then_inc(onehots, 1)
            for k in range(2):
                m = v.tensor_tensor(oh_rs[:, k * TT:(k + 1) * TT, :], oh_blk[:, k * TT:(k + 1) * TT, :],
                                    rs[:, 0:TT].unsqueeze(2).to_broadcast([P, TT, NT]), ALU.mult)
                if k == 0:
                    own.add(m)
            m.then_inc(onehots, 1)
            dve.wait_ge(sched_row, 1)
            v.tensor_copy(sched[0:1, 0:P], bank[3][0:1, 0:P]).then_inc(sched_ready, 1)
            dve.wait_ge(tabs_made, 1)
            own.link(v.tensor_scalar(rt[0:TB, R_CNT:R_CNT + NT], bank[4][0:TB, 0:NT], float(T - NOWHERE), float(-T),
                                     ALU.is_ge, ALU.mult))
            v.scalar_tensor_tensor(out=tab_tok[:, :], in0=bank[4][0:TB, 0:NT], scalar=float(NOWHERE),
                                   in1=rt[0:TB, R_CNT:R_CNT + NT], op0=ALU.add, op1=ALU.add).then_inc(tabs_ready, 1)
            v.tensor_scalar(tab_row[:, :], bank[4][:, 0:NT], 2.0, cst[:, C_HALF:C_HALF + 1],
                            ALU.mult, ALU.add).then_inc(tabs_ready, 1)
            dve.wait_ge(tabs_made, 2)
            v.tensor_copy(tab_rs[:, :], bank[5][:, 0:NT]).then_inc(tabs_ready, 1)

            dve.sem_inc(gu_ready, CR_GU)
            dve.sem_inc(gu_turned, CR_GT)
            dve.sem_inc(hT_ready, CR_H)
            dve.sem_inc(y_evac_v, CR_Y)
            dve.wait_ge(sched_ready, 1)
            nb = dve.value_load(sched[0:1, P:P + 1], min_val=E, max_val=NBLK)

            def rows_turned(base):
                for w in range(2):
                    dve.wait_ge(xg_turned, base + (w + 1))
                    v.tensor_tensor(xgT[:, w * W:(w + 1) * W].rearrange("p (k n) -> p k n", n=TB),
                                    bank[2 + w][:, :].rearrange("p (k n) -> p k n", n=TB),
                                    col[:, K_N2R + 8 * w:K_N2R + 8 * w + 8].unsqueeze(2).to_broadcast([P, 8, TB]),
                                    ALU.mult).then_inc(xgT_ready, 1)

            rows_turned(0)
            dve.wait_ge(tabs_ready, 3)
            with dve.Fori(0, nb) as b:
                dve.wait_ge(e_used, b * EC + (CR_E + 8))
                dve.wait_ge(gu_turned, b + CR_GT)
                v.tensor_scalar(gu, bank[0][:, :], tab_rs[:, bass.ds(b, 1)], None, ALU.mult)\
                    .then_inc(gu_ready, 1)
                dve.wait_ge(sg_ready, b + (CR_SG + 1))
                dve.wait_ge(e_used, b * EC + CR_E)
                v.tensor_tensor(hT.rearrange("p (f n) -> p f n", f=FT), guT[:, :, TB:P],
                                sg.rearrange("p (f n) -> p f n", f=FT), ALU.mult).then_inc(hT_ready, 1)
                dve.wait_ge(y_stored, b * 16 + CR_YS)
                v.tensor_copy(idx_row[:, :], tab_row[:, bass.ds(b, 1)]).then_inc(idx_r_ready, 1)
                dve.wait_ge(e_used, b * EC + (CR_E + EC))
                v.tensor_copy(ysb[:, W:2 * W], bank[5][:, :]).then_inc(y_evac_v, 1)
                rows_turned(b * 2 + 2)
            for t in range(TT):
                h = xh[:, t, :]
                dve.wait_ge(yrow_in[t], 32)
                v.scalar_tensor_tensor(out=h, in0=yrow[t][0], scalar=gates[:, 0, t:t + 1], in1=h,
                                       op0=ALU.mult, op1=ALU.add).then_inc(part_sum, 1)
                dve.wait_ge(part_sum, t + 1)
                v.scalar_tensor_tensor(out=h, in0=yrow[t][1], scalar=gates[:, 1, t:t + 1], in1=h,
                                       op0=ALU.mult, op1=ALU.add).then_inc(out_ready, 1)


R_TAKEN, R_OH1, R_OH2, R_LE, R_EQ, R_POS = (TT * E * i for i in range(6))
R_LG = TT * E * 6
R_EXG = R_LG + TT * 36
R_EQG = R_EXG + TT * NG
R_EX2 = R_EQG + TT * NG
R_ONE = R_EX2 + TT
R_CNT = R_ONE + TT * 11
R_NB = R_CNT + NT
R_SA = R_NB + E
R_SB = R_SA + E
R_OVER = R_SB + E
R_SUMS = R_OVER + E * (T // TB - 1)
R_DEST = R_SUMS + TT * E


def shape_constants():
    c = np.zeros((P, NC_CONST), np.float32)
    p = np.arange(P)
    c[:, C_ID:C_ID + P] = np.eye(P)
    c[:, C_ONE:C_ONE + P] = 1.0
    c[:, C_LOW:C_LOW + P] = p[:, None] < p[None, :]
    c[:, C_TRI:C_TRI + P] = p[:, None] <= p[None, :]
    d = p[:, None] + (T - P) - np.arange(T)[None, :]
    n = np.zeros(d.shape)
    for window, dil in ((128, 1), (512, 4), (2048, 16)):
        n += (d >= 0) & (d <= window) & (d % dil == 0)
    c[:, C_BAND:C_BAND + T] = np.where(n > 0, np.log(np.maximum(n, 1)) / SCALE, OFF)
    c[:, C_GI:C_GI + TT * NG] = np.tile(np.arange(NG) + BIG, TT)
    c[:, C_EI:C_EI + TT * E] = np.tile(np.arange(E), TT)
    c[:, C_EG:C_EG + TT * E] = np.tile(np.arange(E) // EG, TT)
    c[:, C_P] = p
    c[:, C_HALF] = 2 * NOWHERE + (p >= TB)
    c[:, C_TH:C_TH + T // TB - 1] = TB * np.arange(1, T // TB)
    c[:, C_SLOT:C_SLOT + P] = np.arange(P) % TB
    c[:, C_BLK:C_BLK + NT] = np.arange(NT)
    c[:, C_PAIR:C_PAIR + 2 * TT] = np.arange(2 * TT)[None, :] * P + p[:, None] - NOWHERE
    c[:, C_FOLD:C_FOLD + 36] = (p[:, None] % RC) == np.arange(36)[None, :]
    return c


def kernel(**inputs):
    import concourse.bacc as bacc
    from concourse.bass_utils import run_bass_kernel_spmd

    a = {k: np.asarray(v) for k, v in inputs.items()}
    consts = shape_constants()

    def by_tile(v):
        return v.reshape(-1, P).T

    def spread(v):
        return np.broadcast_to(v, (P, v.shape[-1]))

    cols = np.concatenate([
        np.concatenate([a["conv_w"][0], a["conv_b"]]).reshape(TAPS + 1, 4, P).transpose(2, 1, 0).reshape(P, -1),
        by_tile(a["conv_ln_g"][0]), by_tile(a["conv_ln_b"][0]),
        by_tile(a["out_norm"][0, W:2 * W]), a["q_norm"][0][:, None], a["k_norm"][0][:, None],
        a["sgu_b"][0].T, by_tile(a["norm2"][0]), a["norm2"][0].reshape(P, KT)], axis=1)
    w_in, w_out = a["w_in"][0], a["w_out"][0]
    U, VA, CA, CG, QQ, KK, VV = 0, 512, 1024, 1536, 2048, 3072, 4096

    def token_group(w, c0):
        return w[:, c0:c0 + W].reshape(4, 4, P, W).transpose(0, 2, 1, 3).reshape(4, P, CH)

    def tiles(*starts):
        return np.stack([w_in[:, c:c + P].reshape(KT, P, P).transpose(1, 0, 2).reshape(P, CH) for c in starts])

    stream = np.concatenate(
        [token_group(w_in, VV), token_group(w_in, VV + W)]
        + [tiles(CA + j * P, CG + j * P) for j in range(4)]
        + [token_group(w_in, U), token_group(w_in, VA)]
        + [tiles(QQ + h * P, KK + h * P) for h in range(H)]
        + [token_group(w_out, g * W) for g in range(4)])
    w_rt = np.concatenate([a["w_router_group"][0], a["w_router_expert"][0]], axis=1)
    w_rt = np.pad(w_rt, ((0, 0), (0, RC - 36))).reshape(KT, P, RC).transpose(1, 0, 2)
    rbias = np.broadcast_to(np.concatenate([a["b_router_group"][0], a["b_router_expert"][0]]), (P, TT, 36))
    ins = {
        "x": a["x"][0], "consts": consts, "cols": cols,
        "rows_a": np.concatenate([spread(a["sgu_norm"][0]), spread(a["out_norm"][0, :W])], axis=1),
        "row_c": spread(a["out_norm"][0, 2 * W:]), "row_n1": spread(a["norm1"][0]),
        "rbias": rbias, "sgu_wt": a["sgu_w"][0].transpose(2, 0, 1),
        "w_stream": stream, "w_rt": w_rt,
        "w_gate": a["w_expert_gate"][0], "w_up": a["w_expert_up"][0], "w_down": a["w_expert_down"][0],
    }
    ins = {f"in_{k}": np.ascontiguousarray(v) for k, v in ins.items()}
    nc = bacc.Bacc("TRN2", target_bir_lowering=False, num_devices=1)
    args = [nc.dram_tensor(k, list(v.shape), mybir.dt.from_np(v.dtype), kind="ExternalInput").ap()
            for k, v in ins.items()]
    out = nc.dram_tensor("out_rows", [T, D], F32, kind="ExternalOutput").ap()
    build(nc, *args, out)
    r = run_bass_kernel_spmd(nc, [ins], core_ids=[0])
    return r.results[0]["out_rows"].reshape(1, T, D)
```

```python
import math
from contextlib import ExitStack

import numpy as np

import concourse.bass as bass
from concourse import mybir

F32 = mybir.dt.float32
I32 = mybir.dt.int32
F32R = mybir.dt.float32r
ALU = mybir.AluOpType
ACT = mybir.ActivationFunctionType
AX = mybir.AxisListType.X

P = 128
T = 512
D = 2048
TT = T // P
KT = D // P
W = 512
CH = 2048
HC = CH // 2
QS = 32
H = 8
TAPS = 31
E = 32
EG = 8
NG = E // EG
FE = 512
FT = FE // P
TB = 64
NBLK = E + 2 * T // TB
NT = NBLK + 1
RC = 64
EC = 12
EPS = 1e-6
SCALE = P ** -0.5
OFF = -1.0e30
GONE = -3.0e38
NOWHERE = 1 << 20
BIG = 64.0

C_ID, C_ONE, C_LOW, C_TRI, C_BAND = 0, 128, 256, 384, 512
C_GI = C_BAND + W
C_EI = C_GI + TT * NG
C_EG = C_EI + TT * E
C_P = C_EG + TT * E
C_HALF = C_P + 1
C_TH = C_HALF + 1
C_SLOT = C_TH + T // TB - 1
C_BLK = C_SLOT + P
C_PAIR = C_BLK + NT
C_FOLD = C_PAIR + 2 * TT
NC_CONST = C_FOLD + 36

K_CW, K_LG, K_LB, K_OB = 0, 128, 132, 136
K_Q, K_K, K_SB = 140, 141, 142
K_N2, K_N2R = 146, 162
NC_COLS = 178

R_SGU, R_OA = 0, 512

Q_V, Q_B, Q_A, Q_QK, Q_O, QUADS = 0, 2, 4, 6, 10, 14


class Chain:

    def __init__(self, eng, sem, base=0):
        self.eng, self.sem, self.base, self.n = eng, sem, base, 0

    def add(self, ins):
        ins.then_inc(self.sem, 1)
        self.n += 1

    def wait(self):
        self.eng.wait_ge(self.sem, self.base + self.n)

    def link(self, ins):
        self.add(ins)
        self.wait()


def build(nc, x, consts, cols, rows_a, row_c, row_n1, rbias, sgu_wt, w_stream, w_rt,
          w_gate, w_up, w_down, out):
    with ExitStack() as ctx:
        def sb(name, shape, dt=F32):
            return ctx.enter_context(nc.sbuf_tensor(name, shape, dt))

        def sem(name):
            return ctx.enter_context(nc.semaphore(name))

        y_dram = nc.dram_tensor("y_rows", [4 * T, D // 2], F32, kind="Internal").ap()

        def shared(*shapes):
            with ExitStack() as place:
                return [place.enter_context(nc.sbuf_tensor(name, shape, dt)) for name, shape, dt in shapes]

        _, w_parts = shared(("stream_slots", [P, 2 * CH], F32), ("w_parts", [P, 2 * CH], F32R))
        arena = sb("arena", [P, EC * CH])
        hn_low, = shared(("hn_low", [P, KT, T], F32R))
        xh = sb("xh", [P, TT, D])
        hn_high, = shared(("hn_high", [P, KT, T], F32R))
        hnT = sb("hnT", [P, KT, T])
        mix_ab, = shared(("mix_ab", [P, KT, T], F32R))
        mixT = sb("mixT", [P, KT, T])
        cst = sb("cst", [P, NC_CONST])
        col = sb("col", [P, NC_COLS])
        rowa = sb("rowa", [P, 2 * W])
        sguw = sb("sguw", [P, 4, P])
        ss = sb("ss", [P, 16])
        rs = sb("rs", [P, 16])
        nmax = sb("nmax", [P, TT])
        pmax = sb("pmax", [P, TT])
        den = sb("den", [P, 2 * TT])
        rden = sb("rden", [P, TT])
        cwj = sb("cwj", [P, 32])
        eps = sb("eps", [P, 1])
        place_i = sb("place_i", [P, 2, TT], I32)
        gates = sb("gates", [P, 2, TT])
        sched = sb("sched", [1, P + 1], I32)
        tab_row = sb("tab_row", [P, NT], I32)
        tab_rs = sb("tab_rs", [P, NT])
        slot_i = sb("slot_i", [P, 2, TT], I32)
        blk_i = sb("blk_i", [P, 2, TT], I32)
        ss_h = sb("ss_h", [P, TT, 4])
        idx_row = sb("idx_row", [2 * TB, 1], I32)

        ident = cst[:, C_ID:C_ID + P]
        ones = cst[:, C_ONE:C_ONE + P]
        low = cst[:, C_LOW:C_LOW + P]

        def rows_by_tile(ap):
            return ap.rearrange("(t p) n -> p t n", p=P)

        def slot(c):
            return arena[:, c * CH:(c + 1) * CH]

        w_hi = [w_parts[:, i * HC:(i + 1) * HC] for i in range(2)]
        w_lo = [w_parts[:, CH + i * HC:CH + (i + 1) * HC] for i in range(2)]
        x_rows = mixT[:, :, :].rearrange("p k t -> p (k t)").rearrange("p (t n) -> p t n", t=TT)

        def hn_parts(k):
            return hn_high[:, k, :], hn_low[:, k, :]

        def mix_parts(k):
            home = mix_ab if k < 8 else mix_c
            return home[:, k % 8, :], home[:, 8 + k % 8, :]

        mix_c = hn_high

        def low_part(eng, low, x, high):
            return eng.tensor_tensor(low, x, high.bitcast(F32), ALU.subtract)

        vt = arena[:, 4 * CH:6 * CH].rearrange("p (t n) -> p t n", t=TT)
        tmp = arena[:, 6 * CH:12 * CH]
        n1row = tmp[:, 0:2048]
        hn = [tmp[:, 2048:4096], tmp[:, 4096:6144]]
        x_sq = tmp[:, 6144:8192]
        u_sb = tmp[:, 0:2048].rearrange("p (t n) -> p t n", t=TT)
        va = tmp[:, 2048:4096].rearrange("p (t n) -> p t n", t=TT)
        BB = 6144
        sig = tmp[:, BB:BB + 512]
        ZW = W + 32
        z = [tmp[:, BB + 512 + ZW * i:BB + 512 + ZW * (i + 1)] for i in range(2)]
        sqb = tmp[:, BB:BB + 2048].rearrange("p (j n) -> p j n", j=4)
        cbuf = tmp[:, BB + 2112:BB + 4160].rearrange("p (j n) -> p j n", j=4)
        mu = tmp[:, BB + 4160:BB + 4672]
        rb = tmp[:, BB + 4672:BB + 5184]
        yc = tmp[:, 0:4096].rearrange("p (t n) -> p t n", t=TT)
        qT = [tmp[:, 4096 + 1024 * i:4608 + 1024 * i] for i in range(2)]
        kT = [tmp[:, 4608 + 1024 * i:5120 + 1024 * i] for i in range(2)]
        sqq, sqk = tmp[:, 6144:6656], tmp[:, 6656:7168]
        rqk = [tmp[:, 7168:7680], tmp[:, 10752:11264]]
        sp_ = [tmp[:, 7680 + 512 * i:8192 + 512 * i] for i in range(2)]
        pT = [tmp[:, 8704 + 512 * i:9216 + 512 * i] for i in range(2)]
        rowc = tmp[:, 9728:10752]
        wrt = tmp[:, 4 * CH:4 * CH + KT * RC].rearrange("p (k n) -> p k n", n=RC)
        rbr = tmp[:, 4 * CH + 1024:4 * CH + 1024 + TT * 36].rearrange("p (t n) -> p t n", t=TT)
        h_sq = tmp[:, 4 * CH + 1200:4 * CH + 1712]
        hT_all = arena[:, 4 * CH:8 * CH].rearrange("p (k n) -> p k n", k=KT)
        junk_a = mixT[:, 8:12, :]
        junk_c = hnT[:, 0:8, :].rearrange("p (t k) n -> p t (k n)", t=TT)
        rt = hnT[:, :, :].rearrange("p k t -> p (k t)")
        logitT = rt[:, 6144:6144 + T]
        place = rt[:, R_DEST:R_DEST + 2 * TT].rearrange("p (k t) -> p k t", k=2)
        oh_slot = rt[:, 2048:2048 + 2 * TT * P].rearrange("p (i n) -> p i n", n=P)
        oh_blk = rt[:, 3072:3072 + 2 * TT * NT].rearrange("p (i n) -> p i n", n=NT)
        oh_vals = rt[:, 3584:3584 + 4 * TT * NT].rearrange("p (i n) -> p i n", n=2 * NT)
        oh_pair, oh_rs = oh_vals[:, :, 0:NT], oh_vals[:, :, NT:2 * NT]
        blk = mixT[:, :, :].rearrange("p k t -> p (k t)")
        xg = blk[:, 0:D // 2]
        at_slot = blk[:, D // 2:D // 2 + 2 * TT * TB].rearrange("p (i n) -> p i n", n=TB)
        picks = blk[:, D // 2 + 512:D // 2 + 512 + TT * TB].rearrange("p (t n) -> p t n", t=TT)
        ysb = blk[:, D:D + 2 * W]
        gu = blk[:, D + 2 * W:D + 3 * W]
        xgT = blk[:, 2 * D:2 * D + KT * TB]
        sg, hT = (blk[:, 5120 + i * FT * TB:5120 + (i + 1) * FT * TB] for i in range(2))
        yrow = [[slot(2 * t + k) for k in range(2)] for t in range(TT)]

        bank = [ctx.enter_context(nc.psum_tensor(f"bank{i}", [P, W], F32)) for i in range(8)]
        acc, pat = bank[0:4], bank[4:8]
        z_bank = pat[0:3] + acc[2:3]
        u_bank = acc[0:2] + pat[1:3]
        cacc = pat[0][:, :]
        guT = bank[1][:, :].rearrange("p (f n) -> p f n", f=FT)

        eps_set = sem("eps_set")
        x_in = [sem(f"x_in{t}") for t in range(TT)]
        const_in = sem("const_in")
        ident_in = sem("ident_in")
        n1_in = sem("n1_in")
        rowc_in = sem("rowc_in")
        n2_in = sem("n2_in")
        w_in_slot = [sem(f"w_in_slot{c}") for c in range(2)]
        w_hi_ready = sem("w_hi_ready")
        w_lo_ready = sem("w_lo_ready")
        lo_evac = sem("lo_evac")
        dve_own = sem("dve_own")
        hn_ready = sem("hn_ready")
        turned = sem("turned")
        act_evac = sem("act_evac")
        proj_steps = sem("proj_steps")
        z_ready = sem("z_ready")
        sig_ready = sem("sig_ready")
        conv_own = sem("conv_own")
        conv_done = sem("conv_done")
        b_added = sem("b_added")
        b_sum = sem("b_sum")
        b_cent = sem("b_cent")
        b_norm = sem("b_norm")
        b_sq = sem("b_sq")
        b_silu = sem("b_silu")
        b_mixed = sem("b_mixed")
        sguw_ready = sem("sguw_ready")
        va_normed = sem("va_normed")
        spatial = sem("spatial")
        ya_ready = sem("ya_ready")
        qk_sq = sem("qk_sq")
        qk_sum = sem("qk_sum")
        qkT_ready = sem("qkT_ready")
        qk_root = sem("qk_root")
        r_own = sem("r_own")
        stat_ready = sem("stat_ready")
        root_done = sem("root_done")
        s_ready = sem("s_ready")
        s_max = sem("s_max")
        s_masked = sem("s_masked")
        p_ready = sem("p_ready")
        p_turned = sem("p_turned")
        pT_ready = sem("pT_ready")
        pv_done = sem("pv_done")
        rden_ready = sem("rden_ready")
        o_done = sem("o_done")
        yc_ready = sem("yc_ready")
        h_added = sem("h_added")
        h_sq_done = sem("h_sq_done")
        wrt_scaled = sem("wrt_scaled")
        logitT_ready = sem("logitT_ready")
        folded = sem("folded")
        logits = sem("logits")
        gate_exp = sem("gate_exp")
        exp_in = sem("exp_in")
        picked = sem("picked")
        ranked = sem("ranked")
        sched_col = sem("sched_col")
        sched_row = sem("sched_row")
        sched_ready = sem("sched_ready")
        onehots = sem("onehots")
        tabs_made = sem("tabs_made")
        tabs_ready = sem("tabs_ready")
        e_in_slot = [sem(f"e_in_slot{c}") for c in range(EC)]
        e_used = sem("e_used")
        place_ready = sem("place_ready")
        at_slot_ready = sem("at_slot_ready")
        picks_ready = sem("picks_ready")
        xg_made = sem("xg_made")
        xg_evac = sem("xg_evac")
        idx_r_ready = sem("idx_r_ready")
        xg_turned = sem("xg_turned")
        xgT_ready = sem("xgT_ready")
        gu_ready = sem("gu_ready")
        gu_turned = sem("gu_turned")
        sg_ready = sem("sg_ready")
        hT_ready = sem("hT_ready")
        y_evac_a = sem("y_evac_a")
        y_evac_v = sem("y_evac_v")
        y_stored = sem("y_stored")
        yrow_in = [sem(f"yrow_in{t}") for t in range(TT)]
        part_sum = sem("part_sum")
        out_ready = sem("out_ready")
        out_stored = sem("out_stored")

        CR_Z, CR_QK, CR_S, CR_PT, CR_O = 2, 2, 4, 4, 1
        CR_E, CR_GU, CR_GT, CR_SG, CR_H, CR_Y, CR_YS = EC, 1, 1, 1, 1, 1, 16
        EV_V = 16
        EV_U = EV_V + 8
        EV_A = EV_U + 8
        EV_C = EV_A + 4
        EV_R = EV_C + 8

        counts = {}

        def wait_alone(eng, *waits):
            for i in range(len(waits)):
                if (eng, i) not in counts:
                    counts[eng, i] = eng.alloc_register(f"count{i}")
                eng.reg_mov(counts[eng, i], waits[i][1])
            eng.wait_ge(const_in, 16 * 4)
            for i, (s, _) in enumerate(waits):
                eng.wait_ge(s, counts[eng, i])

        block = ctx.enter_context(nc.Block())

        @block.sync
        def _(sp):
            sp.dma_start(x_rows[:, 0, :], x[0:P, :]).then_inc(x_in[0], 16)
            sp.dma_start(n1row, row_n1).then_inc(n1_in, 16)
            sp.dma_start(cst[:, 0:P], consts[:, 0:P]).then_inc(ident_in, 16)
            for t in range(1, TT):
                sp.dma_start(x_rows[:, t, :], x[t * P:(t + 1) * P, :]).then_inc(x_in[t], 16)
            for c in range(2):
                sp.dma_start(slot(c), w_stream[c]).then_inc(w_in_slot[c], 16)
            sp.dma_start(cst[:, P:], consts[:, P:]).then_inc(const_in, 16)
            sp.dma_start(col[:, :], cols).then_inc(const_in, 16)
            sp.dma_start(rowa[:, :], rows_a).then_inc(const_in, 16)
            sp.dma_start(sguw[:, :, :], sgu_wt).then_inc(const_in, 16)

            def stream(q, c):
                src = w_stream[4 * q + c] if isinstance(q, int) else \
                    w_stream[bass.ds(q * 4 + c, 1)].rearrange("o p n -> (o p) n")
                wait_alone(sp, (w_lo_ready, q * 16 + (4 * c - 4)))
                sp.dma_start(slot(c % 2), src).then_inc(w_in_slot[c % 2], 16)

            for c in range(2, 4):
                stream(0, c)
            with sp.Fori(1, Q_O) as q:
                for c in range(4):
                    stream(q, c)
            for c in range(4):
                stream(Q_O, c)
            sp.wait_ge(proj_steps, QS * Q_O)
            for t in range(TT):
                sp.dma_start(xh[:, t, :], x[t * P:(t + 1) * P, :]).then_inc(x_in[t], 16)
            with sp.Fori(Q_O + 1, QUADS) as q:
                for c in range(4):
                    stream(q, c)

            def expert(c, e):
                if c < 8:
                    m = w_gate if c % 2 == 0 else w_up
                    k = (c // 2) * 4
                    return m[e].rearrange("o (p k) n -> (o p) k n", k=KT)[:, k:k + 4, :]
                return w_down[e].rearrange("o (f p) n -> f (o p) n", p=P)[c - 8]

            def dst(c):
                return slot(c).rearrange("p (k n) -> p k n", k=4) if c < 8 else slot(c)

            def first_expert(*chunks):
                for c in chunks:
                    sp.dma_start(dst(c), expert(c, slice(0, 1))).then_inc(e_in_slot[c], 16)

            sp.wait_ge(lo_evac, 28)
            first_expert(8, 9, 11)
            sp.wait_ge(w_lo_ready, 16 * QUADS)
            first_expert(0, 1)
            sp.wait_ge(proj_steps, QS * QUADS)
            first_expert(2, 3)
            sp.wait_ge(logits, 1)
            first_expert(4, 5, 6, 7)
            sp.wait_ge(picked, 1)
            first_expert(10)
            sp.wait_ge(sched_ready, 1)
            nb = sp.value_load(sched[0:1, P:P + 1], min_val=E, max_val=NBLK)
            with sp.Fori(1, nb) as b:
                e = sp.value_load(sched[0:1, bass.ds(b, 1)], min_val=0, max_val=E - 1)
                before = sp.value_load(sched[0:1, bass.ds(b - 1, 1)], min_val=0, max_val=E - 1)
                for c in range(EC):
                    wait_alone(sp, (e_used, b * EC + (c + 1)))
                    sp.dma_start(dst(c), expert(c, bass.ds(e, 1)), cond=(e != before))\
                        .then_inc(e_in_slot[c], 16)
            sp.wait_ge(y_stored, nb * 16 + CR_YS)
            for t in range(TT):
                for k in range(2):
                    r = k * T + t * P
                    sp.dma_start(yrow[t][k], y_dram.rearrange("(r h) n -> r (h n)", h=2)[r:r + P, :])\
                        .then_inc(yrow_in[t], 16)
            for t in range(TT):
                sp.wait_ge(out_ready, t + 1)
                sp.dma_start(out[t * P:(t + 1) * P, :], xh[:, t, :]).then_inc(out_stored, 16)
            sp.wait_ge(out_stored, 16 * TT)

        @block.gpsimd
        def _(pool):
            pool.memset(eps[:, :], EPS).then_inc(eps_set, 1)
            with pool.Fori(0, QUADS) as q:
                for h in range(8):
                    for i in range(2):
                        c0 = i * W
                        pool.wait_ge(w_hi_ready, q * 8 + (h + 1))
                        low_part(pool, w_lo[h % 2][:, c0:c0 + W],
                                 slot((h // 2) % 2)[:, (h % 2) * HC + c0:(h % 2) * HC + c0 + W],
                                 w_hi[h % 2][:, c0:c0 + W]).then_inc(w_lo_ready, 1)
            pool.dma_start(idx_row[0:1, :].bitcast(F32), x[0:1, 0:1]).then_inc(y_stored, CR_YS)
            pool.wait_ge(sched_ready, 1)
            nb = pool.value_load(sched[0:1, P:P + 1], min_val=E, max_val=NBLK)
            with pool.Fori(0, nb) as b:
                wait_alone(pool, (idx_r_ready, b + 1), (y_evac_a, b + (CR_Y + 1)),
                           (y_evac_v, b + (CR_Y + 1)))
                pool.indirect_dma_start(
                    out=y_dram, out_offset=bass.IndirectOffsetOnAxis(ap=idx_row[:, 0:1], axis=0),
                    in_=ysb, in_offset=None, bounds_check=4 * T - 1, oob_is_err=False).then_inc(y_stored, 16)

        @block.tensor
        def _(pe):
            def turn(dst_bank, col0, src, idn, rows, last=None):
                m = pe.transpose(dst_bank[0:rows, col0:col0 + src.shape[0]], src, idn)
                if last is not None:
                    m.then_inc(last, 1)

            pe.wait_ge(ident_in, 16)
            for t in range(TT):
                pe.wait_ge(hn_ready, t + 1)
                for q in range(4):
                    f = t * 4 + q
                    if f >= 8:
                        pe.wait_ge(lo_evac, f - 7)
                    for i in range(4):
                        k = q * 4 + i
                        turn(bank[f % 8], i * P, hn[t % 2][:, k * P:(k + 1) * P], ident, P,
                             turned if i == 3 else None)

            def three(bank_, a, b, first, last):
                pe.matmul(bank_, a[0], b[0], start=first, stop=False)
                pe.matmul(bank_, a[1], b[0], start=False, stop=False)
                return pe.matmul(bank_, a[0], b[1], start=False, stop=last)

            def half_split(q, h):
                pe.wait_ge(w_lo_ready, q * 16 + (2 * h + 2))

            def tokens_step(h, j, parts, banks=acc):
                for i in range(2):
                    k = 2 * h + i
                    m = three(banks[j][:, :], [a[:, j * P:(j + 1) * P] for a in parts(k)],
                              [w[h % 2][:, i * W:(i + 1) * W] for w in (w_hi, w_lo)], k == 0, k == KT - 1)
                m.then_inc(proj_steps, 1)

            def half_tokens(h, q, parts, free, banks=acc):
                half_split(q, h)
                for j in range(TT):
                    if h == 0:
                        free(j)
                    tokens_step(h, j, parts, banks)

            def tile_step(c, k, q):
                h = 2 * c + k // 8
                if k % 8 == 0:
                    half_split(q, h)
                m = three(acc[c][:, :], [w[h % 2][:, (k % 8) * P:(k % 8 + 1) * P] for w in (w_hi, w_lo)],
                          hn_parts(k), k == 0, k == KT - 1)
                if k % 2 == 1:
                    m.then_inc(proj_steps, 1)

            def free_v(j):
                pe.wait_ge(act_evac, g * 8 + (EV_V - 7 + j))
                pe.wait_ge(lo_evac, max(9 + j, 4 * (j + 1)))

            with pe.Fori(0, 2) as g:
                for h in range(8):
                    half_tokens(h, g, hn_parts, free_v)
            pe.wait_ge(act_evac, EV_U)
            with pe.Fori(0, 2) as i:
                for u in range(2):
                    for w in range(2):
                        c = 2 * u + w
                        pe.wait_ge(z_ready if w == 0 else sig_ready, i * 2 + (u + CR_Z - 1))
                        for k in range(KT):
                            tile_step(c, k, i + Q_B)
            pe.wait_ge(z_ready, CR_Z + 3)
            for h in range(8):
                half_tokens(h, Q_A, hn_parts, lambda j: None, u_bank)

            def free_va(j):
                if j < 2:
                    pe.wait_ge(act_evac, EV_U + 1 + j)
                else:
                    pe.wait_ge(z_ready, CR_Z + 4)

            for h in range(8):
                half_tokens(h, Q_A + 1, hn_parts, free_va)
                if h == 3:
                    pe.wait_ge(b_added, 1)
                    pe.matmul(pat[3][:, :], ones, mu, start=True, stop=True).then_inc(b_sum, 1)
            pe.wait_ge(b_added, 2)
            pe.matmul(pat[3][:, :], ones, rb, start=True, stop=True).then_inc(b_sum, 1)

            def proj_head(h, q, c0, lo, hi):
                for s in range(lo, hi):
                    w, k = divmod(s, KT)
                    if k == 0:
                        if w == 0:
                            pe.wait_ge(qkT_ready, h * 2 + (CR_QK - 2))
                    tile_step(c0 + w, k, q)

            pe.wait_ge(act_evac, EV_A)
            for k in range(KT):
                tile_step(0, k, Q_QK)
            pe.wait_ge(sguw_ready, 1)
            for n in range(TT):
                pe.wait_ge(va_normed, n + 1)
                for hh in range(4):
                    m = pe.matmul(z_bank[n][:, hh * P:(hh + 1) * P], sguw[:, hh, :], va[:, n, hh * P:(hh + 1) * P],
                                  start=True, stop=True)
                m.then_inc(spatial, 1)
            for k in range(KT):
                tile_step(1, k, Q_QK)
            pe.wait_ge(b_added, 3)
            pe.matmul(pat[3][:, :], ones, rb, start=True, stop=True).then_inc(b_sum, 1)
            for n in range(TT):
                pe.wait_ge(ya_ready, n + 1)
                if n == 3:
                    pe.wait_ge(root_done, 8)
                for i in range(4):
                    turn(pat[n], i * P, u_sb[:, n, i * P:(i + 1) * P], ident, P, turned if i == 3 else None)

            def norm_sums(g):
                pe.wait_ge(lo_evac, 20)
                pe.wait_ge(s_masked, g * 4 + CR_S)
                for w, sq in enumerate((sqq, sqk)):
                    pe.wait_ge(qk_sq, g * 2 + (w + 1))
                    pe.matmul(pat[w][:, :], ones, sq, start=True, stop=True).then_inc(qk_sum, 1)

            def scores(g, par, qi):
                if qi == 0:
                    pe.wait_ge(qkT_ready, g * 2 + (CR_QK + 2))
                if qi >= 2:
                    pe.wait_ge(s_masked, g * 4 + (CR_S + qi - 1))
                n = (qi + 1) * P
                pe.matmul(pat[qi % 2][:, 0:n], qT[par][:, qi * P:n], kT[par][:, 0:n],
                          start=True, stop=True).then_inc(s_ready, 1)

            def turn_p(g, qi):
                pe.wait_ge(p_ready, g * 4 + (qi + 1))
                pe.wait_ge(pT_ready, g * 4 + (CR_PT + qi))
                for j in range(qi + 1):
                    turn(pat[2], j * P, sp_[qi % 2][:, j * P:(j + 1) * P], ident, P,
                         p_turned if j == qi else None)

            def pv(g, qi):
                pe.wait_ge(pT_ready, g * 4 + (CR_PT + qi + 1))
                if qi == 0:
                    pe.wait_ge(o_done, g + CR_O)
                for j in range(qi + 1):
                    v_head = vt[:, j, bass.ds(g * P, P)] if not isinstance(g, int) else vt[:, j, g * P:(g + 1) * P]
                    m = pe.matmul(pat[3][:, qi * P:(qi + 1) * P], pT[qi % 2][:, j * P:(j + 1) * P], v_head,
                                  start=(j == 0), stop=(j == qi))
                m.then_inc(pv_done, 1)

            def attention_part(g, par, s):
                if s == 0:
                    norm_sums(g)
                if 1 <= s <= 4:
                    scores(g, par, s - 1)
                if 2 <= s <= 5:
                    turn_p(g, s - 2)
                if 3 <= s <= 6:
                    pv(g, s - 3)

            CUTS = [0, 2, 14, 18, 22, 25, 28, 32]
            with pe.Fori(0, 3) as i:
                for s in range(7):
                    proj_head(i * 2 + 1, i + Q_QK, 2, CUTS[s], CUTS[s + 1])
                    attention_part(i * 2, 0, s)
                for s in range(7):
                    proj_head(i * 2 + 2, i + (Q_QK + 1), 0, CUTS[s], CUTS[s + 1])
                    attention_part(i * 2 + 1, 1, s)
            for s in range(7):
                proj_head(H - 1, Q_QK + 3, 2, CUTS[s], CUTS[s + 1])
                attention_part(H - 2, 0, s)

            ATT = ((0,), (), (1,), (2,), (3,), (4,), (5,), (6,))
            for s in range(8):
                h, j0 = 2 * (s // 4) + s % 2, 2 * (s // 2 % 2)
                if s % 4 < 2:
                    half_split(Q_O, h)
                if s == 0:
                    pe.wait_ge(qkT_ready, CR_QK + 2 * (H - 1))
                    pe.wait_ge(qk_sq, 2 * (H - 1))
                if s == 2:
                    pe.wait_ge(qkT_ready, CR_QK + 2 * H)
                tokens_step(h, j0, mix_parts)
                if s < 7:
                    tokens_step(h, j0 + 1, mix_parts)
                for part in ATT[s]:
                    attention_part(H - 1, 1, part)
            tokens_step(h, j0 + 1, mix_parts)
            for n in range(TT):
                pe.wait_ge(yc_ready, n + 1)
                for w in range(2):
                    f = 2 * n + w
                    if f >= 4:
                        pe.wait_ge(lo_evac, 20 + f - 3)
                    if f < 4:
                        pe.wait_ge(o_done, CR_O + H)
                    for i in range(4):
                        turn(pat[f % 4], i * P, yc[:, n, (4 * w + i) * P:(4 * w + i + 1) * P], ident, P,
                             turned if i == 3 else None)
            pe.wait_ge(lo_evac, 28)
            for h in range(4, 8):
                half_tokens(h, Q_O, mix_parts, None)
            def group_added(g):
                return lambda j: pe.wait_ge(h_added, g * 4 + (j - 3))

            with pe.Fori(1, 3) as g:
                for h in range(8):
                    half_tokens(h, g + Q_O, mix_parts, group_added(g))

            def turn_h(g, banks):
                for t in range(TT):
                    pe.wait_ge(h_added, 4 * g + t + 1)
                    pe.wait_ge(act_evac, EV_R + (4 * (g - 1) + t + 1 if g else 0))
                    for i in range(4):
                        k = 4 * g + i
                        turn(banks[t], i * P, xh[:, t, k * P:(k + 1) * P], ident, P, turned if i == 3 else None)

            for h in range(8):
                half_tokens(h, QUADS - 1, mix_parts, group_added(3))
                if h in (1, 3, 5):
                    turn_h(h // 2, pat)

            def router(k_lo, k_hi):
                for k in range(k_lo, k_hi):
                    m = pe.matmul(pat[3][(k % 2) * RC:(k % 2 + 1) * RC, :], wrt[:, k, :], hT_all[:, k, :],
                                  start=(k < 2), stop=(k >= KT - 2))
                return m

            pe.wait_ge(act_evac, EV_R + 12)
            pe.wait_ge(wrt_scaled, 1)
            router(0, 12)
            turn_h(3, pat[0:3] + acc[0:1])
            pe.wait_ge(act_evac, EV_R + 16)
            router(12, KT).then_inc(logits, 1)
            pe.wait_ge(logitT_ready, 1)
            for t in range(TT):
                m = pe.matmul(bank[1][:, t * 36:(t + 1) * 36], logitT[:, t * P:(t + 1) * P],
                              cst[:, C_FOLD:C_FOLD + 36], start=True, stop=True)
            m.then_inc(folded, 1)
            pgu, pguT, px, py, pxg = bank[0], bank[1], bank[2:4], bank[4:6], bank[6:8]

            def x_block(k):
                at = (k % 8 * 2 + k // 8) * TB
                return xgT[:, at:at + TB]

            def pick_rows(n):
                for t in range(TT):
                    for w in range(2):
                        k = 4 * n + 8 * w
                        m = pe.matmul(pxg[n][w * TB:(w + 1) * TB, :].rearrange("s (k p) -> s k p", p=P), picks[:, t, :],
                                      xh[:, t, :].rearrange("t (p k) -> t k p", k=KT)[:, k:k + 4, :],
                                      start=(t == 0), stop=(t == TT - 1))
                m.then_inc(xg_made, 1)

            def turn_rows(n):
                for i in range(4):
                    turn(px[n], i * P, xg[:, (4 * n + i) * P:(4 * n + i + 1) * P], ident, P,
                         xg_turned if i == 3 else None)

            pe.wait_ge(picked, 1)
            taken = rt[:, 0:TT * E]
            pe.matmul(bank[2][:, 0:TT * E], low, taken, start=True, stop=True)
            pe.matmul(bank[2][:, TT * E:2 * TT * E], ones, taken, start=True, stop=True).then_inc(ranked, 1)
            pe.wait_ge(picks_ready, 1)
            pick_rows(0)
            pe.wait_ge(sched_col, 1)
            pe.transpose(bank[0][0:1, 0:P], ss[:, 15:16], ident).then_inc(sched_row, 1)
            pick_rows(1)
            for n in range(2):
                pe.wait_ge(xg_evac, n + 1)
                turn_rows(n)
            pe.wait_ge(onehots, 2)
            for i in range(2 * TT):
                m = pe.matmul(bank[4][:, 0:2 * NT], oh_slot[:, i, :], oh_vals[:, i, :],
                              start=(i == 0), stop=(i == 2 * TT - 1))
            m.then_inc(tabs_made, 1)

            pe.sem_inc(e_used, CR_E)
            pe.wait_ge(sched_ready, 1)
            nb = pe.value_load(sched[0:1, P:P + 1], min_val=E, max_val=NBLK)
            with pe.Fori(0, nb) as b:
                pe.wait_ge(xgT_ready, b * 2 + 2)
                for c in range(4):
                    pe.wait_ge(e_in_slot[2 * c], b * 16 + 16)
                    pe.wait_ge(e_in_slot[2 * c + 1], b * 16 + 16)
                    if c == 0:
                        pe.wait_ge(gu_ready, b + CR_GU)
                    for i in range(4):
                        k = 4 * c + i
                        for w in range(2):
                            m = pe.matmul(pgu[w * TB:(w + 1) * TB, :], x_block(k),
                                          slot(2 * c + w)[:, i * FE:(i + 1) * FE], start=(k == 0), stop=(k == KT - 1))
                            if i == 3:
                                m.then_inc(e_used, 1)
                pe.wait_ge(gu_ready, b + (CR_GU + 1))
                for f in range(FT):
                    turn(pguT, f * P, gu[:, f * P:(f + 1) * P], ident, P, gu_turned if f == FT - 1 else None)
                pe.wait_ge(picks_ready, b + 2)
                pick_rows(0)
                pe.wait_ge(hT_ready, b + (CR_H + 1))
                pe.wait_ge(y_evac_a, b + CR_Y)
                pe.wait_ge(y_evac_v, b + CR_Y)
                for f in range(FT):
                    pe.wait_ge(e_in_slot[8 + f], b * 16 + 16)
                    for n, w in ((0, 0), (0, 1), (1, 0), (1, 1)):
                        m = pe.matmul(py[n][w * TB:(w + 1) * TB, :], hT[:, f * TB:(f + 1) * TB],
                                      slot(8 + f)[:, (2 * w + n) * W:(2 * w + n + 1) * W],
                                      start=(f == 0), stop=(f == FT - 1))
                    m.then_inc(e_used, 1)
                pick_rows(1)
                for n in range(2):
                    pe.wait_ge(xg_evac, b * 2 + (n + 3))
                    turn_rows(n)

        @block.scalar
        def _(act):
            def evac(dst, src):
                nc.scalar.activation(dst, src, ACT.Copy).then_inc(act_evac, 1)

            def root(dst, src, width):
                nc.scalar.activation(dst, src, ACT.Sqrt, bias=eps[:, 0:1], scale=1.0 / width).then_inc(root_done, 1)

            act.wait_ge(eps_set, 1)

            def high(dst, src):
                nc.scalar.activation(dst, src, ACT.Copy).then_inc(act_evac, 1)

            def split(q, h):
                q, h = q + h // 8, h % 8
                c = h // 2
                act.wait_ge(w_in_slot[c % 2], q * 32 + (16 * (c // 2) + 16))
                if not (isinstance(q, int) and 8 * q + h < 2):
                    late = 2 if isinstance(q, int) and q == Q_O and h in (2, 4) else 0
                    act.wait_ge(proj_steps, q * QS + (4 * h - 4 + late))
                nc.scalar.activation(w_hi[h % 2], slot(c % 2)[:, (h % 2) * HC:(h % 2 + 1) * HC],
                                     ACT.Copy).then_inc(w_hi_ready, 1)

            def x_stats(t):
                act.wait_ge(x_in[t], 16)
                nc.scalar.activation(x_sq, x_rows[:, t, :], ACT.Square, accum_out=ss[:, t:t + 1])\
                    .then_inc(stat_ready, 1)
                act.wait_ge(stat_ready, t + 1)
                root(rs[:, t:t + 1], ss[:, t:t + 1], D)

            nc.scalar.activation(den[:, TT:TT + 1], eps[:, 0:1], ACT.Sqrt)
            x_stats(0)
            x_stats(1)
            for f in range(16):
                t, q = divmod(f, 4)
                act.wait_ge(turned, f + 1)
                high(hn_high[:, 4 * q:4 * q + 4, t * P:(t + 1) * P],
                     bank[f % 8][:, :].rearrange("p (k n) -> p k n", k=4))
                if q == 3 and t + 2 < TT:
                    x_stats(t + 2)
                if f in (8, 11):
                    split(0, f // 10)
            with act.Fori(0, 2) as g:
                for h in range(2, 9):
                    split(g, h)
                for j in range(TT):
                    act.wait_ge(proj_steps, g * QS + (28 + j + 1))
                    nc.scalar.activation(vt[:, j, bass.ds(g * W, W)], acc[j][:, :], ACT.Copy).then_inc(act_evac, 1)
                split(g, 9)
            act.sem_inc(sig_ready, CR_Z)
            with act.Fori(0, 2) as i:
                for u in range(2):
                    for h in range(4 * u + 2, 4 * u + 6):
                        split(i + Q_B, h)
                    act.wait_ge(proj_steps, i * QS + (QS * Q_B + 16 * u + 16))
                    act.wait_ge(z_ready, i * 2 + (u + CR_Z))
                    nc.scalar.activation(sig, acc[2 * u + 1][:, :], ACT.Sigmoid).then_inc(sig_ready, 1)
            for g in range(2):
                dst = u_sb if g == 0 else va
                for h in range(2, 9):
                    split(Q_A + g, h)
                    if g == 1 and h == 5:
                        for j in range(4):
                            act.wait_ge(b_cent, j + 1)
                            nc.scalar.activation(sqb[:, j, :], cbuf[:, j, :], ACT.Square).then_inc(b_sq, 1)
                for j in range(TT):
                    act.wait_ge(proj_steps, QS * (Q_A + g) + 28 + j + 1)
                    nc.scalar.activation(dst[:, j, :], (acc if g else u_bank)[j][:, :], ACT.Gelu_apprx_tanh)\
                        .then_inc(act_evac, 1)
                split(Q_A + g, 9)
            act.wait_ge(b_sum, 2)
            root(rb, pat[3][:, :], W)
            act.wait_ge(stat_ready, 8)
            root(rs[:, 4:8], ss[:, 4:8], W)
            split(Q_QK, 2)
            for j in range(4):
                act.wait_ge(b_norm, j + 1)
                nc.scalar.activation(cbuf[:, j, :], cbuf[:, j, :], ACT.Silu, bias=col[:, K_LB + j:K_LB + j + 1],
                                     scale=col[:, K_LG + j:K_LG + j + 1]).then_inc(b_silu, 1)
            for j in range(4):
                act.wait_ge(b_silu, j + 1)
                nc.scalar.activation(sqb[:, j, :], cbuf[:, j, :], ACT.Square).then_inc(b_sq, 1)
            split(Q_QK, 3)
            act.wait_ge(stat_ready, 12)
            root(rs[:, 8:12], ss[:, 8:12], W)
            split(Q_QK, 4)
            act.wait_ge(b_sum, 3)
            root(rb, pat[3][:, :], W)
            for n in range(TT):
                act.wait_ge(turned, 16 + n + 1)
                high(mix_ab[:, 0:4, n * P:(n + 1) * P], pat[n][:, :].rearrange("p (k n) -> p k n", k=4))

            def squares(h, q, c0):
                for w, sq in enumerate((sqq, sqk)):
                    act.wait_ge(proj_steps, q * QS + (8 * (c0 + w) + 8))
                    if not isinstance(h, int) or h > 0:
                        act.wait_ge(qk_sum, h * 2 + (w - 1))
                    nc.scalar.activation(sq, acc[c0 + w][:, :], ACT.Square).then_inc(qk_sq, 1)

            def qk_roots(g):
                for w in range(2):
                    act.wait_ge(qk_sum, g * 2 + (w + 1))
                    nc.scalar.activation(rqk[w], pat[w][:, :], ACT.Sqrt, bias=eps[:, 0:1], scale=1.0 / P)\
                        .then_inc(qk_root, 1)

            def probs(g, q, h):
                qk_roots(g)
                split(q, h + 2)
                for qi in range(TT):
                    n = (qi + 1) * P
                    act.wait_ge(s_masked, g * 4 + (CR_S + qi + 1))
                    nc.scalar.activation(sp_[qi % 2][:, 0:n], sp_[qi % 2][:, 0:n], ACT.Exp,
                                         bias=nmax[:, qi:qi + 1], scale=SCALE,
                                         accum_out=den[:, qi:qi + 1]).then_inc(p_ready, 1)
                    if qi in (1, 2):
                        split(q, h + 2 + qi)
                    act.wait_ge(p_turned, g * 4 + (qi + 1))
                    if qi >= 2:
                        act.wait_ge(pv_done, g * 4 + (qi - 1))
                    nc.scalar.activation(pT[qi % 2][:, 0:n], pat[2][:, 0:n], ACT.Copy).then_inc(pT_ready, 1)

            split(Q_QK, 5)
            squares(0, Q_QK, 0)
            act.wait_ge(b_mixed, 4)
            act.dma_start(rowc, row_c).then_inc(rowc_in, 16)
            act.sem_inc(pT_ready, CR_PT)
            with act.Fori(0, 3) as i:
                probs(i * 2, i + Q_QK, 4)
                split(i + Q_QK, 9)
                squares(i * 2 + 1, i + Q_QK, 2)
                probs(i * 2 + 1, i + (Q_QK + 1), 0)
                split(i + (Q_QK + 1), 5)
                squares(i * 2 + 2, i + (Q_QK + 1), 0)
            probs(H - 2, Q_QK + 3, 4)
            split(Q_O, 1)
            squares(H - 1, Q_QK + 3, 2)
            probs(H - 1, Q_O, 0)
            split(Q_O, 5)
            act.wait_ge(stat_ready, 21)
            root(rs[:, 12:16], ss[:, 12:16], 2 * W)
            for n in range(TT):
                for w in range(2):
                    f = 2 * n + w
                    act.wait_ge(turned, 20 + f + 1)
                    high(mix_c[:, 4 * w:4 * w + 4, n * P:(n + 1) * P],
                         pat[f % 4][:, :].rearrange("p (k n) -> p k n", k=4))
            act.dma_start(wrt, w_rt).then_inc(n2_in, 16)
            act.dma_start(rbr, rbias).then_inc(n2_in, 16)
            for h in range(6, 10):
                split(Q_O, h)
            with act.Fori(Q_O + 1, QUADS - 1) as q:
                for h in range(2, 10):
                    split(q, h)

            def h_turned(g, banks):
                for t in range(TT):
                    act.wait_ge(turned, 28 + 4 * g + t + 1)
                    evac(hT_all[:, 4 * g:4 * g + 4, t * P:(t + 1) * P],
                         banks[t][:, :].rearrange("p (k n) -> p k n", k=4))

            for h in range(2, 8):
                split(QUADS - 1, h)
                if h % 2 == 1:
                    h_turned(h // 2 - 1, pat)
            h_turned(3, pat[0:3] + acc[0:1])
            act.wait_ge(stat_ready, 22)
            root(rs[:, 0:TT], ss[:, 0:TT], D)
            for n, (lo, hi) in enumerate(((R_EXG, R_EXG + TT * NG), (R_EX2, R_EX2 + TT))):
                act.wait_ge(exp_in, n + 1)
                nc.scalar.activation(rt[:, lo:hi], rt[:, lo:hi], ACT.Exp).then_inc(gate_exp, 1)

            py = bank[4:6]

            def xg_out(base, n):
                act.wait_ge(xg_turned, base)
                act.wait_ge(xg_made, base + (n + 1))
                nc.scalar.activation(xg[:, n * W:(n + 1) * W], bank[6 + n][:, :], ACT.Copy).then_inc(xg_evac, 1)

            act.wait_ge(xg_made, 1)
            nc.scalar.activation(xg[:, 0:W], bank[6][:, :], ACT.Copy).then_inc(xg_evac, 1)
            act.wait_ge(xg_made, 2)
            nc.scalar.activation(xg[:, W:2 * W], bank[7][:, :], ACT.Copy).then_inc(xg_evac, 1)
            act.sem_inc(sg_ready, CR_SG)
            act.sem_inc(y_evac_a, CR_Y)
            act.wait_ge(sched_ready, 1)
            nb = act.value_load(sched[0:1, P:P + 1], min_val=E, max_val=NBLK)

            with act.Fori(0, nb) as b:
                act.wait_ge(gu_turned, b + (CR_GT + 1))
                act.wait_ge(hT_ready, b + CR_H)
                nc.scalar.activation(sg.rearrange("p (f n) -> p f n", f=FT), guT[:, :, 0:TB], ACT.Silu)\
                    .then_inc(sg_ready, 1)
                xg_out(b * 2 + 2, 0)
                act.wait_ge(y_stored, b * 16 + CR_YS)
                act.wait_ge(e_used, b * EC + (CR_E + EC))
                nc.scalar.activation(ysb[:, 0:W], py[0][:, :], ACT.Copy).then_inc(y_evac_a, 1)
                xg_out(b * 2 + 2, 1)

        @block.vector
        def _(dve):
            own = Chain(dve, dve_own)

            roots = [0]

            def inverse(ap, root_number=None):
                roots[0] += 1
                dve.wait_ge(root_done, root_number or roots[0])
                own.link(nc.vector.reciprocal(ap, ap))

            def sum_sq(scratch, src, c):
                nc.vector.tensor_tensor_reduce(out=scratch, in0=src, in1=src, scale=1.0, scalar=0.0,
                                               op0=ALU.mult, op1=ALU.add, accum_out=ss[:, c:c + 1])\
                    .then_inc(stat_ready, 1)

            def low_turned(f, low, src, high):
                dve.wait_ge(act_evac, f)
                low_part(nc.vector, low, src[:, :].rearrange("p (k n) -> p k n", k=4), high).then_inc(lo_evac, 1)

            def low_x(t):
                for q in range(4):
                    at = (slice(None), slice(4 * q, 4 * q + 4), slice(t * P, (t + 1) * P))
                    low_turned(4 * t + q + 1, hn_low[at], bank[(4 * t + q) % 8], hn_high[at])

            dve.wait_ge(n1_in, 16)
            for t in range(TT):
                if t >= 2:
                    dve.wait_ge(turned, 4 * (t - 1))
                inverse(rs[:, t:t + 1])
                nc.vector.scalar_tensor_tensor(out=hn[t % 2], in0=x_rows[:, t, :], scalar=rs[:, t:t + 1], in1=n1row,
                                               op0=ALU.mult, op1=ALU.mult).then_inc(hn_ready, 1)
                if t >= 1:
                    low_x(t - 1)
            low_x(TT - 1)
            dve.wait_ge(const_in, 16 * 4)
            for hh in range(4):
                m = nc.vector.tensor_tensor(sguw[:, hh, :], sguw[:, hh, :], cst[:, C_TRI:C_TRI + P], ALU.mult)
                if hh < 3:
                    own.add(m)
            m.then_inc(sguw_ready, 1)
            for i in range(2):
                own.add(nc.vector.memset(z[i][:, 0:TAPS - 1], 0.0))
            own.wait()

            dve.sem_inc(z_ready, CR_Z)
            STEPS = TAPS
            with dve.Fori(0, 2) as i:
                for u in range(2):
                    conv = Chain(dve, conv_own, i * (2 * STEPS) + u * STEPS)
                    conv.add(nc.vector.tensor_copy(cwj[:, :], col[:, bass.ds(i * 64 + u * 32, TAPS + 1)]))
                    dve.wait_ge(proj_steps, i * QS + (QS * Q_B + 16 * u + 8))
                    dve.wait_ge(sig_ready, i * 2 + (u + CR_Z + 1))
                    nc.vector.tensor_tensor(z[u][:, TAPS - 1:TAPS - 1 + T], acc[2 * u][:, :], sig, ALU.mult)\
                        .then_inc(z_ready, 1)
                    dve.wait_ge(z_ready, i * 2 + (u + CR_Z + 1))
                    conv.wait()
                    conv.link(nc.vector.tensor_scalar(cacc, z[u][:, 0:T], cwj[:, 0:1], cwj[:, TAPS:TAPS + 1],
                                                      ALU.mult, ALU.add))
                    for k in range(1, TAPS - 1):
                        conv.link(nc.vector.scalar_tensor_tensor(
                            out=cacc, in0=z[u][:, k:k + T], scalar=cwj[:, k:k + 1], in1=cacc,
                            op0=ALU.mult, op1=ALU.add))
                    assert conv.n == STEPS
                    nc.vector.scalar_tensor_tensor(
                        out=cbuf[:, bass.ds(i * 2 + u, 1), :].rearrange("p o n -> p (o n)"),
                        in0=z[u][:, TAPS - 1:TAPS - 1 + T], scalar=cwj[:, TAPS - 1:TAPS],
                        in1=cacc, op0=ALU.mult, op1=ALU.add).then_inc(conv_done, 1)
                    dve.wait_ge(conv_done, i * 2 + (u + 1))
            def add_tiles(dst, src):
                own.link(nc.vector.tensor_tensor(dst, src[:, 0, :], src[:, 1, :], ALU.add))
                own.link(nc.vector.tensor_tensor(dst, dst, src[:, 2, :], ALU.add))
                nc.vector.tensor_tensor(dst, dst, src[:, 3, :], ALU.add).then_inc(b_added, 1)

            dve.wait_ge(conv_done, 4)
            add_tiles(mu, cbuf)
            dve.wait_ge(b_sum, 1)
            own.link(nc.vector.tensor_scalar(mu, pat[3][:, :], 1.0 / W, None, ALU.mult))
            for j in range(4):
                nc.vector.tensor_tensor(cbuf[:, j, :], cbuf[:, j, :], mu, ALU.subtract).then_inc(b_cent, 1)
            dve.wait_ge(b_sq, 4)
            add_tiles(rb, sqb)
            for n in range(TT):
                dve.wait_ge(act_evac, EV_U + 4 + n + 1)
                sum_sq(junk_a[:, n, :], va[:, n, :], 4 + n)
            inverse(rb)
            for j in range(4):
                nc.vector.tensor_tensor(cbuf[:, j, :], cbuf[:, j, :], rb, ALU.mult).then_inc(b_norm, 1)
            inverse(rs[:, 4:4 + TT])
            for n in range(TT):
                nc.vector.scalar_tensor_tensor(out=va[:, n, :], in0=va[:, n, :], scalar=rs[:, 4 + n:5 + n],
                                               in1=rowa[:, R_SGU:R_SGU + W], op0=ALU.mult, op1=ALU.mult)\
                    .then_inc(va_normed, 1)
            for n in range(TT):
                dve.wait_ge(spatial, n + 1)
                for hh in range(4):
                    sl = u_sb[:, n, hh * P:(hh + 1) * P]
                    own.add(nc.vector.scalar_tensor_tensor(out=sl, in0=z_bank[n][:, hh * P:(hh + 1) * P],
                                                           scalar=col[:, K_SB + hh:K_SB + hh + 1], in1=sl,
                                                           op0=ALU.add, op1=ALU.mult))
                own.wait()
                sum_sq(junk_a[:, n, :], u_sb[:, n, :], 8 + n)
            dve.wait_ge(b_sq, 8)
            add_tiles(rb, sqb)
            inverse(rs[:, 8:8 + TT], 7)
            for n in range(TT):
                nc.vector.scalar_tensor_tensor(out=u_sb[:, n, :], in0=u_sb[:, n, :], scalar=rs[:, 8 + n:9 + n],
                                               in1=rowa[:, R_OA:R_OA + W], op0=ALU.mult, op1=ALU.mult)\
                    .then_inc(ya_ready, 1)

            inverse(rb, 8)
            for n in range(TT):
                low_turned(EV_A + n + 1, mix_ab[:, 8:12, n * P:(n + 1) * P], pat[n], mix_ab[:, 0:4, n * P:(n + 1) * P])
            for j in range(4):
                own.add(nc.vector.scalar_tensor_tensor(out=cbuf[:, j, :], in0=cbuf[:, j, :],
                                                       scalar=col[:, K_OB + j:K_OB + j + 1], in1=rb,
                                                       op0=ALU.mult, op1=ALU.mult))
            own.wait()
            for j in range(4):
                own.add(nc.vector.tensor_copy(mix_ab[:, 4 + j, :], cbuf[:, j, :]))
            own.wait()
            for j in range(4):
                low_part(nc.vector, mix_ab[:, 12 + j, :], cbuf[:, j, :], mix_ab[:, 4 + j, :]).then_inc(b_mixed, 1)
            def qk_norm(g, c0):
                for w, dst in enumerate((qT[c0 // 2], kT[c0 // 2])):
                    dve.wait_ge(qk_root, g * 2 + (w + 1))
                    nc.vector.reciprocal(rqk[w], rqk[w]).then_inc(r_own, 1)
                    dve.wait_ge(r_own, g * 2 + (w + 1))
                    nc.vector.scalar_tensor_tensor(out=dst, in0=acc[c0 + w][:, :], scalar=col[:, K_Q + w:K_Q + w + 1],
                                                   in1=rqk[w], op0=ALU.mult, op1=ALU.mult).then_inc(qkT_ready, 1)

            def mask_max(g):
                for qi in range(TT):
                    n = (qi + 1) * P
                    if qi >= 2:
                        dve.wait_ge(p_turned, g * 4 + (qi - 1))
                    wait_alone(dve, (s_ready, g * 4 + (qi + 1)))
                    nc.vector.tensor_tensor_reduce(
                        out=sp_[qi % 2][:, 0:n], in0=pat[qi % 2][:, 0:n], in1=cst[:, C_BAND + T - n:C_BAND + T],
                        scale=1.0, scalar=-3.0e38, op0=ALU.add, op1=ALU.max, accum_out=pmax[:, qi:qi + 1])\
                        .then_inc(s_max, 1)
                    dve.wait_ge(s_max, g * 4 + (qi + 1))
                    nc.vector.tensor_scalar(nmax[:, qi:qi + 1], pmax[:, qi:qi + 1], -SCALE, None, ALU.mult)\
                        .then_inc(s_masked, 1)

            def rows_out(g):
                dve.wait_ge(p_ready, g * 4 + 4)
                nc.vector.reciprocal(rden[:, :], den[:, 0:TT]).then_inc(rden_ready, 1)
                dve.wait_ge(rden_ready, g + 1)
                dve.wait_ge(pv_done, g * 4 + 4)
                for qi in range(TT):
                    dst = yc[:, qi, g * P:(g + 1) * P] if isinstance(g, int) else yc[:, qi, bass.ds(g * P, P)]
                    m = nc.vector.tensor_scalar(dst, pat[3][:, qi * P:(qi + 1) * P], rden[:, qi:qi + 1], None, ALU.mult)
                m.then_inc(o_done, 1)

            dve.sem_inc(qkT_ready, CR_QK)
            dve.sem_inc(s_masked, CR_S)
            dve.sem_inc(o_done, CR_O)
            with dve.Fori(0, 3) as i:
                for u in range(2):
                    qk_norm(i * 2 + u, 2 * u)
                    mask_max(i * 2 + u)
                    rows_out(i * 2 + u)
            for g in range(H - 2, H):
                qk_norm(g, 2 * (g % 2))
                mask_max(g)
                if g == H - 1:
                    dve.wait_ge(o_done, CR_O + H - 1)
                    for n in range(TT):
                        sum_sq(junk_c[:, n, 0:g * P], yc[:, n, 0:g * P], 12 + n)
                rows_out(g)
            dve.wait_ge(o_done, CR_O + H)
            for n in range(TT):
                sum_sq(junk_c[:, n, (H - 1) * P:], yc[:, n, (H - 1) * P:], n)
            dve.wait_ge(stat_ready, 20)
            nc.vector.tensor_tensor(ss[:, 12:16], ss[:, 12:16], ss[:, 0:4], ALU.add).then_inc(stat_ready, 1)
            inverse(rs[:, 12:12 + TT])
            dve.wait_ge(rowc_in, 16)
            for n in range(TT):
                nc.vector.scalar_tensor_tensor(out=yc[:, n, :], in0=yc[:, n, :], scalar=rs[:, 12 + n:13 + n],
                                               in1=rowc, op0=ALU.mult, op1=ALU.mult).then_inc(yc_ready, 1)
            for f in range(2 * TT):
                n, w = divmod(f, 2)
                low_turned(EV_C + f + 1, mix_c[:, 8 + 4 * w:12 + 4 * w, n * P:(n + 1) * P], pat[f % 4],
                           mix_c[:, 4 * w:4 * w + 4, n * P:(n + 1) * P])
            dve.wait_ge(n2_in, 32)
            nc.vector.tensor_tensor(wrt, wrt, col[:, K_N2:K_N2 + KT].unsqueeze(2).to_broadcast([P, KT, RC]), ALU.mult)\
                .then_inc(wrt_scaled, 1)
            for t in range(TT):
                dve.wait_ge(x_in[t], 32)
            dve.sem_inc(h_sq_done, 1)
            for g in range(4):
                for j in range(TT):
                    part = xh[:, j, g * W:(g + 1) * W]
                    dve.wait_ge(proj_steps, QS * (Q_O + g) + 28 + j + 1)
                    nc.vector.tensor_tensor(part, acc[j][:, :], part, ALU.add).then_inc(h_added, 1)
                for j in range(TT):
                    part = xh[:, j, g * W:(g + 1) * W]
                    dve.wait_ge(h_added, 4 * g + j + 1)
                    dve.wait_ge(h_sq_done, 4 * g + j + 1)
                    nc.vector.tensor_tensor_reduce(out=h_sq, in0=part, in1=part, scale=1.0, scalar=0.0, op0=ALU.mult,
                                                   op1=ALU.add, accum_out=ss_h[:, j, g:g + 1]).then_inc(h_sq_done, 1)
            dve.wait_ge(h_sq_done, 4 * TT + 1)
            nc.vector.tensor_reduce(ss[:, 0:TT], ss_h[:, :, :], AX, ALU.add).then_inc(stat_ready, 1)

            def r3(o, n):
                return rt[:, o:o + TT * n].rearrange("p (t n) -> p t n", t=TT)

            def per_tile(ap, n):
                return ap.unsqueeze(2).to_broadcast([P, TT, n])

            taken, oh1, oh2 = r3(R_TAKEN, E), r3(R_OH1, E), r3(R_OH2, E)
            lg, le, eq, pos = r3(R_LG, 36), r3(R_LE, E), r3(R_EQ, E), r3(R_POS, E)
            exg, eqg = r3(R_EXG, NG), r3(R_EQG, NG)
            one = lambda i: rt[:, R_ONE + TT * i:R_ONE + TT * (i + 1)]
            gmax, gsum, gi, m1, i1, m2, i2, gg, g2r, den2, d1 = (one(i) for i in range(11))
            ex2 = rt[:, R_EX2:R_EX2 + TT]
            c3 = lambda o, n: cst[:, o:o + TT * n].rearrange("p (t n) -> p t n", t=TT)
            v = nc.vector
            dve.wait_ge(logits, 1)
            v.tensor_copy(logitT, pat[3][:, :]).then_inc(logitT_ready, 1)
            inverse(rs[:, 0:TT])
            dve.wait_ge(folded, 1)
            for t in range(TT):
                own.add(v.scalar_tensor_tensor(out=lg[:, t, :], in0=bank[1][:, t * 36:(t + 1) * 36],
                                               scalar=rs[:, t:t + 1], in1=rbr[:, t, :], op0=ALU.mult, op1=ALU.add))
            own.wait()
            own.link(v.tensor_reduce(gmax, lg[:, :, 0:NG], AX, ALU.max))
            v.tensor_tensor(exg, lg[:, :, 0:NG], per_tile(gmax, NG), ALU.subtract).then_inc(exp_in, 1)
            own.link(v.tensor_tensor(eqg, lg[:, :, 0:NG], per_tile(gmax, NG), ALU.is_equal))
            own.link(v.scalar_tensor_tensor(out=eqg, in0=eqg, scalar=-BIG, in1=c3(C_GI, NG), op0=ALU.mult, op1=ALU.add))
            own.link(v.tensor_reduce(gi, eqg, AX, ALU.min))
            own.link(v.tensor_tensor(eq, c3(C_EG, E), per_tile(gi, E), ALU.not_equal))
            own.link(v.scalar_tensor_tensor(out=le, in0=eq, scalar=OFF, in1=lg[:, :, NG:36], op0=ALU.mult, op1=ALU.add))

            def largest(mx, ix, oh):
                own.link(v.tensor_reduce(mx, le, AX, ALU.max))
                own.link(v.tensor_tensor(eq, le, per_tile(mx, E), ALU.not_equal))
                own.link(v.scalar_tensor_tensor(out=pos, in0=eq, scalar=BIG, in1=c3(C_EI, E), op0=ALU.mult, op1=ALU.add))
                own.link(v.tensor_reduce(ix, pos, AX, ALU.min))
                own.link(v.tensor_tensor(oh, c3(C_EI, E), per_tile(ix, E), ALU.is_equal))

            largest(m1, i1, oh1)
            own.link(v.scalar_tensor_tensor(out=le, in0=oh1, scalar=GONE, in1=le, op0=ALU.mult, op1=ALU.add))
            largest(m2, i2, oh2)
            v.tensor_tensor(taken, oh1, oh2, ALU.add).then_inc(picked, 1)
            v.tensor_tensor(ex2, m2, m1, ALU.subtract).then_inc(exp_in, 1)
            dve.wait_ge(gate_exp, 2)
            own.link(v.tensor_reduce(gsum, exg, AX, ALU.add))
            own.link(v.tensor_scalar(den2, ex2, 1.0, None, ALU.add))
            own.link(v.tensor_tensor(den2, den2, gsum, ALU.mult))
            own.link(v.reciprocal(gates[:, 0, :], den2))
            own.link(v.tensor_tensor(gates[:, 1, :], gates[:, 0, :], ex2, ALU.mult))
            dve.wait_ge(ranked, 1)
            cnt, nblk, over = rt[:, R_CNT:R_CNT + E], rt[:, R_NB:R_NB + E], rt[:, R_OVER:R_OVER + E * (T // TB - 1)]
            sums = r3(R_SUMS, E)
            own.link(v.tensor_copy(sums, bank[2][:, TT * E:2 * TT * E].rearrange("p (t e) -> p t e", t=TT)))
            for t in range(1, TT):
                own.link(v.tensor_tensor(sums[:, t, :], sums[:, t, :], sums[:, t - 1, :], ALU.add))
            over = over.rearrange("p (e m) -> p e m", e=E)
            M = T // TB - 1
            own.link(v.tensor_tensor(over, sums[:, TT - 1, :].unsqueeze(2).to_broadcast([P, E, M]),
                                     cst[:, C_TH:C_TH + M].unsqueeze(1).to_broadcast([P, E, M]), ALU.is_gt))
            own.link(v.tensor_reduce(nblk, over, AX, ALU.add))
            own.link(v.tensor_scalar(nblk, nblk, 1.0, None, ALU.add))
            a, bb = rt[:, R_SA:R_SA + E], rt[:, R_SB:R_SB + E]
            own.link(v.tensor_tensor_scan(a, ones[:, 0:E], nblk, 0.0, ALU.mult, ALU.add))
            own.add(v.tensor_copy(sched[0:1, P:P + 1], a[0:1, E - 1:E]))
            own.link(v.tensor_tensor(bb, a, nblk, ALU.subtract))
            own.link(v.tensor_scalar(a, bb, float(TB), None, ALU.mult))
            own.link(v.tensor_tensor(pos, bank[2][:, 0:TT * E].rearrange("p (t e) -> p t e", t=TT),
                                     a.unsqueeze(1).to_broadcast([P, TT, E]), ALU.add))
            own.link(v.tensor_tensor(pos[:, 1:TT, :], pos[:, 1:TT, :], sums[:, 0:TT - 1, :], ALU.add))
            def pick_slots(n=0):
                v.tensor_tensor(at_slot, cst[:, C_SLOT:C_SLOT + TB].unsqueeze(1).to_broadcast([P, 2 * TT, TB]),
                                place.rearrange("p k t -> p (k t)").unsqueeze(2).to_broadcast([P, 2 * TT, TB]),
                                ALU.is_equal).then_inc(at_slot_ready, 1)
                dve.wait_ge(at_slot_ready, n + 1)
                v.tensor_tensor(picks, at_slot[:, 0:TT, :], at_slot[:, TT:2 * TT, :], ALU.add).then_inc(picks_ready, 1)

            for k, (oh, at) in enumerate(((oh1, eq), (oh2, le))):
                own.add(v.tensor_tensor(at, pos, oh, ALU.mult))
            own.wait()
            for k, at in enumerate((eq, le)):
                own.add(v.tensor_reduce(place[:, k, :], at, AX, ALU.add))
            own.wait()
            pick_slots()
            own.link(v.tensor_scalar(cnt, bb, cst[:, C_P:C_P + 1], None, ALU.is_le))
            own.link(v.tensor_reduce(ss[:, 14:15], cnt, AX, ALU.add))
            v.tensor_scalar(ss[:, 15:16], ss[:, 14:15], -1.0, None, ALU.add).then_inc(sched_col, 1)
            own.link(v.tensor_copy(place_i[:, :, :], place))
            own.add(v.tensor_scalar(slot_i[:, :, :], place_i[:, :, :], TB - 1, None, ALU.bitwise_and))
            own.link(v.tensor_scalar(blk_i[:, :, :], place_i[:, :, :], TB.bit_length() - 1, None,
                                     ALU.logical_shift_right))

            def pairs_by(ap, n):
                return ap.rearrange("p k t -> p (k t)").unsqueeze(2).to_broadcast([P, 2 * TT, n])

            own.add(v.tensor_tensor(oh_blk, cst[:, C_BLK:C_BLK + NT].unsqueeze(1).to_broadcast([P, 2 * TT, NT]),
                                    pairs_by(blk_i[:, :, :], NT), ALU.is_equal))
            own.link(v.tensor_tensor(oh_slot, cst[:, C_SLOT:C_SLOT + P].unsqueeze(1).to_broadcast([P, 2 * TT, P]),
                                     pairs_by(slot_i[:, :, :], P), ALU.is_equal))
            v.tensor_tensor(oh_pair, oh_blk, cst[:, C_PAIR:C_PAIR + 2 * TT].unsqueeze(2)
                            .to_broadcast([P, 2 * TT, NT]), ALU.mult).then_inc(onehots, 1)
            for k in range(2):
                m = v.tensor_tensor(oh_rs[:, k * TT:(k + 1) * TT, :], oh_blk[:, k * TT:(k + 1) * TT, :],
                                    rs[:, 0:TT].unsqueeze(2).to_broadcast([P, TT, NT]), ALU.mult)
                if k == 0:
                    own.add(m)
            m.then_inc(onehots, 1)
            dve.wait_ge(sched_row, 1)
            v.tensor_copy(sched[0:1, 0:P], bank[0][0:1, 0:P]).then_inc(sched_ready, 1)
            dve.sem_inc(gu_ready, CR_GU)
            dve.sem_inc(gu_turned, CR_GT)
            dve.sem_inc(hT_ready, CR_H)
            dve.sem_inc(y_evac_v, CR_Y)
            dve.wait_ge(sched_ready, 1)
            nb = dve.value_load(sched[0:1, P:P + 1], min_val=E, max_val=NBLK)

            def rows_turned(base):
                for w in range(2):
                    dve.wait_ge(xg_turned, base + (w + 1))
                    v.tensor_tensor(xgT[:, w * W:(w + 1) * W].rearrange("p (k n) -> p k n", n=TB),
                                    bank[2 + w][:, :].rearrange("p (k n) -> p k n", n=TB),
                                    col[:, K_N2R + 8 * w:K_N2R + 8 * w + 8].unsqueeze(2).to_broadcast([P, 8, TB]),
                                    ALU.mult).then_inc(xgT_ready, 1)

            rows_turned(0)
            dve.wait_ge(tabs_made, 1)
            v.tensor_scalar(tab_row[:, :], bank[4][:, 0:NT], 2.0, cst[:, C_HALF:C_HALF + 1],
                            ALU.mult, ALU.add).then_inc(tabs_ready, 1)
            v.tensor_copy(tab_rs[:, :], bank[4][:, NT:2 * NT]).then_inc(tabs_ready, 1)
            dve.wait_ge(tabs_ready, 2)
            with dve.Fori(0, nb) as b:
                dve.wait_ge(e_used, b * EC + (CR_E + 8))
                dve.wait_ge(gu_turned, b + CR_GT)
                v.tensor_scalar(gu, bank[0][:, :], tab_rs[:, bass.ds(b, 1)], None, ALU.mult)\
                    .then_inc(gu_ready, 1)
                v.tensor_scalar(place, place, float(TB), None, ALU.subtract).then_inc(place_ready, 1)
                dve.wait_ge(place_ready, b + 1)
                dve.wait_ge(xg_made, b * 2 + 2)
                pick_slots(b + 1)
                dve.wait_ge(sg_ready, b + (CR_SG + 1))
                dve.wait_ge(e_used, b * EC + CR_E)
                v.tensor_tensor(hT.rearrange("p (f n) -> p f n", f=FT), guT[:, :, TB:P],
                                sg.rearrange("p (f n) -> p f n", f=FT), ALU.mult).then_inc(hT_ready, 1)
                dve.wait_ge(y_stored, b * 16 + CR_YS)
                v.tensor_copy(idx_row[:, :], tab_row[:, bass.ds(b, 1)]).then_inc(idx_r_ready, 1)
                dve.wait_ge(e_used, b * EC + (CR_E + EC))
                v.tensor_copy(ysb[:, W:2 * W], bank[5][:, :]).then_inc(y_evac_v, 1)
                rows_turned(b * 2 + 2)
            for t in range(TT):
                h = xh[:, t, :]
                dve.wait_ge(yrow_in[t], 32)
                v.scalar_tensor_tensor(out=h, in0=yrow[t][0], scalar=gates[:, 0, t:t + 1], in1=h,
                                       op0=ALU.mult, op1=ALU.add).then_inc(part_sum, 1)
                dve.wait_ge(part_sum, t + 1)
                v.scalar_tensor_tensor(out=h, in0=yrow[t][1], scalar=gates[:, 1, t:t + 1], in1=h,
                                       op0=ALU.mult, op1=ALU.add).then_inc(out_ready, 1)


R_TAKEN, R_OH1, R_OH2, R_LE, R_EQ, R_POS = (TT * E * i for i in range(6))
R_LG = TT * E * 6
R_EXG = R_LG + TT * 36
R_EQG = R_EXG + TT * NG
R_EX2 = R_EQG + TT * NG
R_ONE = R_EX2 + TT
R_CNT = R_ONE + TT * 11
R_NB = R_CNT + NT
R_SA = R_NB + E
R_SB = R_SA + E
R_OVER = R_SB + E
R_SUMS = R_OVER + E * (T // TB - 1)
R_DEST = R_SUMS + TT * E


def shape_constants():
    c = np.zeros((P, NC_CONST), np.float32)
    p = np.arange(P)
    c[:, C_ID:C_ID + P] = np.eye(P)
    c[:, C_ONE:C_ONE + P] = 1.0
    c[:, C_LOW:C_LOW + P] = p[:, None] < p[None, :]
    c[:, C_TRI:C_TRI + P] = p[:, None] <= p[None, :]
    d = p[:, None] + (T - P) - np.arange(T)[None, :]
    n = np.zeros(d.shape)
    for window, dil in ((128, 1), (512, 4), (2048, 16)):
        n += (d >= 0) & (d <= window) & (d % dil == 0)
    c[:, C_BAND:C_BAND + T] = np.where(n > 0, np.log(np.maximum(n, 1)) / SCALE, OFF)
    c[:, C_GI:C_GI + TT * NG] = np.tile(np.arange(NG) + BIG, TT)
    c[:, C_EI:C_EI + TT * E] = np.tile(np.arange(E), TT)
    c[:, C_EG:C_EG + TT * E] = np.tile(np.arange(E) // EG, TT)
    c[:, C_P] = p
    c[:, C_HALF] = 2 * NOWHERE + (p >= TB)
    c[:, C_TH:C_TH + T // TB - 1] = TB * np.arange(1, T // TB)
    c[:, C_SLOT:C_SLOT + P] = np.arange(P) % TB
    c[:, C_BLK:C_BLK + NT] = np.arange(NT)
    c[:, C_PAIR:C_PAIR + 2 * TT] = np.arange(2 * TT)[None, :] * P + p[:, None] - NOWHERE
    c[:, C_FOLD:C_FOLD + 36] = (p[:, None] % RC) == np.arange(36)[None, :]
    return c


def kernel(**inputs):
    import concourse.bacc as bacc
    from concourse.bass_utils import run_bass_kernel_spmd

    a = {k: np.asarray(v) for k, v in inputs.items()}
    consts = shape_constants()

    def by_tile(v):
        return v.reshape(-1, P).T

    def spread(v):
        return np.broadcast_to(v, (P, v.shape[-1]))

    cols = np.concatenate([
        np.concatenate([a["conv_w"][0], a["conv_b"]]).reshape(TAPS + 1, 4, P).transpose(2, 1, 0).reshape(P, -1),
        by_tile(a["conv_ln_g"][0]), by_tile(a["conv_ln_b"][0]),
        by_tile(a["out_norm"][0, W:2 * W]), a["q_norm"][0][:, None], a["k_norm"][0][:, None],
        a["sgu_b"][0].T, by_tile(a["norm2"][0]),
        a["norm2"][0].reshape(P, 2, KT // 2).transpose(0, 2, 1).reshape(P, KT)], axis=1)
    w_in, w_out = a["w_in"][0], a["w_out"][0]
    U, VA, CA, CG, QQ, KK, VV = 0, 512, 1024, 1536, 2048, 3072, 4096

    def token_group(w, c0):
        return w[:, c0:c0 + W].reshape(4, 4, P, W).transpose(0, 2, 1, 3).reshape(4, P, CH)

    def tiles(*starts):
        return np.stack([w_in[:, c:c + P].reshape(KT, P, P).transpose(1, 0, 2).reshape(P, CH) for c in starts])

    stream = np.concatenate(
        [token_group(w_in, VV), token_group(w_in, VV + W)]
        + [tiles(CA + j * P, CG + j * P) for j in range(4)]
        + [token_group(w_in, U), token_group(w_in, VA)]
        + [tiles(QQ + h * P, KK + h * P) for h in range(H)]
        + [token_group(w_out, g * W) for g in range(4)])
    w_rt = np.concatenate([a["w_router_group"][0], a["w_router_expert"][0]], axis=1)
    w_rt = np.pad(w_rt, ((0, 0), (0, RC - 36))).reshape(KT, P, RC).transpose(1, 0, 2)
    rbias = np.broadcast_to(np.concatenate([a["b_router_group"][0], a["b_router_expert"][0]]), (P, TT, 36))
    ins = {
        "x": a["x"][0], "consts": consts, "cols": cols,
        "rows_a": np.concatenate([spread(a["sgu_norm"][0]), spread(a["out_norm"][0, :W])], axis=1),
        "row_c": spread(a["out_norm"][0, 2 * W:]), "row_n1": spread(a["norm1"][0]),
        "rbias": rbias, "sgu_wt": a["sgu_w"][0].transpose(2, 0, 1),
        "w_stream": stream, "w_rt": w_rt,
        "w_gate": a["w_expert_gate"][0], "w_up": a["w_expert_up"][0], "w_down": a["w_expert_down"][0],
    }
    ins = {f"in_{k}": np.ascontiguousarray(v) for k, v in ins.items()}
    nc = bacc.Bacc("TRN2", target_bir_lowering=False, num_devices=1)
    args = [nc.dram_tensor(k, list(v.shape), mybir.dt.from_np(v.dtype), kind="ExternalInput").ap()
            for k, v in ins.items()]
    out = nc.dram_tensor("out_rows", [T, D], F32, kind="ExternalOutput").ap()
    build(nc, *args, out)
    r = run_bass_kernel_spmd(nc, [ins], core_ids=[0])
    return r.results[0]["out_rows"].reshape(1, T, D)
```
